# Optimizing a Trainium2 kernel written in Bass

```python
import math
import jax, jax.numpy as jnp
from jax import lax
import numpy as np

D_MODEL = 1024
BATCH = 1
SEQ = 256
DEPTH = 1

MEM_LEN = 256
D_CONV = 512
CONV_HEADS = 8
D_SSM = 512
SSM_GROUP = 16
SSM_GROUPS = D_SSM // SSM_GROUP
SSM_STATE = 64
CONV_WIDTH = 3
D_IN_PROJ = 3 * D_CONV + D_SSM
D_MIX = D_CONV + D_SSM
XATTN_HEADS = 4
XATTN_HEAD_DIM = D_MODEL // XATTN_HEADS
N_EXPERTS = 32
TOP_K = 4
D_EXPERT = D_MODEL
SWIGLU_LIMIT = 7.0
SWIGLU_ALPHA = 1.702
EXPERT_BLOCK = 256
NORM_EPS = 1e-5

kernel_name = "hybrid_conv_s5_xattn_moe"

def _rmsnorm(x, g):
    xf = x.astype(jnp.float32)
    y = xf * lax.rsqrt(jnp.mean(xf * xf, axis=-1, keepdims=True) + NORM_EPS)
    return (y * g.astype(jnp.float32)).astype(x.dtype)

def _conv_mixer(bg, cg, xc, conv_w):
    v = cg * xc
    conv = lax.conv_general_dilated(
        v, conv_w[:, None, :].astype(v.dtype), window_strides=(1,),
        padding=[(CONV_WIDTH - 1, 0)],
        dimension_numbers=("NWC", "WIO", "NWC"),
        feature_group_count=D_CONV)
    return bg * conv

def _cplx_scan_op(e1, e2):
    a1r, a1i, b1r, b1i = e1
    a2r, a2i, b2r, b2i = e2
    ar = a1r * a2r - a1i * a2i
    ai = a1r * a2i + a1i * a2r
    br = a2r * b1r - a2i * b1i + b2r
    bi = a2r * b1i + a2i * b1r + b2i
    return ar, ai, br, bi

def _ssm_mixer(u, a_re, a_im, log_dt, b_re, b_im, c_re, c_im, d, w_glu):
    bsz, seq, _ = u.shape
    f32 = jnp.float32
    uf = u.astype(f32)
    ug = uf.reshape(bsz, seq, SSM_GROUPS, SSM_GROUP)
    a_re = a_re.astype(f32); a_im = a_im.astype(f32)
    b_re = b_re.astype(f32); b_im = b_im.astype(f32)
    dt = jnp.exp(log_dt.astype(f32))[:, None]
    mag = jnp.exp(dt * a_re)
    abar_re = mag * jnp.cos(dt * a_im)
    abar_im = mag * jnp.sin(dt * a_im)
    den = a_re * a_re + a_im * a_im
    p_re = abar_re - 1.0
    p_im = abar_im
    q_re = (p_re * a_re + p_im * a_im) / den
    q_im = (p_im * a_re - p_re * a_im) / den
    bb_re = q_re[..., None] * b_re - q_im[..., None] * b_im
    bb_im = q_re[..., None] * b_im + q_im[..., None] * b_re
    bu_re = jnp.einsum("blgc,gnc->blgn", ug, bb_re)
    bu_im = jnp.einsum("blgc,gnc->blgn", ug, bb_im)
    ar = jnp.broadcast_to(abar_re, bu_re.shape)
    ai = jnp.broadcast_to(abar_im, bu_re.shape)
    _, _, s_re, s_im = lax.associative_scan(_cplx_scan_op, (ar, ai, bu_re, bu_im), axis=1)
    y = (jnp.einsum("blgn,gcn->blgc", s_re, c_re.astype(f32))
         - jnp.einsum("blgn,gcn->blgc", s_im, c_im.astype(f32)))
    y = y.reshape(bsz, seq, D_SSM) + d.astype(f32) * uf
    y = jax.nn.gelu(y)
    y = y * jax.nn.sigmoid(y @ w_glu.astype(f32))
    return y.astype(u.dtype)

def _cross_attn(h, mem_n, w_q, w_kv, w_o):
    bsz, seq, _ = h.shape
    m = mem_n.shape[1]
    q = (h @ w_q).reshape(bsz, seq, XATTN_HEADS, XATTN_HEAD_DIM)
    kv = mem_n @ w_kv
    k = kv[..., :D_MODEL].reshape(bsz, m, XATTN_HEADS, XATTN_HEAD_DIM)
    v = kv[..., D_MODEL:].reshape(bsz, m, XATTN_HEADS, XATTN_HEAD_DIM)
    s = jnp.einsum("blhd,bmhd->bhlm", q, k).astype(jnp.float32) * (XATTN_HEAD_DIM ** -0.5)
    p = jax.nn.softmax(s, axis=-1).astype(h.dtype)
    o = jnp.einsum("bhlm,bmhd->blhd", p, v).reshape(bsz, seq, D_MODEL)
    return o @ w_o

def _moe(h2d, w_router, b_router, w_gu, b_gu, w_down, b_down):
    n_tok = h2d.shape[0]
    logits = (h2d @ w_router + b_router).astype(jnp.float32)
    top_val, top_idx = lax.top_k(logits, TOP_K)
    gates = jax.nn.softmax(top_val, axis=-1)
    n_assign = n_tok * TOP_K
    e_flat = top_idx.reshape(-1)
    tok_flat = jnp.arange(n_assign, dtype=jnp.int32) // TOP_K
    g_flat = gates.reshape(-1)
    order = jnp.argsort(e_flat)
    e_sorted = e_flat[order]
    tok_sorted = tok_flat[order]
    g_sorted = g_flat[order]
    counts = jnp.bincount(e_flat, length=N_EXPERTS)
    starts = jnp.cumsum(counts) - counts
    padded = (counts + EXPERT_BLOCK - 1) // EXPERT_BLOCK * EXPERT_BLOCK
    pends = jnp.cumsum(padded)
    pstarts = pends - padded
    dest = pstarts[e_sorted] + (jnp.arange(n_assign) - starts[e_sorted])
    n_blocks = -(-(n_assign + N_EXPERTS * (EXPERT_BLOCK - 1)) // EXPERT_BLOCK)
    n_rows = n_blocks * EXPERT_BLOCK
    tok_buf = jnp.zeros((n_rows,), jnp.int32).at[dest].set(tok_sorted)
    g_buf = jnp.zeros((n_rows,), h2d.dtype).at[dest].set(g_sorted.astype(h2d.dtype))
    blk_expert = jnp.minimum(
        jnp.searchsorted(pends, jnp.arange(n_blocks) * EXPERT_BLOCK, side="right"),
        N_EXPERTS - 1)

    def run_block(args):
        tok, g, e = args
        xb = h2d[tok]
        gu = xb @ w_gu[e] + b_gu[e]
        x_glu = jnp.minimum(gu[:, :D_EXPERT], SWIGLU_LIMIT)
        x_lin = jnp.clip(gu[:, D_EXPERT:], -SWIGLU_LIMIT, SWIGLU_LIMIT)
        act = x_glu * jax.nn.sigmoid(SWIGLU_ALPHA * x_glu) * (x_lin + 1.0)
        out = act @ w_down[e] + b_down[e]
        return out * g[:, None]

    out_blocks = lax.map(run_block, (tok_buf.reshape(n_blocks, EXPERT_BLOCK),
                                     g_buf.reshape(n_blocks, EXPERT_BLOCK), blk_expert))
    return jnp.zeros_like(h2d).at[tok_buf].add(out_blocks.reshape(n_rows, D_MODEL))

def setup_inputs(seed: int = 0) -> dict:
    key = jax.random.key(seed)
    ks = jax.random.split(key, 32)
    f32 = jnp.float32

    def nrm(k, shape, scale):
        return jax.random.normal(k, shape, f32) * scale

    def gain(k, shape):
        return 1.0 + 0.02 * jax.random.normal(k, shape, f32)

    L, G, N, C = DEPTH, SSM_GROUPS, SSM_STATE, SSM_GROUP
    n_idx = jnp.arange(N, dtype=f32)
    a_re = -0.5 + 0.01 * jax.random.normal(ks[4], (L, G, N), f32)
    a_im = math.pi * n_idx + 0.01 * jax.random.normal(ks[5], (L, G, N), f32)
    log_dt = jax.random.uniform(ks[6], (L, G), f32, math.log(1e-3), math.log(1e-1))
    return {
        "x": nrm(ks[0], (BATCH, SEQ, D_MODEL), 1.0),
        "mem": nrm(ks[1], (BATCH, MEM_LEN, D_MODEL), 1.0),
        "norm_mix": gain(ks[2], (L, D_MODEL)),
        "w_in": nrm(ks[3], (L, D_MODEL, D_IN_PROJ), D_MODEL ** -0.5),
        "conv_w": nrm(ks[7], (L, CONV_WIDTH, D_CONV), CONV_WIDTH ** -0.5),
        "ssm_a_re": a_re,
        "ssm_a_im": a_im,
        "ssm_log_dt": log_dt,
        "ssm_b_re": nrm(ks[8], (L, G, N, C), (2 * C) ** -0.5),
        "ssm_b_im": nrm(ks[9], (L, G, N, C), (2 * C) ** -0.5),
        "ssm_c_re": nrm(ks[10], (L, G, C, N), (2 * N) ** -0.5),
        "ssm_c_im": nrm(ks[11], (L, G, C, N), (2 * N) ** -0.5),
        "ssm_d": nrm(ks[12], (L, D_SSM), 1.0),
        "w_glu": nrm(ks[13], (L, D_SSM, D_SSM), D_SSM ** -0.5),
        "norm_conv_out": gain(ks[14], (L, D_CONV)),
        "norm_ssm_out": gain(ks[15], (L, D_SSM)),
        "w_out": nrm(ks[16], (L, D_MIX, D_MODEL), D_MIX ** -0.5),
        "norm_xattn": gain(ks[17], (L, D_MODEL)),
        "norm_mem": gain(ks[18], (L, D_MODEL)),
        "w_q": nrm(ks[19], (L, D_MODEL, D_MODEL), D_MODEL ** -0.5),
        "w_kv": nrm(ks[20], (L, D_MODEL, 2 * D_MODEL), D_MODEL ** -0.5),
        "w_o": nrm(ks[21], (L, D_MODEL, D_MODEL), D_MODEL ** -0.5),
        "norm_moe": gain(ks[22], (L, D_MODEL)),
        "w_router": nrm(ks[23], (L, D_MODEL, N_EXPERTS), D_MODEL ** -0.5),
        "b_router": nrm(ks[24], (L, N_EXPERTS), 0.01),
        "w_gu": nrm(ks[25], (L, N_EXPERTS, D_MODEL, 2 * D_EXPERT), D_MODEL ** -0.5),
        "b_gu": nrm(ks[26], (L, N_EXPERTS, 2 * D_EXPERT), 0.01),
        "w_down": nrm(ks[27], (L, N_EXPERTS, D_EXPERT, D_MODEL), D_EXPERT ** -0.5),
        "b_down": nrm(ks[28], (L, N_EXPERTS, D_MODEL), 0.01),
        "norm_final": gain(ks[29], (D_MODEL,)),
    }

def reference(x, mem, norm_mix, w_in, conv_w, ssm_a_re, ssm_a_im, ssm_log_dt,
              ssm_b_re, ssm_b_im, ssm_c_re, ssm_c_im, ssm_d, w_glu,
              norm_conv_out, norm_ssm_out, w_out, norm_xattn, norm_mem,
              w_q, w_kv, w_o, norm_moe, w_router, b_router, w_gu, b_gu,
              w_down, b_down, norm_final):
    bsz, seq, _ = x.shape
    for l in range(DEPTH):
        h = _rmsnorm(x, norm_mix[l])
        proj = h @ w_in[l]
        bg = proj[..., :D_CONV]
        cg = proj[..., D_CONV:2 * D_CONV]
        xc = proj[..., 2 * D_CONV:3 * D_CONV]
        u = proj[..., 3 * D_CONV:]
        y_conv = _rmsnorm(_conv_mixer(bg, cg, xc, conv_w[l]), norm_conv_out[l])
        y_ssm = _rmsnorm(_ssm_mixer(u, ssm_a_re[l], ssm_a_im[l], ssm_log_dt[l],
                                    ssm_b_re[l], ssm_b_im[l], ssm_c_re[l], ssm_c_im[l],
                                    ssm_d[l], w_glu[l]), norm_ssm_out[l])
        x = x + jnp.concatenate([y_conv, y_ssm], axis=-1) @ w_out[l]
        h = _rmsnorm(x, norm_xattn[l])
        m = _rmsnorm(mem, norm_mem[l])
        x = x + _cross_attn(h, m, w_q[l], w_kv[l], w_o[l])
        h = _rmsnorm(x, norm_moe[l])
        y = _moe(h.reshape(bsz * seq, D_MODEL), w_router[l], b_router[l],
                 w_gu[l], b_gu[l], w_down[l], b_down[l])
        x = x + y.reshape(bsz, seq, D_MODEL)
    return _rmsnorm(x, norm_final)


_drawn_inputs = setup_inputs


def setup_inputs(seed=0):
    import zlib

    import numpy as np

    out = dict(_drawn_inputs(seed))
    spreads = {}
    factors = {'ssm_a_re': 64.0,
     'norm_conv_out': 3.53,
     'norm_xattn': 6.362,
     'norm_mem': 8.0,
     'b_router': 21.12,
     'b_gu': 64.0,
     'b_down': 64.0,
     'norm_final': 8.609,
     'norm_moe': 8.0}
    for name, (base, spread) in spreads.items():
        noise = np.random.default_rng([zlib.crc32(name.encode()), seed]).standard_normal(out[name].shape)
        drawn = base * np.exp(spread * noise) if base else spread * noise
        out[name] = __import__('jax').numpy.asarray(drawn.astype(out[name].dtype))
    for name, factor in factors.items():
        out[name] = (out[name] * factor).astype(out[name].dtype)
    return out
```

```python
import math
from contextlib import ExitStack

import concourse.bass as bass
from concourse import mybir

F32 = mybir.dt.float32
BF16 = mybir.dt.bfloat16
I32 = mybir.dt.int32
ALU = mybir.AluOpType
ACT = mybir.ActivationFunctionType
AX = mybir.AxisListType

P = 128
D = 1024
SEQ = 256
TT = SEQ // P
KT = D // P
HALF = 512
D_CONV = 512
CT = D_CONV // P
GROUPS, GCH, NST = 32, 16, 64
ST_TILES = GROUPS * NST // P
HEADS, HD = 4, 256
E = 32
C = 64
TOPK = 4
LIMIT, ALPHA = 7.0, 1.702
EPS = 1e-5
MAX_EXTRA = SEQ * TOPK // (C + 1)
PASSES = SEQ // C - 1
JT = E + MAX_EXTRA + 1

PRE_SLOTS = 9
SLOTS = 12
U_CH, CONV_CH, K_CH, V_CH, GLU_CH, WO_CH, WQ_CH, XO_CH = 0, 2, 8, 12, 16, 17, 21, 25
N_PRE = 29
DVE_LOOP_LINKS = 3


class Chain:

    def __init__(self, engine, sem):
        self.engine, self.sem, self.count = engine, sem, 0

    def link(self, instruction):
        instruction.then_inc(self.sem, 1)
        self.count = self.count + 1
        self.engine.wait_ge(self.sem, self.count)


def hybrid_layer(nc, x, mem, norm_mix, w_in, conv_w, ssm_a_re, ssm_a_im, ssm_log_dt, ssm_b_re, ssm_b_im,
                 ssm_c_re, ssm_c_im, ssm_d, w_glu, norm_conv_out, norm_ssm_out, w_out, norm_xattn, norm_mem,
                 w_q, w_kv, w_o, norm_moe, w_router, b_router, w_gu, b_gu, w_down, b_down, norm_final, out):
    ctx = ExitStack()
    with ctx:
        def sb(name, cols, dt=F32, parts=P):
            return ctx.enter_context(nc.sbuf_tensor(name, [parts, cols], dt))

        def sem(name):
            return ctx.enter_context(nc.semaphore(name))

        W = ctx.enter_context(nc.sbuf_tensor("W", [P, SLOTS, 2 * D], F32))
        R1 = sb("R1", 12288)
        XR = sb("XR", TT * D)
        HT = sb("HT", KT * SEQ)
        MT = sb("MT", KT * SEQ)
        KR = sb("KR", KT * SEQ)
        VR = sb("VR", KT * SEQ)
        R3 = sb("R3", 3 * CT * SEQ)
        CTm = sb("CTm", 2 * CT * P)
        ident = sb("ident", P)
        small = sb("small", 256)
        gT = sb("gT", 56)
        Cs = sb("Cs", 2 * SEQ)
        vp = sb("vp", 2 * (SEQ + 2))
        cv = sb("cv", SEQ)
        SCR = W[:, PRE_SLOTS:SLOTS, :].rearrange("p s n -> p (s n)")

        x_res = XR[:, :].rearrange("p (t n) -> p t n", t=TT)
        hT = HT[:, :].rearrange("p (k t) -> p k t", k=KT)
        mT = MT[:, :].rearrange("p (k t) -> p k t", k=KT)
        xn = KR[:, :].rearrange("p (t n) -> p t n", t=TT)
        mem_n = VR[:, :].rearrange("p (t n) -> p t n", t=TT)
        kT = KR[:, :].rearrange("p (k t) -> p k t", k=KT)
        V = VR[:, :].rearrange("p (t n) -> p t n", t=TT)
        uT = R3[:, 0:1024].rearrange("p (c t) -> p c t", c=CT)
        ycT = R3[:, 1024:2048].rearrange("p (c t) -> p c t", c=CT)
        ysT = R3[:, 2048:3072].rearrange("p (c t) -> p c t", c=CT)
        tmp_dve = R3[:, 1024:2048]
        tmp_pool = R3[:, 2048:3072]
        cosT = R1[:, 0:4096].rearrange("p (i t) -> p i t", i=ST_TILES)
        sinT = R1[:, 4096:8192].rearrange("p (i t) -> p i t", i=ST_TILES)
        BT = R1[:, 8192:12288].rearrange("p (m j r s) -> p m j r s", m=CT, j=4, r=2)
        CTv = CTm[:, :].rearrange("p (r m c) -> p r m c", r=2, m=CT)

        ssx, sdx, rsx = small[:, 0:2], small[:, 2:4], small[:, 4:6]
        ssm, sdm, rsm = small[:, 6:8], small[:, 8:10], small[:, 10:12]
        eps = small[:, 12:13]
        ones2 = small[:, 14:16]
        sel_mask = small[:, 16:20]
        r_conv, r_ssm, sd_cs = small[:, 20:22], small[:, 22:24], small[:, 24:28]
        mx, nmx, sm, rsum = small[:, 32:40], small[:, 40:48], small[:, 48:56], small[:, 56:64]
        pT = small[:, 64:144].rearrange("p (q i) -> p q i", q=5)

        BDn = SCR[:, 0:1024].rearrange("p (r i w c) -> p r i w c", r=2, i=ST_TILES, w=2)
        CNn = SCR[:, 1024:2048].rearrange("p (r m w n) -> p r m w n", r=2, m=CT, w=2)
        b_nat = SCR[:, 2048:2560].rearrange("p (r i c) -> p r i c", r=2, i=ST_TILES)
        b_bar = SCR[:, 2560:3072].rearrange("p (r i c) -> p r i c", r=2, i=ST_TILES)
        b_tmp = SCR[:, 3072:3584].rearrange("p (r i c) -> p r i c", r=2, i=ST_TILES)
        c_nat = SCR[:, 3584:4096].rearrange("p (r m n) -> p r m n", r=2, m=CT)
        rows = SCR[0:56, 4096:4224]
        PR = SCR[0:16, 4224:6144]

        def par(i):
            return PR[:, P * i:P * (i + 1)]

        sA = SCR[:, 0:1024].rearrange("p (b r t) -> p b r t", b=2, r=2)
        sB = SCR[:, 1024:2048].rearrange("p (b r t) -> p b r t", b=2, r=2)
        zin = SCR[:, 2048:3072].rearrange("p (b r t) -> p b r t", b=2, r=2)
        zz = SCR[:, 3072:4096].rearrange("p (b r t) -> p b r t", b=2, r=2)
        Qb = SCR[:, 4096:5120].rearrange("p (b r t) -> p b r t", b=2, r=2)
        Pb = SCR[:, 5120:5632].rearrange("p (r t) -> p r t", r=2)
        s4 = XR[:, :].rearrange("p (j r t) -> p j r t", j=4, r=2)
        ge = SCR[:, 0:1024].rearrange("p (c t) -> p c t", c=CT)
        ge2 = SCR[:, 1024:2048].rearrange("p (c t) -> p c t", c=CT)
        yg = SCR[:, 2048:3072].rearrange("p (c t) -> p c t", c=CT)
        sq_s = SCR[:, 3072:4096].rearrange("p (c t) -> p c t", c=CT)
        sq_c = SCR[:, 4096:5120].rearrange("p (c t) -> p c t", c=CT)

        QT = R1[:, 0:2048].rearrange("p (k t) -> p k t", k=KT)
        PA = R1[:, 2048:4096].rearrange("p (h t m) -> p h t m", h=HEADS, t=TT)
        PT = R1[:, 4096:6144].rearrange("p (h m t) -> p h m t", h=HEADS, m=TT)
        OT = R1[:, 6144:8192].rearrange("p (k t) -> p k t", k=KT)
        xn2 = R1[:, 8192:10240].rearrange("p (t n) -> p t n", t=TT)

        bg_raw = R1[0:96, 10240:12288]
        bias3 = MT[0:96, 0:1024].bitcast(BF16)
        bdown = MT[0:E, 1024:2048]

        xr3 = R1[:, 0:3072].bitcast(BF16).rearrange("p (t s n) -> p t s n", t=TT, s=3)
        wr = R1[:, 10240:10496].rearrange("p (k e) -> p k e", k=KT)
        br = R1[:, 10496:10528]
        gfin = R1[:, 10528:11552]
        EB = R1[:, 3072:8192]
        lg = EB[:, 0:64].rearrange("p (t e) -> p t e", t=TT)
        top8 = EB[:, 64:80].rearrange("p (t e) -> p t e", t=TT)
        gt = EB[:, 80:144].rearrange("p (t e) -> p t e", t=TT)
        eq = EB[:, 144:208].rearrange("p (t e) -> p t e", t=TT)
        cum = EB[:, 208:272].rearrange("p (t e) -> p t e", t=TT)
        need = EB[:, 272:274]
        maskf = EB[:, 288:352].rearrange("p (t e) -> p t e", t=TT)
        mask16 = EB[:, 352:384].bitcast(BF16).rearrange("p (t e) -> p t e", t=TT)
        gates = EB[:, 384:450].rearrange("p (t e) -> p t e", t=TT)
        rankm = EB[:, 450:516].rearrange("p (t e) -> p t e", t=TT)
        gexp = EB[:, 516:580].rearrange("p (t e) -> p t e", t=TT)
        gsum, grec, ngm = EB[:, 580:582], EB[:, 582:584], EB[:, 584:586]
        cnt = EB[:, 586:618]
        flag = EB[:, 618:714]
        incl = EB[:, 714:810]
        pos = EB[:, 810:906]
        id_e = EB[:, 906:1002]
        id_b = EB[:, 1002:1098]
        iota_j = EB[:, 1098:1114]
        iota_c = EB[:, 1114:1178]
        job_e = EB[:, 1178:1178 + JT]
        job_b = EB[:, 1242:1242 + JT]
        job_ei = EB[:, 1306:1306 + JT].bitcast(I32)
        n_jobs_i = EB[:, 1370:1371].bitcast(I32)
        ones96 = EB[:, 1376:1472]
        tri = EB[:, 1472:1536].bitcast(BF16)
        ones_b = EB[:, 1536:1600].bitcast(BF16)
        onehot = EB[0:96, 1600:1664].bitcast(BF16)[:, 0:E + 1]
        oh_cur = EB[0:96, 1664:1696].bitcast(BF16)
        sel = EB[:, 1696:1760].bitcast(BF16).rearrange("p (t c) -> p t c", t=TT)
        selG = EB[:, 1760:2016].rearrange("p (t w c) -> p t w c", t=TT, w=2)
        eqj = EB[:, 2048:3584].rearrange("p (j f) -> p j f", j=16)
        eqi = EB[:, 3584:5120].rearrange("p (j f) -> p j f", j=16)
        gatesT = EB[0:E, 2048:2304]

        g7 = KR[:, 0:512]
        sg = KR[:, 512:1024]
        l7 = KR[:, 1024:1536]
        aa = KR[:, 1536:2048]
        actT = VR[:, 0:512].rearrange("p (k c) -> p k c", k=KT)
        hTe = VR[:, 512:1024].rearrange("p (k c) -> p k c", k=KT)
        ye = VR[:, 1024:1536]
        STz = VR[:, 1536:2048].rearrange("p (w t) -> p w t", w=2)

        bk = [ctx.enter_context(nc.psum_tensor(f"bank{i}", [P, HALF], F32)) for i in range(8)]
        acc = [[bk[2 * t + h] for h in range(2)] for t in range(TT)]
        pg_glu, pg_lin, pg_t, pg_g = bk[4], bk[5], bk[6], bk[7]

        full = [sem(f"slot{i}_full") for i in range(SLOTS)]
        chunk_used = sem("chunk_used")
        x_ld, mem_ld, rows_ld, par_ld, bc_ld = sem("x_ld"), sem("mem_ld"), sem("rows_ld"), sem("par_ld"), sem("bc_ld")
        x2_ld, bg_ld, bd_ld, wr_ld, gf_ld = sem("x2_ld"), sem("bg_ld"), sem("bd_ld"), sem("wr_ld"), sem("gf_ld")
        consts, dve_consts, dvec, actc, poolc = sem("consts"), sem("dve_consts"), sem("dve_step"), sem("act_step"), sem("pool_step")
        dvel = sem("dve_loop_step")
        x_sd, m_sd, xn_ready, mn_ready = sem("x_sd"), sem("m_sd"), sem("xn_ready"), sem("mn_ready")
        rows_t, gT_ready, xT_ps, xT_ready, mT_ps, mT_ready = sem("rows_t"), sem("gT_ready"), sem("xT_ps"), sem("xT_ready"), sem("mT_ps"), sem("mT_ready")
        dt_ready, arg_ready, trig_ready, par_math, par_ps, pT_ready = sem("dt_ready"), sem("arg_ready"), sem("trig_ready"), sem("par_math"), sem("par_ps"), sem("pT_ready")
        bd_ready, cn_ready, bct_ps, bct_ready = sem("bd_ready"), sem("cn_ready"), sem("bct_ps"), sem("bct_ready")
        tab_dve, tab_pool = sem("tab_dve"), sem("tab_pool")
        proj_ps, proj_used = sem("proj_ps"), sem("proj_used")
        bu_ps, ab_ready, zin_ready, z_ready, q_ready, s_ready = sem("bu_ps"), sem("ab_ready"), sem("zin_ready"), sem("z_ready"), sem("q_ready"), sem("s_ready")
        y_ps, yv_ready, gelu_arg, gelu_sig, yg_ready = sem("y_ps"), sem("yv_ready"), sem("gelu_arg"), sem("gelu_sig"), sem("yg_ready")
        yc_ready, ycg_ready = sem("yc_ready"), sem("ycg_ready")
        v_ps, v_evac = sem("v_ps"), sem("v_evac")
        glu_ps, glu_sig, ys_ready, ysg_ready = sem("glu_ps"), sem("glu_sig"), sem("ys_ready"), sem("ysg_ready")
        ss_ps, ss_sd, r_ready = sem("ss_ps"), sem("ss_sd"), sem("r_ready")
        mix_ps, x1_ready = sem("mix_ps"), sem("x1_ready")
        x1_sd, x1n_ready, x1T_ps, x1T_ready = sem("x1_sd"), sem("x1n_ready"), sem("x1T_ps"), sem("x1T_ready")
        q_ps, qT_ready, sc_ps, mx_ready, exp_ready, p_ready = sem("q_ps"), sem("qT_ready"), sem("sc_ps"), sem("mx_ready"), sem("exp_ready"), sem("p_ready")
        pt_ps, pt_ready, o_ps, o_ready, xo_ps, x2_ready = sem("pt_ps"), sem("pt_ready"), sem("o_ps"), sem("o_ready"), sem("xo_ps"), sem("x2_ready")
        x2_sd, x2n_ready, x2T_ps, x2T_ready = sem("x2_sd"), sem("x2n_ready"), sem("x2T_ps"), sem("x2T_ready")
        lg_ps, lmax_ready, gexp_ready, mask_ready, rank_ps, xr3_ready = sem("lg_ps"), sem("lmax_ready"), sem("gexp_ready"), sem("mask_ready"), sem("rank_ps"), sem("xr3_ready")
        gates_ready, gT_ps, gatesT_ready, seeded = sem("gates_ready"), sem("gatesT_ps"), sem("gatesT_ready"), sem("seeded")
        bias_ready, jobs_ready = sem("bias_ready"), sem("jobs_ready")
        sel_ready, oh_ready, g_ps, hTe_ready, st_ps, st_ready = sem("sel_ready"), sem("onehot_ready"), sem("gather_ps"), sem("hTe_ready"), sem("st_ps"), sem("st_ready")
        glu_min, sig_ready, act_ready, actT_ps, actT_ready = sem("glu_min"), sem("sig_ready"), sem("act_ready"), sem("actT_ps"), sem("actT_ready")
        y_ready, scat_done = sem("y_ready"), sem("scatter_done")
        fin_x, fin_sd, fin_ready, out_done = sem("fin_x"), sem("fin_sd"), sem("fin_ready"), sem("out_done")

        block = ctx.enter_context(nc.Block())

        def bc_last(ap, shape):
            return ap.unsqueeze(len(ap.shape)).to_broadcast(shape)

        @block.sync
        def _(sp):
            sp.dma_start(x_res, x[0].rearrange("(t p) n -> p t n", p=P)).then_inc(x_ld, 16)
            sp.dma_start(mem_n, mem[0].rearrange("(t p) n -> p t n", p=P)).then_inc(mem_ld, 16)

            def slot(n):
                return W[:, n % PRE_SLOTS, :]

            def cols(w, c0):
                return w.rearrange("(k p) n -> p k n", p=P)[:, :, c0:c0 + 256], KT

            def two_rows(w, k0, c0):
                return w.rearrange("(k p) n -> p k n", p=P)[:, k0:k0 + 2, c0:c0 + D], 2

            chunks = [cols(w_in[0], 3 * D_CONV + 256 * i) for i in range(2)]
            chunks += [cols(w_in[0], base + 256 * i) for i in range(2) for base in (D_CONV, 2 * D_CONV, 0)]
            chunks += [cols(w_kv[0], 256 * i) for i in range(4)]
            chunks += [two_rows(w_kv[0], 2 * i, D) for i in range(4)]
            chunks += [(w_glu[0].rearrange("(k p) n -> p k n", p=P), CT)]
            chunks += [two_rows(w_out[0], 2 * i, 0) for i in range(4)]
            chunks += [cols(w_q[0], 256 * i) for i in range(4)]
            chunks += [two_rows(w_o[0], 2 * i, 0) for i in range(4)]
            assert len(chunks) == N_PRE
            for n, (src, k) in enumerate(chunks):
                if n >= PRE_SLOTS:
                    sp.wait_ge(chunk_used, n - PRE_SLOTS + 1)
                sp.dma_start(slot(n).rearrange("p (k n) -> p k n", k=k), src).then_inc(full[n % PRE_SLOTS], 16)

            def expert_chunk(e, c):
                if c < KT:
                    src = w_gu[0][bass.ds(e, 1), P * c:P * (c + 1), :].rearrange("o p n -> p (o n)")
                    sp.dma_start(W[:, c, :], src).then_inc(full[c], 16)
                else:
                    k0 = 2 * (c - KT)
                    src = w_down[0][bass.ds(e, 1), P * k0:P * (k0 + 2), :].rearrange("o (k p) n -> p (o k) n", p=P)
                    sp.dma_start(W[:, c, :].rearrange("p (k n) -> p k n", k=2), src).then_inc(full[c], 16)

            for c in range(SLOTS):
                if c < PRE_SLOTS:
                    last = max(n for n in range(N_PRE) if n % PRE_SLOTS == c)
                    sp.wait_ge(chunk_used, last + 1)
                elif c == PRE_SLOTS:
                    sp.wait_ge(ss_ps, 2)
                expert_chunk(0, c)
            with sp.Fori(1, E) as t:
                for c in range(SLOTS):
                    sp.wait_ge(chunk_used, t * SLOTS + (N_PRE - SLOTS + c + 1))
                    expert_chunk(t, c)
            sp.wait_ge(jobs_ready, 1)
            n_jobs = sp.value_load(n_jobs_i[0:1, :], min_val=E, max_val=E + MAX_EXTRA)
            with sp.If(n_jobs > E):
                with sp.Fori(E, n_jobs) as t:
                    e = sp.value_load(job_ei[0:1, bass.ds(t, 1)], min_val=0, max_val=E - 1)
                    for c in range(SLOTS):
                        sp.wait_ge(chunk_used, t * SLOTS + (N_PRE - SLOTS + c + 1))
                        expert_chunk(e, c)
            sp.wait_ge(fin_ready, 1)
            sp.dma_start(out[0].rearrange("(t p) n -> p t n", p=P), xn2).then_inc(out_done, 16)
            sp.wait_ge(out_done, 16)

        @block.tensor
        def _(pe):
            mm, tr = nc.tensor.matmul, nc.tensor.transpose

            def chunk(n):
                pe.wait_ge(full[n % PRE_SLOTS], 16 * (n // PRE_SLOTS + 1))
                return W[:, n % PRE_SLOTS, :]

            pe.wait_ge(consts, 2)
            pe.wait_ge(rows_ld, 16 * 8)
            tr(bk[6][:, 0:56], rows, ident[0:56, 0:56]).then_inc(rows_t, 1)

            def transpose_tokens(src, banks, done, before=None):
                for q, b in enumerate(banks):
                    if before is not None:
                        before(q)
                    for k in range(2):
                        for t in range(TT):
                            last = tr(bk[b][:, k * SEQ + t * P:k * SEQ + (t + 1) * P],
                                      src[:, t, (2 * q + k) * P:(2 * q + k + 1) * P], ident[:, :])
                    last.then_inc(done, 1)

            pe.wait_ge(xn_ready, 1)
            transpose_tokens(xn, (0, 1, 2, 3), xT_ps)
            pe.wait_ge(mn_ready, 1)

            def bank0_free(q):
                if q == 3:
                    pe.wait_ge(xT_ready, 1)
            transpose_tokens(mem_n, (4, 5, 7, 0), mT_ps, bank0_free)

            def proj(q, n, act):
                w = chunk(n).rearrange("p (k n) -> p k n", k=KT)
                if q >= 4:
                    pe.wait_ge(proj_used, q - 3)
                elif q == 3:
                    pe.wait_ge(mT_ready, 4)
                for m in range(2):
                    for k in range(KT):
                        last = mm(bk[(q + 1) % 4][:, m * SEQ:(m + 1) * SEQ], w[:, k, m * P:(m + 1) * P],
                                  act[:, k, :], start=(k == 0), stop=(k == KT - 1))
                last.then_inc(chunk_used, 1)

            pe.wait_ge(xT_ready, 4)
            proj(0, 0, hT)
            proj(1, 1, hT)
            pe.wait_ge(gT_ready, 1)
            pe.wait_ge(par_math, 1)
            for i in range(5):
                last = tr(bk[6][:, 64 + 16 * i:80 + 16 * i], par(8 + i), ident[0:16, 0:16])
            last.then_inc(par_ps, 1)
            pe.wait_ge(mT_ready, 3)
            pe.wait_ge(cn_ready, 1)
            for r, b in ((0, 7), (1, 6)):
                if r == 1:
                    pe.wait_ge(pT_ready, 1)
                for m in range(CT):
                    last = tr(bk[b][:, m * P:(m + 1) * P], CNn[:, r, m].rearrange("p w n -> p (w n)"), ident[:, :])
                last.then_inc(bct_ps, 1)
            pe.wait_ge(bd_ready, 1)
            for r, b in ((0, 4), (1, 5)):
                for m in range(CT):
                    last = tr(bk[b][:, m * P:(m + 1) * P],
                              BDn[:, r, 4 * m:4 * m + 4].rearrange("p i w c -> p (i w c)"), ident[:, :])
                last.then_inc(bct_ps, 1)

            def b_u(i):
                if i >= 2:
                    pe.wait_ge(ab_ready, i - 1)
                for r in range(2):
                    last = mm(bk[4 + i % 2][:, r * SEQ:(r + 1) * SEQ], BT[:, i // 4, i % 4, r, :], uT[:, i // 4, :],
                              start=True, stop=True)
                last.then_inc(bu_ps, 1)

            def y_out(m):
                pe.wait_ge(s_ready, 4 * (m + 1))
                if m >= 2:
                    pe.wait_ge(yv_ready, m - 1)
                for r in range(2):
                    for j in range(4):
                        last = mm(bk[6 + m % 2][32 * j:32 * j + 32, 0:SEQ], CTv[:, r, m, 32 * j:32 * j + 32],
                                  s4[:, j, r, :], start=(r == 0), stop=(r == 1))
                last.then_inc(y_ps, 1)

            pe.wait_ge(bct_ready, 4)
            pe.wait_ge(proj_used, 2)
            for q in range(2, 12):
                if q - 2 < 8:
                    b_u(2 * (q - 2))
                    b_u(2 * (q - 2) + 1)
                if q == 8:
                    pe.wait_ge(mT_ready, 4)
                proj(q, q, hT if q < 8 else mT)
                if q in (5, 7, 9):
                    y_out((q - 5) // 2)

            for i in range(4):
                w = chunk(V_CH + i).rearrange("p (k n) -> p k n", k=2)
                if i == 0:
                    pe.wait_ge(proj_used, 12)
                for k in range(2):
                    for t in range(TT):
                        for h in range(2):
                            last = mm(bk[2 * t + h][:, :], mT[:, 2 * i + k, t * P:(t + 1) * P],
                                      w[:, k, h * HALF:(h + 1) * HALF], start=(i + k == 0), stop=(i == 3 and k == 1))
                last.then_inc(chunk_used, 1)
            y_out(3)

            w = chunk(GLU_CH).rearrange("p (k n) -> p k n", k=CT)
            pe.wait_ge(yg_ready, 1)
            for m in range(CT):
                for k in range(CT):
                    last = mm(bk[4 + m // 2][:, (m % 2) * SEQ:(m % 2 + 1) * SEQ], w[:, k, m * P:(m + 1) * P],
                              yg[:, k, :], start=(k == 0), stop=(k == CT - 1))
            last.then_inc(chunk_used, 1)
            pe.wait_ge(ycg_ready, 1)
            pe.wait_ge(yv_ready, 4)
            for t in range(TT):
                for k in range(CT):
                    last = mm(bk[6][:, 2 * t:2 * t + 2], sq_c[:, k, t * P:(t + 1) * P], ones2,
                              start=(k == 0), stop=(k == CT - 1))
            last.then_inc(ss_ps, 1)

            def out_proj(first_chunk, n_chunks, act, banks):
                for i in range(n_chunks):
                    w = chunk(first_chunk + i).rearrange("p (k n) -> p k n", k=2)
                    for k in range(2):
                        for t in range(TT):
                            for h in range(2):
                                last = mm(bk[banks[2 * t + h]][:, :], act[:, 2 * i + k, t * P:(t + 1) * P],
                                          w[:, k, h * HALF:(h + 1) * HALF], start=(i + k == 0),
                                          stop=(i == n_chunks - 1 and k == 1))
                    last.then_inc(chunk_used, 1)
                return last

            pe.wait_ge(v_evac, 4)
            out_proj(WO_CH, 2, ycT, (0, 1, 2, 3))
            pe.wait_ge(ysg_ready, 1)
            for t in range(TT):
                for k in range(CT):
                    last = mm(bk[6][:, 8 + 2 * t:10 + 2 * t], sq_s[:, k, t * P:(t + 1) * P], ones2,
                              start=(k == 0), stop=(k == CT - 1))
            last.then_inc(ss_ps, 1)
            pe.wait_ge(r_ready, 1)
            out_proj(WO_CH + 2, 2, ysT, (4, 5, 6, 7))
            mix_done = N_PRE - 8
            assert mix_done == WQ_CH

            pe.wait_ge(x1n_ready, 1)
            transpose_tokens(xn2, (0, 1, 2, 3), x1T_ps)
            pe.wait_ge(x1T_ready, 4)
            for i in range(4):
                w = chunk(WQ_CH + i).rearrange("p (k n) -> p k n", k=KT)
                for m in range(2):
                    for k in range(KT):
                        last = mm(bk[4 + i][:, m * SEQ:(m + 1) * SEQ], w[:, k, m * P:(m + 1) * P], hT[:, k, :],
                                  start=(k == 0), stop=(k == KT - 1))
                last.then_inc(chunk_used, 1)
            for h in range(HEADS):
                pe.wait_ge(qT_ready, h + 1)
                for t in range(TT):
                    for k in range(2):
                        last = mm(bk[h][:, t * SEQ:(t + 1) * SEQ], QT[:, 2 * h + k, t * P:(t + 1) * P],
                                  kT[:, 2 * h + k, :], start=(k == 0), stop=(k == 1))
                last.then_inc(sc_ps, 1)
            for h in range(HEADS):
                pe.wait_ge(p_ready, h + 1)
                for m in range(TT):
                    for t in range(TT):
                        last = tr(bk[4 + h][:, m * SEQ + t * P:m * SEQ + (t + 1) * P],
                                  PA[:, h, t, m * P:(m + 1) * P], ident[:, :])
                last.then_inc(pt_ps, 1)
            for h in range(HEADS):
                pe.wait_ge(pt_ready, h + 1)
                for d in range(2):
                    for m in range(TT):
                        last = mm(bk[h][:, d * SEQ:(d + 1) * SEQ], V[:, m, h * HD + d * P:h * HD + (d + 1) * P],
                                  PT[:, h, m, :], start=(m == 0), stop=(m == TT - 1))
                last.then_inc(o_ps, 1)
            pe.wait_ge(o_ready, 4)
            out_proj(XO_CH, 4, OT, (4, 5, 6, 7))

            pe.wait_ge(x2n_ready, 1)
            transpose_tokens(xn2, (0, 1, 2, 3), x2T_ps)
            pe.wait_ge(wr_ld, 32)
            pe.wait_ge(x2T_ready, 4)
            for t in range(TT):
                for k in range(KT):
                    last = mm(bk[4][:, E * t:E * (t + 1)], hT[:, k, t * P:(t + 1) * P], wr[:, k, :],
                              start=(k == 0), stop=(k == KT - 1))
            last.then_inc(lg_ps, 1)
            pe.wait_ge(mask_ready, 1)
            mm(bk[5][:, 0:E], tri, mask16[:, 0, :], start=True, stop=True)
            mm(bk[5][:, E:2 * E], ones_b, mask16[:, 0, :], start=True, stop=False)
            mm(bk[5][:, E:2 * E], tri, mask16[:, 1, :], start=False, stop=True)
            mm(bk[5][:, 2 * E:3 * E], ones_b, mask16[:, 0, :], start=True, stop=False)
            mm(bk[5][:, 2 * E:3 * E], ones_b, mask16[:, 1, :], start=False, stop=True).then_inc(rank_ps, 1)
            pe.wait_ge(gates_ready, 1)
            for t in range(TT):
                last = tr(bk[6][0:E, t * P:(t + 1) * P], gates[:, t, 0:E], ident[:, :])
            last.then_inc(gT_ps, 1)
            pe.wait_ge(xr3_ready, 1)

            def gather(t):
                pe.wait_ge(sel_ready, t + 1)
                for k in range(KT):
                    for tt in range(TT):
                        for s in range(3):
                            last = mm(pg_g[:, k * C:(k + 1) * C], xr3[:, tt, s, k * P:(k + 1) * P], sel[:, tt, :],
                                      start=(tt + s == 0), stop=(tt == TT - 1 and s == 2))
                last.then_inc(g_ps, 1)

            def selection_t(t):
                pe.wait_ge(hTe_ready, t + 1)
                for tt in range(TT):
                    last = tr(pg_g[:, tt * P:(tt + 1) * P], selG[:, tt].rearrange("p w c -> p (w c)"), ident[:, :])
                last.then_inc(st_ps, 1)

            gather(0)
            pe.wait_ge(gatesT_ready, 1)
            pe.wait_ge(bd_ld, 16)
            for t in range(TT):
                for h in range(2):
                    last = mm(acc[t][h][:, :], gatesT[:, t * P:(t + 1) * P], bdown[:, h * HALF:(h + 1) * HALF],
                              start=True, stop=True)
            last.then_inc(seeded, 1)
            selection_t(0)
            pe.wait_ge(bias_ready, 1)

            base = [16 * sum(1 for n in range(N_PRE) if n % PRE_SLOTS == c) if c < PRE_SLOTS else 0
                    for c in range(SLOTS)]

            def job(t):
                pe.wait_ge(oh_ready, t + 1)
                for h in range(2):
                    for w, b in ((0, pg_glu), (1, pg_lin)):
                        mm(b[C * h:C * (h + 1), :], oh_cur, bias3[:, w * D + h * HALF:w * D + (h + 1) * HALF],
                           start=True, stop=False)
                for k in range(KT):
                    pe.wait_ge(full[k], t * 16 + (base[k] + 16))
                    for w, b in ((0, pg_glu), (1, pg_lin)):
                        for h in range(2):
                            last = mm(b[C * h:C * (h + 1), :], hTe[:, k, :],
                                      W[:, k, w * D + h * HALF:w * D + (h + 1) * HALF],
                                      start=False, stop=(k == KT - 1))
                    last.then_inc(chunk_used, 1)
                pe.wait_ge(act_ready, t + 1)
                for c in range(4):
                    last = tr(pg_t[:, c * P:(c + 1) * P], aa[:, c * P:(c + 1) * P], ident[:, :])
                last.then_inc(actT_ps, 1)
                pe.wait_ge(actT_ready, t + 1)
                for c in range(4):
                    pe.wait_ge(full[KT + c], t * 16 + (base[KT + c] + 16))
                    for k in range(2):
                        for h in range(2):
                            last = mm(pg_t[C * h:C * (h + 1), :], actT[:, 2 * c + k, :],
                                      W[:, KT + c, k * D + h * HALF:k * D + (h + 1) * HALF],
                                      start=(c + k == 0), stop=(c == 3 and k == 1))
                    last.then_inc(chunk_used, 1)
                pe.wait_ge(st_ready, t + 1)
                gather(t + 1)
                pe.wait_ge(y_ready, t + 1)
                for tt in range(TT):
                    for h in range(2):
                        last = mm(acc[tt][h][:, :], STz[:, h, tt * P:(tt + 1) * P], ye, start=False, stop=True,
                                  skip_group_check=True)
                last.then_inc(scat_done, 1)
                selection_t(t + 1)

            with pe.Fori(0, E) as t:
                job(t)
            pe.wait_ge(jobs_ready, 1)
            n_jobs = pe.value_load(n_jobs_i[0:1, :], min_val=E, max_val=E + MAX_EXTRA)
            with pe.If(n_jobs > E):
                with pe.Fori(E, n_jobs) as t:
                    job(t)

        @block.scalar
        def _(act):
            A = nc.scalar.activation
            ch = Chain(act, actc)
            for r0, src in ((0, norm_mix[0]), (8, norm_mem[0]), (16, norm_xattn[0]), (24, norm_moe[0]),
                            (44, norm_conv_out[0]), (48, norm_ssm_out[0]), (52, ssm_d[0])):
                n = src.shape[0] // P
                act.dma_start(rows[r0:r0 + n, :], src.rearrange("(r c) -> r c", c=P)).then_inc(rows_ld, 16)
            act.dma_start(rows[32:44, :], conv_w[0].rearrange("w (r c) -> (w r) c", c=P)).then_inc(rows_ld, 16)
            act.dma_start(par(0), ssm_a_re[0].rearrange("(i w) n -> i (w n)", w=2)).then_inc(par_ld, 16)
            act.dma_start(par(1), ssm_a_im[0].rearrange("(i w) n -> i (w n)", w=2)).then_inc(par_ld, 16)
            act.dma_start(par(2)[:, 0:2], ssm_log_dt[0].rearrange("(i w) -> i w", w=2)).then_inc(par_ld, 16)

            def norm_stats(src, junk, ss, sd, done):
                for t in range(TT):
                    ch.link(A(junk[:, t, :], src[:, t, :], ACT.Square, accum_out=ss[:, t:t + 1]))
                A(sd, ss, ACT.Sqrt, bias=eps, scale=1.0 / D).then_inc(done, 1)

            act.wait_ge(dve_consts, 1)
            act.wait_ge(x_ld, 16)
            norm_stats(x_res, xn, ssx, sdx, x_sd)
            act.wait_ge(mem_ld, 16)
            for t in range(TT):
                ch.link(A(mT[:, 4 * t:4 * t + 4, :].rearrange("p k t -> p (k t)"), mem_n[:, t, :], ACT.Square,
                          accum_out=ssm[:, t:t + 1]))
            A(sdm, ssm, ACT.Sqrt, bias=eps, scale=1.0 / D).then_inc(m_sd, 1)
            act.wait_ge(par_ld, 48)
            A(par(3)[:, 0:2], par(2)[:, 0:2], ACT.Exp).then_inc(dt_ready, 1)
            act.wait_ge(arg_ready, 1)
            A(par(8), par(4), ACT.Exp).then_inc(trig_ready, 1)
            A(par(9), par(6), ACT.Sin).then_inc(trig_ready, 1)
            A(par(10), par(5), ACT.Sin).then_inc(trig_ready, 1)

            def evac(q, dst):
                act.wait_ge(chunk_used, q + 1)
                A(dst, bk[(q + 1) % 4][:, :].rearrange("p (m t) -> p m t", m=2), ACT.Copy).then_inc(proj_used, 1)

            evac(0, uT[:, 0:2, :])
            evac(1, uT[:, 2:4, :])
            for r, b in ((0, 7), (1, 6)):
                act.wait_ge(bct_ps, r + 1)
                A(CTv[:, r], bk[b][:, :].rearrange("p (m c) -> p m c", m=CT), ACT.Copy).then_inc(bct_ready, 1)
            act.wait_ge(consts, 3)
            for r, b in ((0, 4), (1, 5)):
                act.wait_ge(bct_ps, 3 + r)
                for j in range(4):
                    last = A(BT[32 * j:32 * j + 32, :, j, r, :],
                             bk[b][32 * j:32 * j + 32, :].rearrange("p (m s) -> p m s", m=CT), ACT.Copy)
                last.then_inc(bct_ready, 1)
            Csv = Cs[:, :].rearrange("p (m t) -> p m t", m=2)
            for i in range(2):
                q = CONV_CH + 3 * i
                evac(q, Csv)
                act.wait_ge(proj_used, q + 3)
            for q in range(K_CH, K_CH + 4):
                evac(q, kT[:, 2 * (q - K_CH):2 * (q - K_CH) + 2, :])
            act.wait_ge(chunk_used, V_CH + 4)
            for t in range(TT):
                for h in range(2):
                    A(V[:, t, h * HALF:(h + 1) * HALF], bk[2 * t + h][:, :], ACT.Copy).then_inc(v_evac, 1)
            act.wait_ge(yc_ready, 2)
            act.wait_ge(s_ready, ST_TILES)
            ch.link(A(sq_c, ycT, ACT.Square))
            for c in range(CT):
                last = A(ycT[:, c, :], ycT[:, c, :], ACT.Copy, scale=gT[:, 44 + c:45 + c])
            last.then_inc(ycg_ready, 1)
            act.wait_ge(gelu_arg, 1)
            A(ge2, ge2, ACT.Sigmoid).then_inc(gelu_sig, 1)
            act.wait_ge(chunk_used, GLU_CH + 1)
            for i in range(2):
                A(ge[:, 2 * i:2 * i + 2, :], bk[4 + i][:, :].rearrange("p (m t) -> p m t", m=2),
                  ACT.Sigmoid).then_inc(glu_sig, 1)
            act.wait_ge(ys_ready, 1)
            ch.link(A(sq_s, ysT, ACT.Square))
            for c in range(CT):
                last = A(ysT[:, c, :], ysT[:, c, :], ACT.Copy, scale=gT[:, 48 + c:49 + c])
            last.then_inc(ysg_ready, 1)
            act.wait_ge(ss_ps, 2)
            for g in range(2):
                for t in range(TT):
                    last = A(sd_cs[:, 2 * g + t:2 * g + t + 1], bk[6][:, 8 * g + 2 * t:8 * g + 2 * t + 1], ACT.Sqrt,
                             bias=eps, scale=1.0 / D_CONV)
            last.then_inc(ss_sd, 1)
            act.wait_ge(x1_ready, 8)
            norm_stats(x_res, xn2, ssx, sdx, x1_sd)
            for h in range(HEADS):
                act.wait_ge(chunk_used, WQ_CH + h + 1)
                A(QT[:, 2 * h:2 * h + 2, :], bk[4 + h][:, :].rearrange("p (m t) -> p m t", m=2),
                  ACT.Copy).then_inc(qT_ready, 1)
            for h in range(HEADS):
                act.wait_ge(mx_ready, h + 1)
                for t in range(TT):
                    last = A(PA[:, h, t, :], bk[h][:, t * SEQ:(t + 1) * SEQ], ACT.Exp,
                             bias=nmx[:, 2 * h + t:2 * h + t + 1], scale=HD ** -0.5,
                             accum_out=sm[:, 2 * h + t:2 * h + t + 1])
                last.then_inc(exp_ready, 1)
            for h in range(HEADS):
                act.wait_ge(pt_ps, h + 1)
                A(PT[:, h], bk[4 + h][:, :].rearrange("p (m t) -> p m t", m=TT), ACT.Copy).then_inc(pt_ready, 1)
            act.wait_ge(x2_ready, 4)
            norm_stats(x_res, xn2, ssx, sdx, x2_sd)
            act.wait_ge(lmax_ready, 1)
            for t in range(TT):
                last = A(gexp[:, t, :], lg[:, t, :], ACT.Exp, bias=ngm[:, t:t + 1])
            last.then_inc(gexp_ready, 1)

            def job(t):
                act.wait_ge(glu_min, t + 1)
                A(sg, g7, ACT.Sigmoid, scale=ALPHA).then_inc(sig_ready, 1)
                act.wait_ge(chunk_used, t * SLOTS + (N_PRE + SLOTS))
                A(ye, pg_t[:, :], ACT.Copy).then_inc(y_ready, 1)

            with act.Fori(0, E) as t:
                job(t)
            act.wait_ge(jobs_ready, 1)
            n_jobs = act.value_load(n_jobs_i[0:1, :], min_val=E, max_val=E + MAX_EXTRA)
            with act.If(n_jobs > E):
                with act.Fori(E, n_jobs) as t:
                    job(t)
            act.wait_ge(fin_x, 1)
            norm_stats(x_res, xn2, ssx, sdx, fin_sd)

        @block.vector
        def _(dve):
            v = nc.vector
            TTo, TS, STT, TC = v.tensor_tensor, v.tensor_scalar, v.scalar_tensor_tensor, v.tensor_copy
            ch = Chain(dve, dvec)
            v.memset(eps, EPS)
            v.memset(ones2, 1.0)
            v.memset(BDn, 0.0)
            v.memset(vp[:, :], 0.0).then_inc(dve_consts, 1)

            def normalise(src, dst, sd, rs, sd_done, done):
                dve.wait_ge(sd_done, 1)
                ch.link(v.reciprocal(rs, sd))
                for t in range(TT):
                    last = TS(dst[:, t, :], src[:, t, :], rs[:, t:t + 1], None, ALU.mult)
                last.then_inc(done, 1)

            def gained(dst, banks, g0, ps, ready):
                for q, b in enumerate(banks):
                    dve.wait_ge(ps, q + 1)
                    TTo(dst[:, 2 * q:2 * q + 2, :], bk[b][:, :].rearrange("p (k t) -> p k t", k=2),
                        bc_last(gT[:, g0 + 2 * q:g0 + 2 * q + 2], [P, 2, SEQ]), ALU.mult).then_inc(ready, 1)

            dve.wait_ge(dve_consts, 1)
            normalise(x_res, xn, sdx, rsx, x_sd, xn_ready)
            normalise(mem_n, mem_n, sdm, rsm, m_sd, mn_ready)
            dve.wait_ge(rows_t, 1)
            TC(gT[:, :], bk[6][:, 0:56]).then_inc(gT_ready, 1)
            dve.wait_ge(gT_ready, 1)
            gained(hT, (0, 1, 2, 3), 0, xT_ps, xT_ready)

            dve.wait_ge(dt_ready, 1)
            dtb = bc_last(par(3)[:, 0:2], [16, 2, NST])

            def wn(ap):
                return ap.rearrange("p (w n) -> p w n", w=2)
            TTo(wn(par(4)), wn(par(0)), dtb, ALU.mult)
            ch.link(TTo(wn(par(5)), wn(par(1)), dtb, ALU.mult))
            MAGIC = 1.5 * 2.0 ** 23
            HI = 6.28125
            LO = 2 * math.pi - HI
            PI_DOWN = 3.1415925
            ch.link(TS(par(7), par(5), 1.0 / (2 * math.pi), MAGIC, ALU.mult, ALU.add))
            ch.link(TS(par(7), par(7), MAGIC, None, ALU.subtract))
            ch.link(STT(par(5), par(7), -HI, par(5), ALU.mult, ALU.add))
            ch.link(STT(par(5), par(7), -LO, par(5), ALU.mult, ALU.add))
            ch.link(TS(par(6), par(5), math.pi / 2, None, ALU.add))
            ch.link(TS(par(7), par(6), math.pi, -2 * math.pi, ALU.is_gt, ALU.mult))
            ch.link(TTo(par(6), par(6), par(7), ALU.add))
            TS(par(6), par(6), PI_DOWN, -PI_DOWN, ALU.min, ALU.max)
            TS(par(5), par(5), PI_DOWN, -PI_DOWN, ALU.min, ALU.max).then_inc(arg_ready, 1)
            TTo(par(13), par(0), par(0), ALU.mult)
            ch.link(TTo(par(14), par(1), par(1), ALU.mult))
            ch.link(TTo(par(13), par(13), par(14), ALU.add))
            dve.wait_ge(trig_ready, 3)
            TTo(par(4), par(8), par(9), ALU.mult)
            ch.link(TTo(par(7), par(8), par(10), ALU.mult))
            ch.link(TS(par(4), par(4), 1.0, None, ALU.subtract))
            TTo(par(11), par(4), par(0), ALU.mult)
            TTo(par(12), par(7), par(0), ALU.mult)
            TTo(par(5), par(7), par(1), ALU.mult)
            TTo(par(6), par(4), par(1), ALU.mult)
            ch.link(v.reciprocal(par(13), par(13)))
            TTo(par(11), par(11), par(5), ALU.add)
            ch.link(TTo(par(12), par(12), par(6), ALU.subtract))
            TTo(par(11), par(11), par(13), ALU.mult)
            TTo(par(12), par(12), par(13), ALU.mult).then_inc(par_math, 1)

            gained(mT, (4, 5, 7, 0), 8, mT_ps, mT_ready)
            dve.wait_ge(consts, 4)
            dve.wait_ge(bc_ld, 64)
            for r in range(2):
                for w in range(2):
                    last = TS(CNn[:, r, :, w, :], c_nat[:, r], sel_mask[:, 2 * r + w:2 * r + w + 1], None, ALU.mult)
            last.then_inc(cn_ready, 1)
            dve.wait_ge(par_ps, 1)
            ch.link(TC(pT, bk[6][:, 64:144].rearrange("p (q i) -> p q i", q=5)))
            mag, cos1, sin1, q_re, q_im = (pT[:, i, :] for i in range(5))
            shp = [P, ST_TILES, GCH]
            TTo(b_bar[:, 0], b_nat[:, 0], bc_last(q_re, shp), ALU.mult)
            TTo(b_tmp[:, 0], b_nat[:, 1], bc_last(q_im, shp), ALU.mult)
            TTo(b_bar[:, 1], b_nat[:, 1], bc_last(q_re, shp), ALU.mult)
            ch.link(TTo(b_tmp[:, 1], b_nat[:, 0], bc_last(q_im, shp), ALU.mult))
            for w in range(2):
                ps_ = slice(NST * w, NST * (w + 1))
                TTo(BDn[ps_, 0, :, w, :], b_bar[ps_, 0], b_tmp[ps_, 0], ALU.subtract)
                last = TTo(BDn[ps_, 1, :, w, :], b_bar[ps_, 1], b_tmp[ps_, 1], ALU.add)
            last.then_inc(bd_ready, 1)
            v.memset(sinT[:, :, 0:1], 0.0)
            ch.link(TC(sinT[:, :, 1:2], bc_last(sin1, [P, ST_TILES, 1])))
            v.memset(cosT[:, :, 0:1], 1.0)
            TC(cosT[:, :, 1:2], bc_last(cos1, [P, ST_TILES, 1])).then_inc(pT_ready, 1)
            L, lv = 1, 0
            dve.wait_ge(pT_ready, 1)
            while L < SEQ:
                if lv:
                    dve.wait_ge(tab_pool, lv)
                n = min(L, SEQ - 1 - L)
                for i0, i1 in (((0, 16),) if n * ST_TILES <= 1024 else ((0, 8), (8, 16))):
                    s3 = [P, i1 - i0, n]
                    tv = tmp_dve[:, 0:(i1 - i0) * n].rearrange("p (i t) -> p i t", t=n)
                    dst = sinT[:, i0:i1, L + 1:L + 1 + n]
                    TTo(dst, sinT[:, i0:i1, 1:1 + n], cosT[:, i0:i1, L:L + 1].to_broadcast(s3), ALU.mult)
                    ch.link(TTo(tv, cosT[:, i0:i1, 1:1 + n], sinT[:, i0:i1, L:L + 1].to_broadcast(s3), ALU.mult))
                    ch.link(TTo(dst, dst, tv, ALU.add))
                dve.sem_inc(tab_dve, 1)
                L, lv = 2 * L, lv + 1
            dve.wait_ge(tab_pool, lv)

            def rotate_in(i):
                b = i % 2
                dve.wait_ge(bu_ps, i + 1)
                if i >= 2:
                    dve.wait_ge(zin_ready, i - 1)
                src = bk[4 + b][:, :].rearrange("p (r t) -> p r t", r=2)
                TTo(sA[:, b], src, cosT[:, i:i + 1, :].to_broadcast([P, 2, SEQ]), ALU.mult)
                TTo(sB[:, b], src, sinT[:, i:i + 1, :].to_broadcast([P, 2, SEQ]), ALU.mult).then_inc(ab_ready, 1)

            def scan(i):
                b = i % 2
                dve.wait_ge(zin_ready, i + 1)
                if i >= 2:
                    dve.wait_ge(s_ready, i - 1)
                for r in range(2):
                    last = v.tensor_tensor_scan(zz[:, b, r, :], mag[:, i:i + 1].to_broadcast([P, SEQ]),
                                                zin[:, b, r, :], 0.0, ALU.mult, ALU.add)
                last.then_inc(z_ready, 1)
                dve.wait_ge(z_ready, i + 1)
                TTo(Qb[:, b], zz[:, b], sinT[:, i:i + 1, :].to_broadcast([P, 2, SEQ]), ALU.mult).then_inc(q_ready, 1)

            Csv = Cs[:, :].rearrange("p (m t) -> p m t", m=2)
            vpv = vp[:, :].rearrange("p (m t) -> p m t", m=2)

            def conv_x(i):
                q = CONV_CH + 3 * i + 1
                dve.wait_ge(chunk_used, q + 1)
                dve.wait_ge(proj_used, q)
                ch.link(TTo(vpv[:, :, 2:SEQ + 2], bk[(q + 1) % 4][:, :].rearrange("p (m t) -> p m t", m=2), Csv,
                            ALU.mult))
                dve.sem_inc(proj_used, 1)

            def conv_b(i):
                q = CONV_CH + 3 * i + 2
                dve.wait_ge(chunk_used, q + 1)
                for m in range(2):
                    c = 2 * i + m
                    ch.link(TS(cv[:, :], vpv[:, m, 2:SEQ + 2], gT[:, 40 + c:41 + c], None, ALU.mult))
                    ch.link(STT(cv[:, :], vpv[:, m, 1:SEQ + 1], gT[:, 36 + c:37 + c], cv[:, :], ALU.mult, ALU.add))
                    ch.link(STT(cv[:, :], vpv[:, m, 0:SEQ], gT[:, 32 + c:33 + c], cv[:, :], ALU.mult, ALU.add))
                    ch.link(TTo(ycT[:, c, :], bk[(q + 1) % 4][:, m * SEQ:(m + 1) * SEQ], cv[:, :], ALU.mult))
                dve.sem_inc(proj_used, 1)
                dve.sem_inc(yc_ready, 1)

            def y_add(m):
                dve.wait_ge(y_ps, m + 1)
                STT(ysT[:, m, :], uT[:, m, :], gT[:, 52 + m:53 + m], bk[6 + m % 2][:, 0:SEQ], ALU.mult,
                    ALU.add).then_inc(yv_ready, 1)

            for i in range(ST_TILES):
                rotate_in(i)
                if i >= 1:
                    scan(i - 1)
                q = 2 + i // 2
                if i % 2 == 1:
                    if q in (CONV_CH + 1, CONV_CH + 4):
                        conv_x((q - CONV_CH) // 3)
                    if q in (CONV_CH + 2, CONV_CH + 5):
                        conv_b((q - CONV_CH) // 3)
                    if q == 7:
                        y_add(0)
                    if q == 9:
                        y_add(1)
            scan(ST_TILES - 1)
            y_add(2)
            y_add(3)
            dve.wait_ge(yv_ready, 4)
            dve.wait_ge(s_ready, ST_TILES)
            ch.link(TTo(ge, ysT, ysT, ALU.mult))
            ch.link(TS(ge, ge, 0.044715, 1.0, ALU.mult, ALU.add))
            GC = 2.0 * math.sqrt(2.0 / math.pi)
            STT(ge2, ge, GC, ysT, ALU.mult, ALU.mult).then_inc(gelu_arg, 1)
            dve.wait_ge(gelu_sig, 1)
            TTo(yg, ysT, ge2, ALU.mult).then_inc(yg_ready, 1)
            dve.wait_ge(yg_ready, 1)
            for i in range(2):
                dve.wait_ge(glu_sig, i + 1)
                last = TTo(ysT[:, 2 * i:2 * i + 2, :], yg[:, 2 * i:2 * i + 2, :], ge[:, 2 * i:2 * i + 2, :], ALU.mult)
            last.then_inc(ys_ready, 1)
            dve.wait_ge(ss_sd, 1)
            v.reciprocal(r_conv, sd_cs[:, 0:2])
            ch.link(v.reciprocal(r_ssm, sd_cs[:, 2:4]))
            dve.sem_inc(r_ready, 1)
            dve.wait_ge(x2_ld, 16)
            for g, r in ((0, r_conv), (1, r_ssm)):
                dve.wait_ge(chunk_used, WO_CH + 2 * (g + 1))
                for t in range(TT):
                    for h in range(2):
                        xs = x_res[:, t, h * HALF:(h + 1) * HALF]
                        if g:
                            dve.wait_ge(x1_ready, 2 * t + h + 1)
                        STT(xs, bk[4 * g + 2 * t + h][:, :], r[:, t:t + 1], xs, ALU.mult, ALU.add).then_inc(x1_ready, 1)

            def normalise2(sd_done, done):
                dve.wait_ge(sd_done, 1)
                ch.link(v.reciprocal(rsx, sdx))
                for t in range(TT):
                    last = TS(xn2[:, t, :], x_res[:, t, :], rsx[:, t:t + 1], None, ALU.mult)
                last.then_inc(done, 1)

            normalise2(x1_sd, x1n_ready)
            gained(hT, (0, 1, 2, 3), 16, x1T_ps, x1T_ready)
            for h in range(HEADS):
                dve.wait_ge(sc_ps, h + 1)
                ch.link(v.tensor_reduce(mx[:, 2 * h:2 * h + 2], bk[h][:, :].rearrange("p (t m) -> p t m", t=TT),
                                        AX.X, ALU.max))
                TS(nmx[:, 2 * h:2 * h + 2], mx[:, 2 * h:2 * h + 2], -(HD ** -0.5), None,
                   ALU.mult).then_inc(mx_ready, 1)
            for h in range(HEADS):
                dve.wait_ge(exp_ready, h + 1)
                ch.link(v.reciprocal(rsum[:, 2 * h:2 * h + 2], sm[:, 2 * h:2 * h + 2]))
                for t in range(TT):
                    last = TS(PA[:, h, t, :], PA[:, h, t, :], rsum[:, 2 * h + t:2 * h + t + 1], None, ALU.mult)
                last.then_inc(p_ready, 1)
            for h in range(HEADS):
                dve.wait_ge(o_ps, h + 1)
                TC(OT[:, 2 * h:2 * h + 2, :], bk[h][:, :].rearrange("p (d t) -> p d t", d=2)).then_inc(o_ready, 1)
            dve.wait_ge(chunk_used, XO_CH + 4)
            for t in range(TT):
                for h in range(2):
                    xs = x_res[:, t, h * HALF:(h + 1) * HALF]
                    TTo(xs, xs, bk[4 + 2 * t + h][:, :], ALU.add).then_inc(x2_ready, 1)
            normalise2(x2_sd, x2n_ready)
            gained(hT, (0, 1, 2, 3), 24, x2T_ps, x2T_ready)

            dve.wait_ge(wr_ld, 32)
            dve.wait_ge(lg_ps, 1)
            dve.wait_ge(consts, 5)
            v.memset(gates, 0.0)
            v.memset(rankm, -1.0)
            ch.link(TTo(lg, bk[4][:, 0:2 * E].rearrange("p (t e) -> p t e", t=TT),
                        br.unsqueeze(1).to_broadcast([P, TT, E]), ALU.add))
            for t in range(TT):
                last = v.max(top8[:, t, :], lg[:, t, :])
            ch.link(last)
            TS(ngm, top8[:, :, 0:1].rearrange("p t o -> p (t o)"), -1.0, None, ALU.mult).then_inc(lmax_ready, 1)
            fourth = top8[:, :, TOPK - 1:TOPK].to_broadcast([P, TT, E])
            TTo(gt, lg, fourth, ALU.is_gt)
            ch.link(TTo(eq, lg, fourth, ALU.is_equal))
            for t in range(TT):
                v.tensor_tensor_scan(cum[:, t, :], ones96[:, 0:E], eq[:, t, :], 0.0, ALU.mult, ALU.add)
            ch.link(v.tensor_reduce(need, gt, AX.X, ALU.add))
            ch.link(TS(need, need, -1.0, float(TOPK), ALU.mult, ALU.add))
            for t in range(TT):
                last = STT(cum[:, t, :], cum[:, t, :], need[:, t:t + 1], eq[:, t, :], ALU.is_le, ALU.mult)
            ch.link(last)
            ch.link(TTo(maskf, gt, cum, ALU.add))
            TC(mask16, maskf).then_inc(mask_ready, 1)
            dve.wait_ge(gexp_ready, 1)
            ch.link(TTo(gexp, gexp, maskf, ALU.mult))
            ch.link(v.tensor_reduce(gsum, gexp, AX.X, ALU.add))
            ch.link(v.reciprocal(grec, gsum))
            for t in range(TT):
                last = TS(gates[:, t, 0:E], gexp[:, t, :], grec[:, t:t + 1], None, ALU.mult)
            last.then_inc(gates_ready, 1)
            dve.wait_ge(rank_ps, 1)
            TC(cnt, bk[5][:, 2 * E:3 * E])
            ch.link(STT(rankm[:, :, 0:E], bk[5][:, 0:2 * E].rearrange("p (t e) -> p t e", t=TT), 1.0, maskf,
                        ALU.add, ALU.mult))
            ch.link(TS(rankm[:, :, 0:E], rankm[:, :, 0:E], -1.0, None, ALU.add))
            for s in range(3):
                ch.link(TC(xr3[:, :, s, :], xn2))
                if s < 2:
                    ch.link(TTo(xn2, xn2, xr3[:, :, s, :], ALU.subtract))
            dve.sem_inc(xr3_ready, 1)

            def select(t, e):
                for tt in range(TT):
                    last = TS(sel[:, tt, :], iota_c, job_b[:, bass.ds(t, 1)], rankm[:, tt, bass.ds(e, 1)],
                              ALU.add, ALU.is_equal)
                return last

            def select_gated(e):
                for tt in range(TT):
                    last = TS(selG[:, tt], sel[:, tt:tt + 1, :].to_broadcast([P, 2, C]), gates[:, tt, bass.ds(e, 1)],
                              None, ALU.mult)
                return last

            def gathered(t):
                dve.wait_ge(g_ps, t + 1)
                TTo(hTe, pg_g[:, :].rearrange("p (k c) -> p k c", k=KT), bc_last(gT[:, 24:32], [P, KT, C]),
                    ALU.mult).then_inc(hTe_ready, 1)

            def back(t):
                dve.wait_ge(st_ps, t + 1)
                for w in range(2):
                    last = TC(STz[C * w:C * (w + 1), w, :], pg_g[C * w:C * (w + 1), 0:SEQ])
                last.then_inc(st_ready, 1)

            v.memset(STz, 0.0)
            TC(oh_cur, onehot[:, 0:1].to_broadcast([96, C])).then_inc(oh_ready, 1)
            select(0, 0).then_inc(sel_ready, 1)
            dve.wait_ge(sel_ready, 1)
            ch.link(select_gated(0))
            dve.wait_ge(gT_ps, 1)
            TC(gatesT, bk[6][0:E, 0:SEQ]).then_inc(gatesT_ready, 1)
            gathered(0)
            back(0)
            ch.link(TC(job_ei[:, 0:E], job_e[:, 0:E]))
            for c in range(PASSES):
                last = TS(flag[:, c * E:(c + 1) * E], cnt, float(C * (c + 1)), None, ALU.is_gt)
            ch.link(last)
            ch.link(v.tensor_tensor_scan(incl, ones96, flag, 0.0, ALU.mult, ALU.add))
            ch.link(TTo(pos, incl, flag, ALU.subtract))
            dve.wait_ge(seeded, 1)
            jf = [P, 16, 96]
            ch.link(TTo(eqj, pos.unsqueeze(1).to_broadcast(jf), bc_last(iota_j, jf), ALU.is_equal))
            ch.link(TTo(eqj, eqj, flag.unsqueeze(1).to_broadcast(jf), ALU.mult))
            ch.link(TTo(eqi, eqj, id_b.unsqueeze(1).to_broadcast(jf), ALU.mult))
            ch.link(v.tensor_reduce(job_b[:, E:E + 16], eqi, AX.X, ALU.add))
            ch.link(TTo(eqi, eqj, id_e.unsqueeze(1).to_broadcast(jf), ALU.mult))
            ch.link(v.tensor_reduce(job_e[:, E:E + 16], eqi, AX.X, ALU.add))
            TS(n_jobs_i, incl[:, 95:96], float(E), None, ALU.add)
            ch.link(TS(job_ei[:, E:E + 16], job_e[:, E:E + 16], float(E), None, ALU.add))
            dve.sem_inc(jobs_ready, 1)
            dve.wait_ge(jobs_ready, 1)

            lp = Chain(dve, dvel)

            def job(t):
                lp.count = t * DVE_LOOP_LINKS
                e = dve.value_load(job_ei[0:1, bass.ds(t + 1, 1)], min_val=0, max_val=E)
                dve.wait_ge(st_ps, t + 1)
                select(t + 1, e).then_inc(sel_ready, 1)
                dve.wait_ge(sel_ready, t + 2)
                lp.link(select_gated(e))
                dve.wait_ge(chunk_used, t * SLOTS + (N_PRE + KT))
                TS(g7, pg_glu[:, :], LIMIT, None, ALU.min).then_inc(glu_min, 1)
                lp.link(TS(l7, pg_lin[:, :], LIMIT, -LIMIT, ALU.min, ALU.max))
                dve.wait_ge(glu_min, t + 1)
                lp.link(STT(l7, l7, 1.0, g7, ALU.add, ALU.mult))
                dve.wait_ge(sig_ready, t + 1)
                TTo(aa, l7, sg, ALU.mult).then_inc(act_ready, 1)
                TC(oh_cur, onehot[:, bass.ds(e, 1)].to_broadcast([96, C])).then_inc(oh_ready, 1)
                dve.wait_ge(actT_ps, t + 1)
                TC(actT.rearrange("p (w c) s -> p c w s", w=2),
                   pg_t[:, :].rearrange("p (c w s) -> p c w s", c=4, w=2)).then_inc(actT_ready, 1)
                gathered(t + 1)
                dve.wait_ge(scat_done, t + 1)
                back(t + 1)
                return lp.count

            with dve.Fori(0, E) as t:
                job(t)
            n_jobs = dve.value_load(n_jobs_i[0:1, :], min_val=E, max_val=E + MAX_EXTRA)
            with dve.If(n_jobs > E):
                with dve.Fori(E, n_jobs) as t:
                    job(t)
            dve.wait_ge(scat_done, n_jobs)
            for t in range(TT):
                for h in range(2):
                    xs = x_res[:, t, h * HALF:(h + 1) * HALF]
                    last = TTo(xs, xs, acc[t][h][:, :], ALU.add)
            ch.link(last)
            dve.sem_inc(fin_x, 1)
            dve.wait_ge(fin_sd, 1)
            dve.wait_ge(gf_ld, 16)
            ch.link(v.reciprocal(rsx, sdx))
            for t in range(TT):
                last = STT(xn2[:, t, :], x_res[:, t, :], rsx[:, t:t + 1], gfin, ALU.mult, ALU.mult)
            last.then_inc(fin_ready, 1)

        @block.gpsimd
        def _(pool):
            g = nc.gpsimd
            ch = Chain(pool, poolc)
            ch.link(g.memset(ident[:, :], 0.0))
            pool.sem_inc(consts, 1)
            g.affine_select(out=ident[:, :], in_=ident[:, :], compare_op=ALU.not_equal, fill=1.0, base=0,
                            pattern=[[-1, P]], channel_multiplier=1).then_inc(consts, 1)
            for r, src in ((0, ssm_b_re), (1, ssm_b_im)):
                pool.dma_start(b_nat[:, r], src[0].rearrange("(i w) n c -> (w n) i c", w=2)).then_inc(bc_ld, 16)
            for r, src in ((0, ssm_c_re), (1, ssm_c_im)):
                pool.dma_start(c_nat[:, r], src[0].rearrange("(m g) c n -> (g c) m n", m=CT)).then_inc(bc_ld, 16)
            g.memset(BT, 0.0).then_inc(consts, 1)
            mrow = tmp_pool[:, 0:32].rearrange("p (a b) -> p a b", a=4)
            ch.link(g.memset(tmp_pool[:, 0:64], 0.0))
            for w in range(2):
                for a in range(4):
                    lo = 32 * a + 16 * w
                    col = tmp_pool[:, 8 * w + a:8 * w + a + 1]
                    ch.link(g.affine_select(out=col, in_=tmp_pool[:, 32:33], compare_op=ALU.is_gt, fill=1.0,
                                            base=lo, pattern=[[0, 1]], channel_multiplier=-1))
                    ch.link(g.affine_select(out=col, in_=col, compare_op=ALU.is_gt, fill=0.0,
                                            base=lo + 16, pattern=[[0, 1]], channel_multiplier=-1))
            for w in range(2):
                for a in range(4):
                    col = tmp_pool[:, 8 * w + a:8 * w + a + 1]
                    if a == 0:
                        ch.link(g.tensor_copy(sel_mask[:, w:w + 1], col))
                    else:
                        ch.link(g.tensor_tensor(sel_mask[:, w:w + 1], sel_mask[:, w:w + 1], col, ALU.add))
            ch.link(g.tensor_scalar(sel_mask[:, 2:4], sel_mask[:, 0:2], -1.0, None, ALU.mult))
            pool.sem_inc(consts, 1)
            L, lv = 1, 0
            pool.wait_ge(pT_ready, 1)
            while L < SEQ:
                if lv:
                    pool.wait_ge(tab_dve, lv)
                n = min(L, SEQ - 1 - L)
                for i0, i1 in (((0, 16),) if n * ST_TILES <= 1024 else ((0, 8), (8, 16))):
                    s3 = [P, i1 - i0, n]
                    tv = tmp_pool[:, 0:(i1 - i0) * n].rearrange("p (i t) -> p i t", t=n)
                    dst = cosT[:, i0:i1, L + 1:L + 1 + n]
                    g.tensor_tensor(dst, cosT[:, i0:i1, 1:1 + n], cosT[:, i0:i1, L:L + 1].to_broadcast(s3), ALU.mult)
                    ch.link(g.tensor_tensor(tv, sinT[:, i0:i1, 1:1 + n], sinT[:, i0:i1, L:L + 1].to_broadcast(s3),
                                            ALU.mult))
                    ch.link(g.tensor_tensor(dst, dst, tv, ALU.subtract))
                pool.sem_inc(tab_pool, 1)
                L, lv = 2 * L, lv + 1
            pool.wait_ge(tab_dve, lv)

            def rotate_sum(i):
                b = i % 2
                pool.wait_ge(ab_ready, i + 1)
                if i >= 2:
                    pool.wait_ge(z_ready, i - 1)
                g.tensor_tensor(zin[:, b, 0, :], sA[:, b, 0, :], sB[:, b, 1, :], ALU.add)
                g.tensor_tensor(zin[:, b, 1, :], sA[:, b, 1, :], sB[:, b, 0, :], ALU.subtract).then_inc(zin_ready, 1)

            def states(i):
                b = i % 2
                pool.wait_ge(z_ready, i + 1)
                ch.link(g.tensor_tensor(Pb, zz[:, b], cosT[:, i:i + 1, :].to_broadcast([P, 2, SEQ]), ALU.mult))
                pool.wait_ge(q_ready, i + 1)
                if i >= 4:
                    pool.wait_ge(y_ps, i // 4)
                else:
                    pool.wait_ge(xn_ready, 1)
                g.tensor_tensor(s4[:, i % 4, 0, :], Pb[:, 0, :], Qb[:, b, 1, :], ALU.subtract)
                g.tensor_tensor(s4[:, i % 4, 1, :], Pb[:, 1, :], Qb[:, b, 0, :], ALU.add).then_inc(s_ready, 1)
                pool.wait_ge(s_ready, i + 1)

            for i in range(ST_TILES):
                rotate_sum(i)
                if i >= 1:
                    states(i - 1)
            states(ST_TILES - 1)
            pool.wait_ge(y_ps, 4)
            pool.dma_start(x_res, x[0].rearrange("(t p) n -> p t n", p=P)).then_inc(x2_ld, 16)
            pool.wait_ge(bu_ps, ST_TILES)
            for s in range(3):
                pool.dma_start(bg_raw[E * s:E * (s + 1), :], b_gu[0]).then_inc(bg_ld, 16)
            pool.wait_ge(chunk_used, V_CH + 4)
            pool.dma_start(bdown, b_down[0]).then_inc(bd_ld, 16)
            pool.wait_ge(bg_ld, 48)
            ch.link(g.tensor_copy(bias3, bg_raw))
            for s in (1, 2):
                for q in range(s, 3):
                    rows_q = slice(E * q, E * (q + 1))
                    ch.link(g.tensor_tensor(bg_raw[rows_q, :], bg_raw[rows_q, :], bias3[rows_q, :], ALU.subtract))
                    ch.link(g.tensor_copy(bias3[rows_q, :], bg_raw[rows_q, :]))
            pool.sem_inc(bias_ready, 1)
            pool.dma_start(wr, w_router[0].rearrange("(k p) e -> p k e", p=P)).then_inc(wr_ld, 16)
            pool.dma_start(br, b_router[0].partition_broadcast(P)).then_inc(wr_ld, 16)
            pool.dma_start(gfin, norm_final.partition_broadcast(P)).then_inc(gf_ld, 16)
            pool.wait_ge(chunk_used, N_PRE)
            g.memset(tri, 1.0)
            g.memset(ones_b, 1.0)
            g.memset(ones96, 1.0)
            g.memset(job_b, 0.0)
            ch.link(g.memset(onehot, 0.0))
            g.affine_select(out=tri, in_=tri, compare_op=ALU.is_gt, fill=0.0, base=0, pattern=[[1, P]],
                            channel_multiplier=-1)
            for s in range(3):
                ch.link(g.affine_select(out=onehot[:, 0:E], in_=onehot[:, 0:E], compare_op=ALU.not_equal, fill=1.0,
                                        base=-E * s, pattern=[[-1, E]], channel_multiplier=1))
            g.iota(iota_c, [[1, C]], base=0, channel_multiplier=0, allow_small_or_imprecise_dtypes=True)
            g.iota(iota_j, [[1, 16]], base=0, channel_multiplier=0, allow_small_or_imprecise_dtypes=True)
            g.iota(job_e, [[1, JT]], base=0, channel_multiplier=0, allow_small_or_imprecise_dtypes=True)
            g.iota(id_e, [[0, PASSES], [1, E]], base=-E, channel_multiplier=0, allow_small_or_imprecise_dtypes=True)
            ch.link(g.iota(id_b, [[C, PASSES], [0, E]], base=C, channel_multiplier=0,
                           allow_small_or_imprecise_dtypes=True))
            pool.sem_inc(consts, 1)


_INS = ["x", "mem", "norm_mix", "w_in", "conv_w", "ssm_a_re", "ssm_a_im", "ssm_log_dt", "ssm_b_re", "ssm_b_im",
        "ssm_c_re", "ssm_c_im", "ssm_d", "w_glu", "norm_conv_out", "norm_ssm_out", "w_out", "norm_xattn", "norm_mem",
        "w_q", "w_kv", "w_o", "norm_moe", "w_router", "b_router", "w_gu", "b_gu", "w_down", "b_down", "norm_final"]


def kernel(**inputs):
    import numpy as _np
    import concourse.bacc as _bacc
    from concourse import mybir as _mybir
    from concourse.bass_utils import run_bass_kernel_spmd as _run

    nc = _bacc.Bacc("TRN2", target_bir_lowering=False, num_devices=1)
    arrays, args = {}, []
    for name in _INS:
        a = _np.ascontiguousarray(inputs[name])
        arrays[f"in_{name}"] = a
        args.append(nc.dram_tensor(f"in_{name}", a.shape, _mybir.dt.from_np(a.dtype), kind="ExternalInput").ap())
    out = nc.dram_tensor("out_0", (1, SEQ, D), F32, kind="ExternalOutput").ap()
    hybrid_layer(nc, *args, out)
    r = _run(nc, [arrays], core_ids=[0])
    return r.results[0]["out_0"]
```

```python
import math
from contextlib import ExitStack

import concourse.bass as bass
from concourse import mybir

F32 = mybir.dt.float32
BF16 = mybir.dt.bfloat16
I32 = mybir.dt.int32
ALU = mybir.AluOpType
ACT = mybir.ActivationFunctionType
AX = mybir.AxisListType

P = 128
D = 1024
SEQ = 256
TT = SEQ // P
KT = D // P
HALF = 512
D_CONV = 512
CT = D_CONV // P
GROUPS, GCH, NST = 32, 16, 64
ST_TILES = GROUPS * NST // P
HEADS, HD = 4, 256
E = 32
C = 64
TOPK = 4
LIMIT, ALPHA = 7.0, 1.702
EPS = 1e-5
MAX_EXTRA = SEQ * TOPK // (C + 1)
PASSES = SEQ // C - 1
JT = E + MAX_EXTRA + 1

PRE_SLOTS = 9
SLOTS = 12
U_CH, CONV_CH, K_CH, V_CH, GLU_CH, WO_CH, WQ_CH, XO_CH = 0, 2, 8, 12, 16, 17, 21, 25
N_PRE = 29
X_SLOTS = SLOTS // 2
X_JOBS = 4
TURN = X_SLOTS * (X_JOBS % 2)
TILE_JOB = 5
DVE_LOOP_LINKS = 3


class Chain:

    def __init__(self, engine, sem):
        self.engine, self.sem, self.count = engine, sem, 0

    def link(self, instruction):
        instruction.then_inc(self.sem, 1)
        self.count = self.count + 1
        self.engine.wait_ge(self.sem, self.count)


def hybrid_layer(nc, x, mem, norm_mix, w_in, conv_w, ssm_a_re, ssm_a_im, ssm_log_dt, ssm_b_re, ssm_b_im,
                 ssm_c_re, ssm_c_im, ssm_d, w_glu, norm_conv_out, norm_ssm_out, w_out, norm_xattn, norm_mem,
                 w_q, w_kv, w_o, norm_moe, w_router, b_router, w_gu, b_gu, w_down, b_down, norm_final, out):
    ctx = ExitStack()
    with ctx:
        def sb(name, cols, dt=F32, parts=P):
            return ctx.enter_context(nc.sbuf_tensor(name, [parts, cols], dt))

        def sem(name):
            return ctx.enter_context(nc.semaphore(name))

        W = ctx.enter_context(nc.sbuf_tensor("W", [P, SLOTS, 2 * D], F32))
        R1 = sb("R1", 12288)
        XR = sb("XR", TT * D)
        HT = sb("HT", KT * SEQ)
        MT = sb("MT", KT * SEQ)
        KR = sb("KR", KT * SEQ)
        VR = sb("VR", KT * SEQ)
        R3 = sb("R3", 3 * CT * SEQ)
        CTm = sb("CTm", 2 * CT * P)
        ident = sb("ident", P)
        small = sb("small", 256)
        gT = sb("gT", 56)
        Cs = sb("Cs", 2 * SEQ)
        vp = sb("vp", 2 * (SEQ + 2))
        cv = sb("cv", SEQ)
        SCR = W[:, PRE_SLOTS:SLOTS, :].rearrange("p s n -> p (s n)")

        x_res = XR[:, :].rearrange("p (t n) -> p t n", t=TT)
        hT = HT[:, :].rearrange("p (k t) -> p k t", k=KT)
        mT = MT[:, :].rearrange("p (k t) -> p k t", k=KT)
        xn = KR[:, :].rearrange("p (t n) -> p t n", t=TT)
        mem_n = VR[:, :].rearrange("p (t n) -> p t n", t=TT)
        kT = KR[:, :].rearrange("p (k t) -> p k t", k=KT)
        V = VR[:, :].rearrange("p (t n) -> p t n", t=TT)
        uT = R3[:, 0:1024].rearrange("p (c t) -> p c t", c=CT)
        ycT = R3[:, 1024:2048].rearrange("p (c t) -> p c t", c=CT)
        ysT = R3[:, 2048:3072].rearrange("p (c t) -> p c t", c=CT)
        tmp_dve = R3[:, 1024:2048]
        tmp_pool = R3[:, 2048:3072]
        cosT = R1[:, 0:4096].rearrange("p (i t) -> p i t", i=ST_TILES)
        sinT = R1[:, 4096:8192].rearrange("p (i t) -> p i t", i=ST_TILES)
        BT = R1[:, 8192:12288].rearrange("p (m j r s) -> p m j r s", m=CT, j=4, r=2)
        CTv = CTm[:, :].rearrange("p (r m c) -> p r m c", r=2, m=CT)

        ssx, sdx, rsx = small[:, 0:2], small[:, 2:4], small[:, 4:6]
        ssm, sdm, rsm = small[:, 6:8], small[:, 8:10], small[:, 10:12]
        eps = small[:, 12:13]
        spare = small[:, 13:14]
        r16 = small[:, 28:30]
        ones2 = small[:, 14:16]
        sel_mask = small[:, 16:20]
        r_conv, r_ssm, sd_cs = small[:, 20:22], small[:, 22:24], small[:, 24:28]
        mx, nmx, sm, rsum = small[:, 32:40], small[:, 40:48], small[:, 48:56], small[:, 56:64]
        pT = small[:, 64:144].rearrange("p (q i) -> p q i", q=5)

        BDn = SCR[:, 0:1024].rearrange("p (r i w c) -> p r i w c", r=2, i=ST_TILES, w=2)
        CNn = SCR[:, 1024:2048].rearrange("p (r m w n) -> p r m w n", r=2, m=CT, w=2)
        b_nat = SCR[:, 2048:2560].rearrange("p (r i c) -> p r i c", r=2, i=ST_TILES)
        b_bar = SCR[:, 2560:3072].rearrange("p (r i c) -> p r i c", r=2, i=ST_TILES)
        b_tmp = SCR[:, 3072:3584].rearrange("p (r i c) -> p r i c", r=2, i=ST_TILES)
        c_nat = SCR[:, 3584:4096].rearrange("p (r m n) -> p r m n", r=2, m=CT)
        rows = SCR[0:56, 4096:4224]
        PR = SCR[0:16, 4224:6144]

        def par(i):
            return PR[:, P * i:P * (i + 1)]

        sA = SCR[:, 0:1024].rearrange("p (b r t) -> p b r t", b=2, r=2)
        sB = SCR[:, 1024:2048].rearrange("p (b r t) -> p b r t", b=2, r=2)
        zin = SCR[:, 2048:3072].rearrange("p (b r t) -> p b r t", b=2, r=2)
        zz = SCR[:, 3072:4096].rearrange("p (b r t) -> p b r t", b=2, r=2)
        Qb = SCR[:, 4096:5120].rearrange("p (b r t) -> p b r t", b=2, r=2)
        Pb = SCR[:, 5120:5632].rearrange("p (r t) -> p r t", r=2)
        s4 = [R[:, :].rearrange("p (j r t) -> p j r t", j=4, r=2) for R in (XR, VR)]
        ge = SCR[:, 0:1024].rearrange("p (c t) -> p c t", c=CT)
        ge2 = SCR[:, 1024:2048].rearrange("p (c t) -> p c t", c=CT)
        yg = SCR[:, 2048:3072].rearrange("p (c t) -> p c t", c=CT)
        sq_s = SCR[:, 3072:4096].rearrange("p (c t) -> p c t", c=CT)
        sq_c = SCR[:, 4096:5120].rearrange("p (c t) -> p c t", c=CT)

        QT = R1[:, 0:2048].rearrange("p (k t) -> p k t", k=KT)
        PA = R1[:, 2048:4096].rearrange("p (h t m) -> p h t m", h=HEADS, t=TT)
        PT = R1[:, 4096:6144].rearrange("p (h m t) -> p h m t", h=HEADS, m=TT)
        OT = R1[:, 6144:8192].rearrange("p (k t) -> p k t", k=KT)
        xn2 = R1[:, 8192:10240].rearrange("p (t n) -> p t n", t=TT)

        bg_raw = R1[0:96, 10240:12288]
        bias3 = MT[0:96, 0:1024].bitcast(BF16)
        bdown = MT[0:E, 1024:2048]

        xr3 = R3[:, :].bitcast(BF16).rearrange("p (t s n) -> p t s n", t=TT, s=3)
        wr = Cs[:, 0:256].rearrange("p (k e) -> p k e", k=KT)
        br = Cs[:, 256:288]
        gfin = CTm[:, :]
        out_n = W[:, 4:4 + TT, 0:D]
        junk_n = W[:, 0:TT, 0:D]
        X = [R1[:, c:c + 2 * D] for c in (10240, 2048, 4096, 6144)]
        X += [HT[:, :], R1[:, 8192:10240]]
        EB = R1[:, 0:2048]
        lg = EB[:, 0:64].rearrange("p (t e) -> p t e", t=TT)
        top8 = EB[:, 64:80].rearrange("p (t e) -> p t e", t=TT)
        gt = EB[:, 80:144].rearrange("p (t e) -> p t e", t=TT)
        eq = EB[:, 144:208].rearrange("p (t e) -> p t e", t=TT)
        cum = EB[:, 208:272].rearrange("p (t e) -> p t e", t=TT)
        need = EB[:, 272:274]
        maskf = EB[:, 288:352].rearrange("p (t e) -> p t e", t=TT)
        mask16 = EB[:, 352:384].bitcast(BF16).rearrange("p (t e) -> p t e", t=TT)
        gates = EB[:, 384:450].rearrange("p (t e) -> p t e", t=TT)
        rankm = EB[:, 450:516].rearrange("p (t e) -> p t e", t=TT)
        gexp = EB[:, 516:580].rearrange("p (t e) -> p t e", t=TT)
        gsum, grec, ngm = EB[:, 580:582], EB[:, 582:584], EB[:, 584:586]
        cnt = EB[:, 586:618]
        flag = EB[:, 618:714]
        incl = EB[:, 714:810]
        pos = EB[:, 810:906]
        id_e = EB[:, 906:1002]
        id_b = EB[:, 1002:1098]
        iota_j = EB[:, 1098:1114]
        iota_c = EB[:, 1114:1178]
        job_e = EB[:, 1178:1178 + JT]
        job_b = EB[:, 1242:1242 + JT]
        job_ei = EB[:, 1306:1306 + JT].bitcast(I32)
        n_jobs_i = EB[:, 1370:1371].bitcast(I32)
        ones96 = EB[:, 1376:1472]
        tri = EB[:, 1472:1536].bitcast(BF16)
        ones_b = EB[:, 1536:1600].bitcast(BF16)
        onehot = EB[0:96, 1600:1664].bitcast(BF16)[:, 0:E + 1]
        oh_cur = EB[0:96, 1664:1696].bitcast(BF16)
        sel = EB[:, 1696:1760].bitcast(BF16).rearrange("p (t c) -> p t c", t=TT)
        selG = EB[:, 1760:2016].rearrange("p (t w c) -> p t w c", t=TT, w=2)
        eqj = KR[:, 0:768].rearrange("p (j f) -> p j f", j=8)
        eqi = KR[:, 768:1536].rearrange("p (j f) -> p j f", j=8)
        gatesT = VR[0:E, 1024:1280]

        g7 = KR[:, 0:512]
        sg = KR[:, 512:1024]
        l7 = KR[:, 1024:1536]
        aa = KR[:, 1536:2048]
        actT = VR[:, 0:512].rearrange("p (k c) -> p k c", k=KT)
        hTe = VR[:, 512:1024].rearrange("p (k c) -> p k c", k=KT)
        ye = VR[:, 1024:1536]
        STz = VR[:, 1536:2048].rearrange("p (w t) -> p w t", w=2)

        bk = [ctx.enter_context(nc.psum_tensor(f"bank{i}", [P, HALF], F32)) for i in range(8)]
        acc = [[bk[2 * t + h] for h in range(2)] for t in range(TT)]
        pg_glu, pg_lin, pg_t, pg_g = bk[4], bk[5], bk[6], bk[7]

        full = [sem(f"slot{i}_full") for i in range(SLOTS)]
        x_full = [sem(f"x_slot{i}_full") for i in range(X_SLOTS)]
        chunk_used = sem("chunk_used")
        x_ld = [sem(f"x_tile{t}_ld") for t in range(TT)]
        mem_ld, rows_ld, par_ld, bc_ld = sem("mem_ld"), sem("rows_ld"), sem("par_ld"), sem("bc_ld")
        x2_ld, bg_ld, bd_ld, wr_ld, gf_ld = sem("x2_ld"), sem("bg_ld"), sem("bd_ld"), sem("wr_ld"), sem("gf_ld")
        consts, dve_consts, dvec, actc, poolc = sem("consts"), sem("dve_consts"), sem("dve_step"), sem("act_step"), sem("pool_step")
        dvel = sem("dve_loop_step")
        x_sd, m_sd, xn_ready, mn_ready = sem("x_sd"), sem("m_sd"), sem("xn_ready"), sem("mn_ready")
        rows_t, gT_ready, xT_ps, xT_ready, mT_ps, mT_ready = sem("rows_t"), sem("gT_ready"), sem("xT_ps"), sem("xT_ready"), sem("mT_ps"), sem("mT_ready")
        dt_ready, arg_ready, trig_ready, par_math, par_ps, pT_ready = sem("dt_ready"), sem("arg_ready"), sem("trig_ready"), sem("par_math"), sem("par_ps"), sem("pT_ready")
        bd_ready, cn_ready, bct_ps, bct_ready = sem("bd_ready"), sem("cn_ready"), sem("bct_ps"), sem("bct_ready")
        tab_dve, tab_pool = sem("tab_dve"), sem("tab_pool")
        proj_ps, proj_used = sem("proj_ps"), sem("proj_used")
        bu_ps, ab_ready, zin_ready, z_ready, q_ready, s_ready = sem("bu_ps"), sem("ab_ready"), sem("zin_ready"), sem("z_ready"), sem("q_ready"), sem("s_ready")
        y_ps, yv_ready, gelu_arg, gelu_sig, yg_ready = sem("y_ps"), sem("yv_ready"), sem("gelu_arg"), sem("gelu_sig"), sem("yg_ready")
        yc_ready, ycg_ready = sem("yc_ready"), sem("ycg_ready")
        v_ps, v_evac = sem("v_ps"), sem("v_evac")
        glu_ps, glu_sig, ys_ready, ysg_ready = sem("glu_ps"), sem("glu_sig"), sem("ys_ready"), sem("ysg_ready")
        ss_ps, ss_sd, r_ready = sem("ss_ps"), sem("ss_sd"), sem("r_ready")
        mix_ps, x1_ready = sem("mix_ps"), sem("x1_ready")
        x1_sd, x1n_ready, x1T_ps, x1T_ready = sem("x1_sd"), sem("x1n_ready"), sem("x1T_ps"), sem("x1T_ready")
        q_ps, qT_ready, sc_ps, mx_ready, exp_ready, p_ready = sem("q_ps"), sem("qT_ready"), sem("sc_ps"), sem("mx_ready"), sem("exp_ready"), sem("p_ready")
        pt_ps, pt_ready, o_ps, o_ready, xo_ps, x2_ready = sem("pt_ps"), sem("pt_ready"), sem("o_ps"), sem("o_ready"), sem("xo_ps"), sem("x2_ready")
        x2_sd, x2n_ready, x2T_ps, x2T_ready = sem("x2_sd"), sem("x2n_ready"), sem("x2T_ps"), sem("x2T_ready")
        part_hi = [sem(f"part_copied_tile{t}") for t in range(TT)]
        part_sub = [sem(f"part_subtracted_tile{t}") for t in range(TT)]
        lg_ps, lmax_ready, gexp_ready, mask_ready, rank_ps, xr3_ready = sem("lg_ps"), sem("lmax_ready"), sem("gexp_ready"), sem("mask_ready"), sem("rank_ps"), sem("xr3_ready")
        gates_ready, gT_ps, gatesT_ready = sem("gates_ready"), sem("gatesT_ps"), sem("gatesT_ready")
        bias_ready, jobs_ready = sem("bias_ready"), sem("jobs_ready")
        sel_ready, oh_ready, g_ps, hTe_ready, st_ps, st_ready = sem("sel_ready"), sem("onehot_ready"), sem("gather_ps"), sem("hTe_ready"), sem("st_ps"), sem("st_ready")
        glu_min, sig_ready, act_ready, actT_ps, actT_ready = sem("glu_min"), sem("sig_ready"), sem("act_ready"), sem("actT_ps"), sem("actT_ready")
        y_ready = sem("y_ready")
        scattered = [sem(f"scattered_to_tile{t}") for t in range(TT)]
        fin_x, fin_sd, fin_ready, out_done = sem("fin_x"), sem("fin_sd"), sem("fin_ready"), sem("out_done")

        block = ctx.enter_context(nc.Block())

        COS_DVE = 4

        def shared(step):
            return step >= 32

        def bc_last(ap, shape):
            return ap.unsqueeze(len(ap.shape)).to_broadcast(shape)

        def home(t, c):
            if isinstance(t, int) and t <= X_JOBS:
                return c if t == 0 else c - X_SLOTS + X_SLOTS * (t % 2 == 0)
            return (c + TURN) % SLOTS

        def in_ring(t, c):
            return t == 0 or t > X_JOBS or c >= X_SLOTS

        filled = [sum(1 for n in range(N_PRE) if s < PRE_SLOTS and n % PRE_SLOTS == s)
                  + sum(1 for t in range(X_JOBS + 1) for c in range(SLOTS) if in_ring(t, c) and home(t, c) == s)
                  for s in range(SLOTS)]

        def fill_count(t, c):
            s = home(t, c)
            return filled[s] - sum(1 for u in range(t + 1, X_JOBS + 1) for d in range(SLOTS)
                                   if in_ring(u, d) and home(u, d) == s)

        @block.sync
        def _(sp):
            sp.dma_start(par(0), ssm_a_re[0].rearrange("(i w) n -> i (w n)", w=2)).then_inc(par_ld, 16)
            sp.dma_start(par(1), ssm_a_im[0].rearrange("(i w) n -> i (w n)", w=2)).then_inc(par_ld, 16)
            sp.dma_start(par(2)[:, 0:2], ssm_log_dt[0].rearrange("(i w) -> i w", w=2)).then_inc(par_ld, 16)
            for r0, src in ((0, norm_mix[0]), (8, norm_mem[0]), (16, norm_xattn[0]), (24, norm_moe[0]),
                            (44, norm_conv_out[0]), (48, norm_ssm_out[0]), (52, ssm_d[0])):
                n = src.shape[0] // P
                sp.dma_start(rows[r0:r0 + n, :], src.rearrange("(r c) -> r c", c=P)).then_inc(rows_ld, 16)
            sp.dma_start(rows[32:44, :], conv_w[0].rearrange("w (r c) -> (w r) c", c=P)).then_inc(rows_ld, 16)
            sp.dma_start(mem_n, mem[0].rearrange("(t p) n -> p t n", p=P)).then_inc(mem_ld, 16)

            def slot(n):
                return W[:, n % PRE_SLOTS, :]

            def cols(w, c0):
                return w.rearrange("(k p) n -> p k n", p=P)[:, :, c0:c0 + 256], KT

            def two_rows(w, k0, c0):
                return w.rearrange("(k p) n -> p k n", p=P)[:, k0:k0 + 2, c0:c0 + D], 2

            chunks = [cols(w_in[0], 3 * D_CONV + 256 * i) for i in range(2)]
            chunks += [cols(w_in[0], base + 256 * i) for i in range(2) for base in (D_CONV, 2 * D_CONV, 0)]
            chunks += [cols(w_kv[0], 256 * i) for i in range(4)]
            chunks += [two_rows(w_kv[0], 2 * i, D) for i in range(4)]
            chunks += [(w_glu[0].rearrange("(k p) n -> p k n", p=P), CT)]
            chunks += [two_rows(w_out[0], 2 * i, 0) for i in range(4)]
            chunks += [cols(w_q[0], 256 * i) for i in range(4)]
            chunks += [two_rows(w_o[0], 2 * i, 0) for i in range(4)]
            assert len(chunks) == N_PRE
            for n, (src, k) in enumerate(chunks):
                if n == 2:
                    sp.wait_ge(bc_ld, 16 * 4)
                if n >= PRE_SLOTS:
                    sp.wait_ge(chunk_used, n - PRE_SLOTS + 1)
                sp.dma_start(slot(n).rearrange("p (k n) -> p k n", k=k), src).then_inc(full[n % PRE_SLOTS], 16)

            def expert_chunk(e, c, dst, done):
                if c < KT:
                    src = w_gu[0][bass.ds(e, 1), P * c:P * (c + 1), :].rearrange("o p n -> p (o n)")
                    sp.dma_start(dst, src).then_inc(done, 16)
                else:
                    k0 = 2 * (c - KT)
                    src = w_down[0][bass.ds(e, 1), P * k0:P * (k0 + 2), :].rearrange("o (k p) n -> p (o k) n", p=P)
                    sp.dma_start(dst.rearrange("p (k n) -> p k n", k=2), src).then_inc(done, 16)

            def ring_chunk(e, c, s):
                expert_chunk(e, c, W[:, s, :], full[s])

            def last_chunk(c):
                return max(n for n in range(N_PRE) if n % PRE_SLOTS == c)

            x_free = ((bias_ready, 1), (pt_ps, HEADS), (o_ps, HEADS), (chunk_used, N_PRE), (lg_ps, 1), (xr3_ready, 2))
            scratch_slots = list(range(PRE_SLOTS, SLOTS))
            by_use = sorted(range(PRE_SLOTS), key=last_chunk)
            before_wo = [c for c in by_use if last_chunk(c) < XO_CH]
            after_wo = [c for c in by_use if last_chunk(c) >= XO_CH]

            def first_job(c):
                if c < PRE_SLOTS:
                    sp.wait_ge(chunk_used, last_chunk(c) + 1)
                elif c == PRE_SLOTS:
                    sp.wait_ge(ss_ps, 2)
                ring_chunk(0, c, home(0, c))

            def further(c):
                sp.wait_ge(*x_free[c])
                expert_chunk(1, c, X[c], x_full[c])

            for c in scratch_slots + before_wo:
                first_job(c)
            for c in range(3):
                further(c)
            for c in after_wo:
                first_job(c)
            for c in range(3, X_SLOTS):
                further(c)
            for t in range(1, X_JOBS + 1):
                for c in range(X_SLOTS, SLOTS):
                    used = c - X_SLOTS if t == 1 else (t - 2) * SLOTS + c
                    sp.wait_ge(chunk_used, N_PRE + used + 1)
                    ring_chunk(t, c, home(t, c))
                if t > 1:
                    for c in range(X_SLOTS):
                        sp.wait_ge(chunk_used, N_PRE + (t - 1) * SLOTS + c + 1)
                        expert_chunk(t, c, X[c], x_full[c])
            for c in range(SLOTS):
                used = (X_JOBS - 1) * SLOTS + X_SLOTS + c if c < X_SLOTS else X_JOBS * SLOTS + c
                sp.wait_ge(chunk_used, N_PRE + used + 1)
                ring_chunk(X_JOBS + 1, c, home(X_JOBS + 1, c))

            def later_job(t, e):
                for c in range(SLOTS):
                    sp.wait_ge(chunk_used, t * SLOTS + (N_PRE - SLOTS + c + 1))
                    ring_chunk(e, c, home(t, c))

            with sp.Fori(X_JOBS + 2, E) as t:
                later_job(t, t)
            sp.wait_ge(jobs_ready, 1)
            n_jobs = sp.value_load(n_jobs_i[0:1, :], min_val=E, max_val=E + MAX_EXTRA)
            with sp.If(n_jobs > E):
                with sp.Fori(E, n_jobs) as t:
                    later_job(t, sp.value_load(job_ei[0:1, bass.ds(t, 1)], min_val=0, max_val=E - 1))
            for t in range(TT):
                sp.wait_ge(fin_ready, t + 1)
                sp.dma_start(out[0, t * P:(t + 1) * P, :], out_n[:, t, :]).then_inc(out_done, 16)
            sp.wait_ge(out_done, 16 * TT)

        @block.tensor
        def _(pe):
            mm, tr = nc.tensor.matmul, nc.tensor.transpose

            def chunk(n):
                pe.wait_ge(full[n % PRE_SLOTS], 16 * (n // PRE_SLOTS + 1))
                return W[:, n % PRE_SLOTS, :]

            pe.wait_ge(consts, 2)
            pe.wait_ge(rows_ld, 16 * 8)
            tr(bk[6][:, 0:56], rows, ident[0:56, 0:56]).then_inc(rows_t, 1)

            def transpose_tokens(src, banks, done, ready, base, halves):
                for t in range(TT):
                    for q, b in enumerate(banks):
                        if halves and q % 2 == 0:
                            pe.wait_ge(ready, base + 2 * t + q // 2 + 1)
                        elif not halves and q == 0:
                            pe.wait_ge(ready, base + t + 1)
                        for k in range(2):
                            last = tr(bk[b][:, k * SEQ + t * P:k * SEQ + (t + 1) * P],
                                      src[:, t, (2 * q + k) * P:(2 * q + k + 1) * P], ident[:, :])
                        if t == TT - 1:
                            last.then_inc(done, 1)

            transpose_tokens(xn, (0, 1, 2, 3), xT_ps, xn_ready, 0, False)

            def proj(q, n, act):
                w = chunk(n).rearrange("p (k n) -> p k n", k=KT)
                if q >= 4:
                    pe.wait_ge(proj_used, q - 3)
                for m in range(2):
                    for k in range(KT):
                        if q in (0, K_CH) and m == 0 and k % 2 == 0:
                            pe.wait_ge(xT_ready if q == 0 else mT_ready, k // 2 + 1)
                        last = mm(bk[q % 4][:, m * SEQ:(m + 1) * SEQ], w[:, k, m * P:(m + 1) * P],
                                  act[:, k, :], start=(k == 0), stop=(k == KT - 1))
                last.then_inc(chunk_used, 1)

            proj(0, 0, hT)
            proj(1, 1, hT)
            pe.wait_ge(par_math, 1)
            for i in range(5):
                last = tr(bk[6][:, 64 + 16 * i:80 + 16 * i], par(8 + i), ident[0:16, 0:16])
            last.then_inc(par_ps, 1)
            proj(2, 2, hT)
            pe.wait_ge(cn_ready, 1)
            for r, b in ((0, 7), (1, 6)):
                if r == 1:
                    pe.wait_ge(pT_ready, 1)
                for m in range(CT):
                    last = tr(bk[b][:, m * P:(m + 1) * P], CNn[:, r, m].rearrange("p w n -> p (w n)"), ident[:, :])
                last.then_inc(bct_ps, 1)
            pe.wait_ge(bd_ready, 1)
            for r, b in ((0, 4), (1, 5)):
                for m in range(CT):
                    last = tr(bk[b][:, m * P:(m + 1) * P],
                              BDn[:, r, 4 * m:4 * m + 4].rearrange("p i w c -> p (i w c)"), ident[:, :])
                last.then_inc(bct_ps, 1)
            proj(3, 3, hT)
            proj(4, 4, hT)
            pe.wait_ge(bct_ready, 4)
            transpose_tokens(mem_n, (4, 5, 6, 7), mT_ps, mn_ready, 0, False)

            def b_u(i):
                if i >= 2:
                    pe.wait_ge(ab_ready, i - 1)
                else:
                    pe.wait_ge(mT_ready, i + 1)
                for r in range(2):
                    last = mm(bk[4 + i % 2][:, r * SEQ:(r + 1) * SEQ], BT[:, i // 4, i % 4, r, :], uT[:, i // 4, :],
                              start=True, stop=True)
                last.then_inc(bu_ps, 1)

            def y_out(m):
                pe.wait_ge(s_ready, 4 * (m + 1))
                if m >= 2:
                    pe.wait_ge(yv_ready, m - 1)
                else:
                    pe.wait_ge(mT_ready, 4)
                for r in range(2):
                    for j in range(4):
                        last = mm(bk[6 + m % 2][32 * j:32 * j + 32, 0:SEQ], CTv[:, r, m, 32 * j:32 * j + 32],
                                  s4[m % 2][:, j, r, :], start=(r == 0), stop=(r == 1))
                last.then_inc(y_ps, 1)

            def v_rows(i):
                w = chunk(V_CH + i).rearrange("p (k n) -> p k n", k=2)
                if i == 0:
                    pe.wait_ge(proj_used, V_CH)
                for k in range(2):
                    for t in range(TT):
                        for h in range(2):
                            last = mm(bk[2 * t + h][:, :], mT[:, 2 * i + k, t * P:(t + 1) * P],
                                      w[:, k, h * HALF:(h + 1) * HALF], start=(i + k == 0), stop=(i == 3 and k == 1))
                last.then_inc(chunk_used, 1)

            pe.wait_ge(proj_used, 2)
            for q in range(TILE_JOB, V_CH + 4):
                i = 2 * (q - TILE_JOB)
                if i < ST_TILES:
                    b_u(i)
                    b_u(i + 1)
                if q < V_CH:
                    proj(q, q, hT if q < K_CH else mT)
                else:
                    v_rows(q - V_CH)
                if q in (7, 9, 11, 13):
                    y_out((q - 7) // 2)

            w = chunk(GLU_CH).rearrange("p (k n) -> p k n", k=CT)
            pe.wait_ge(yg_ready, 1)
            for m in range(CT):
                for k in range(CT):
                    last = mm(bk[4 + m // 2][:, (m % 2) * SEQ:(m % 2 + 1) * SEQ], w[:, k, m * P:(m + 1) * P],
                              yg[:, k, :], start=(k == 0), stop=(k == CT - 1))
            last.then_inc(chunk_used, 1)
            pe.wait_ge(ycg_ready, 1)
            pe.wait_ge(yv_ready, 4)
            for t in range(TT):
                for k in range(CT):
                    last = mm(bk[6][:, 2 * t:2 * t + 2], sq_c[:, k, t * P:(t + 1) * P], ones2,
                              start=(k == 0), stop=(k == CT - 1))
            last.then_inc(ss_ps, 1)

            def out_proj(first_chunk, n_chunks, act, banks, bank_done, act_ready=None, bank_free=None):
                for i in range(n_chunks):
                    w = chunk(first_chunk + i).rearrange("p (k n) -> p k n", k=2)
                    if act_ready is not None:
                        pe.wait_ge(act_ready, i + 1)
                    for t in range(TT):
                        if bank_free is not None and i == 0 and t == 1:
                            pe.wait_ge(*bank_free)
                        for k in range(2):
                            for h in range(2):
                                last = mm(bk[banks[2 * t + h]][:, :], act[:, 2 * i + k, t * P:(t + 1) * P],
                                          w[:, k, h * HALF:(h + 1) * HALF], start=(i + k == 0),
                                          stop=(i == n_chunks - 1 and k == 1))
                                if i == n_chunks - 1 and k == 1 and 2 * t + h < 3:
                                    last.then_inc(bank_done, 1)
                    last.then_inc(chunk_used, 1)

            pe.wait_ge(v_evac, 4)
            out_proj(WO_CH, 2, ycT, (0, 1, 2, 3), mix_ps)
            pe.wait_ge(ysg_ready, 1)
            for t in range(TT):
                for k in range(CT):
                    last = mm(bk[6][:, 8 + 2 * t:10 + 2 * t], sq_s[:, k, t * P:(t + 1) * P], ones2,
                              start=(k == 0), stop=(k == CT - 1))
            last.then_inc(ss_ps, 1)
            out_proj(WO_CH + 2, 2, ysT, (4, 5, 6, 7), mix_ps, bank_free=(ss_sd, 1))

            transpose_tokens(x_res, (0, 1, 2, 3), x1T_ps, x1_ready, 2 * TT, True)
            for i in range(4):
                w = chunk(WQ_CH + i).rearrange("p (k n) -> p k n", k=KT)
                for m in range(2):
                    for k in range(KT):
                        if i == m == 0 and k % 2 == 0:
                            pe.wait_ge(x1T_ready, k // 2 + 1)
                        last = mm(bk[4 + i][:, m * SEQ:(m + 1) * SEQ], w[:, k, m * P:(m + 1) * P], hT[:, k, :],
                                  start=(k == 0), stop=(k == KT - 1))
                last.then_inc(chunk_used, 1)
            for h in range(HEADS):
                pe.wait_ge(qT_ready, h + 1)
                for t in range(TT):
                    for k in range(2):
                        last = mm(bk[h][:, t * SEQ:(t + 1) * SEQ], QT[:, 2 * h + k, t * P:(t + 1) * P],
                                  kT[:, 2 * h + k, :], start=(k == 0), stop=(k == 1))
                last.then_inc(sc_ps, 1)
            for h in range(HEADS):
                pe.wait_ge(p_ready, h + 1)
                for m in range(TT):
                    for t in range(TT):
                        last = tr(bk[4 + h][:, m * SEQ + t * P:m * SEQ + (t + 1) * P],
                                  PA[:, h, t, m * P:(m + 1) * P], ident[:, :])
                last.then_inc(pt_ps, 1)
            for h in range(HEADS):
                pe.wait_ge(pt_ready, h + 1)
                for d in range(2):
                    for m in range(TT):
                        last = mm(bk[h][:, d * SEQ:(d + 1) * SEQ], V[:, m, h * HD + d * P:h * HD + (d + 1) * P],
                                  PT[:, h, m, :], start=(m == 0), stop=(m == TT - 1))
                last.then_inc(o_ps, 1)
            out_proj(XO_CH, 4, OT, (4, 5, 6, 7), xo_ps, act_ready=o_ready)

            transpose_tokens(x_res, (0, 1, 2, 3), x2T_ps, x2_ready, 0, True)
            pe.wait_ge(wr_ld, 32)
            for t in range(TT):
                for k in range(KT):
                    if t == 0 and k % 2 == 0:
                        pe.wait_ge(x2T_ready, k // 2 + 1)
                    last = mm(bk[4][:, E * t:E * (t + 1)], hT[:, k, t * P:(t + 1) * P], wr[:, k, :],
                              start=(k == 0), stop=(k == KT - 1))
            last.then_inc(lg_ps, 1)
            pe.wait_ge(mask_ready, 1)
            mm(bk[5][:, 0:E], tri, mask16[:, 0, :], start=True, stop=True)
            mm(bk[5][:, E:2 * E], ones_b, mask16[:, 0, :], start=True, stop=False)
            mm(bk[5][:, E:2 * E], tri, mask16[:, 1, :], start=False, stop=True)
            mm(bk[5][:, 2 * E:3 * E], ones_b, mask16[:, 0, :], start=True, stop=False)
            mm(bk[5][:, 2 * E:3 * E], ones_b, mask16[:, 1, :], start=False, stop=True).then_inc(rank_ps, 1)
            pe.wait_ge(gates_ready, 1)
            for t in range(TT):
                last = tr(bk[6][0:E, t * P:(t + 1) * P], gates[:, t, 0:E], ident[:, :])
            last.then_inc(gT_ps, 1)
            pe.wait_ge(xr3_ready, 2)

            def gather(t):
                pe.wait_ge(sel_ready, t + 1)
                for k in range(KT):
                    for tt in range(TT):
                        for s in range(3):
                            last = mm(pg_g[:, k * C:(k + 1) * C], xr3[:, tt, s, k * P:(k + 1) * P], sel[:, tt, :],
                                      start=(tt + s == 0), stop=(tt == TT - 1 and s == 2))
                last.then_inc(g_ps, 1)

            def selection_t(t):
                pe.wait_ge(hTe_ready, t + 1)
                for tt in range(TT):
                    last = tr(pg_g[:, tt * P:(tt + 1) * P], selG[:, tt].rearrange("p w c -> p (w c)"), ident[:, :])
                last.then_inc(st_ps, 1)

            def biases(t):
                pe.wait_ge(oh_ready, t + 1)
                for h in range(2):
                    for w, b in ((0, pg_glu), (1, pg_lin)):
                        mm(b[C * h:C * (h + 1), :], oh_cur, bias3[:, w * D + h * HALF:w * D + (h + 1) * HALF],
                           start=True, stop=False)

            gather(0)
            selection_t(0)
            pe.wait_ge(bias_ready, 1)
            biases(0)

            def place(t, c):
                if isinstance(t, int) and not in_ring(t, c):
                    pe.wait_ge(x_full[c], 16 * t)
                    return X[c]
                s = home(t, c)
                if isinstance(t, int):
                    pe.wait_ge(full[s], 16 * fill_count(t, c))
                else:
                    pe.wait_ge(full[s], t * 16 + 16 * (filled[s] - X_JOBS))
                return W[:, s, :]

            def job(t):
                for k in range(KT):
                    wk = place(t, k)
                    for w, b in ((0, pg_glu), (1, pg_lin)):
                        for h in range(2):
                            last = mm(b[C * h:C * (h + 1), :], hTe[:, k, :],
                                      wk[:, w * D + h * HALF:w * D + (h + 1) * HALF],
                                      start=False, stop=(k == KT - 1))
                    last.then_inc(chunk_used, 1)
                if isinstance(t, int) and t == 0:
                    pe.wait_ge(gatesT_ready, 1)
                    pe.wait_ge(bd_ld, 16)
                    for tt in range(TT):
                        for h in range(2):
                            last = mm(acc[tt][h][:, :], gatesT[:, tt * P:(tt + 1) * P],
                                      bdown[:, h * HALF:(h + 1) * HALF], start=True, stop=True)
                pe.wait_ge(st_ready, t + 1)
                gather(t + 1)
                pe.wait_ge(act_ready, t + 1)
                for c in range(4):
                    last = tr(pg_t[:, c * P:(c + 1) * P], aa[:, c * P:(c + 1) * P], ident[:, :])
                last.then_inc(actT_ps, 1)
                pe.wait_ge(actT_ready, t + 1)
                for c in range(4):
                    wk = place(t, KT + c)
                    for k in range(2):
                        for h in range(2):
                            last = mm(pg_t[C * h:C * (h + 1), :], actT[:, 2 * c + k, :],
                                      wk[:, k * D + h * HALF:k * D + (h + 1) * HALF],
                                      start=(c + k == 0), stop=(c == 3 and k == 1))
                    last.then_inc(chunk_used, 1)
                selection_t(t + 1)
                biases(t + 1)
                pe.wait_ge(y_ready, t + 1)
                for tt in range(TT):
                    for h in range(2):
                        last = mm(acc[tt][h][:, :], STz[:, h, tt * P:(tt + 1) * P], ye, start=False, stop=True,
                                  skip_group_check=True)
                    last.then_inc(scattered[tt], 1)

            for t in range(X_JOBS + 1):
                job(t)
            with pe.Fori(X_JOBS + 1, E) as t:
                job(t)
            pe.wait_ge(jobs_ready, 1)
            n_jobs = pe.value_load(n_jobs_i[0:1, :], min_val=E, max_val=E + MAX_EXTRA)
            with pe.If(n_jobs > E):
                with pe.Fori(E, n_jobs) as t:
                    job(t)

        @block.scalar
        def _(act):
            A = nc.scalar.activation
            ch = Chain(act, actc)
            for t in range(TT):
                act.dma_start(x_res[:, t, :], x[0, t * P:(t + 1) * P, :]).then_inc(x_ld[t], 16)

            def norm_stats(src, junk, ss, sd, done, ready=None):
                for t in range(TT):
                    if isinstance(ready, list):
                        act.wait_ge(ready[t], 16)
                    elif ready is not None:
                        act.wait_ge(ready[0], ready[1] + ready[2] * t)
                    ch.link(A(junk[:, t, :], src[:, t, :], ACT.Square, accum_out=ss[:, t:t + 1]))
                    A(sd[:, t:t + 1], ss[:, t:t + 1], ACT.Sqrt, bias=eps, scale=1.0 / D).then_inc(done, 1)

            def fetch(func):
                ch.link(A(spare, eps, func))

            act.wait_ge(dve_consts, 1)
            fetch(ACT.Sqrt)
            norm_stats(x_res, xn, ssx, sdx, x_sd, x_ld)
            act.wait_ge(mem_ld, 16)
            norm_stats(mem_n, mT[:, :, :].rearrange("p k t -> p (k t)").rearrange("p (t n) -> p t n", t=TT), ssm, sdm, m_sd)
            act.wait_ge(par_ld, 48)
            A(par(3)[:, 0:2], par(2)[:, 0:2], ACT.Exp).then_inc(dt_ready, 1)
            act.wait_ge(arg_ready, 1)
            A(par(8), par(4), ACT.Exp).then_inc(trig_ready, 1)
            A(par(9), par(6), ACT.Sin).then_inc(trig_ready, 1)
            A(par(10), par(5), ACT.Sin).then_inc(trig_ready, 1)

            def evac(q, dst):
                act.wait_ge(chunk_used, q + 1)
                A(dst, bk[q % 4][:, :].rearrange("p (m t) -> p m t", m=2), ACT.Copy).then_inc(proj_used, 1)

            evac(0, uT[:, 0:2, :])
            evac(1, uT[:, 2:4, :])
            Csv = Cs[:, :].rearrange("p (m t) -> p m t", m=2)
            evac(CONV_CH, Csv)
            for r, b in ((0, 7), (1, 6)):
                act.wait_ge(bct_ps, r + 1)
                A(CTv[:, r], bk[b][:, :].rearrange("p (m c) -> p m c", m=CT), ACT.Copy).then_inc(bct_ready, 1)
            act.wait_ge(consts, 3)
            for r, b in ((0, 4), (1, 5)):
                act.wait_ge(bct_ps, 3 + r)
                for j in range(4):
                    last = A(BT[32 * j:32 * j + 32, :, j, r, :],
                             bk[b][32 * j:32 * j + 32, :].rearrange("p (m s) -> p m s", m=CT), ACT.Copy)
                last.then_inc(bct_ready, 1)
            act.wait_ge(gT_ready, 1)
            for q in range(4):
                act.wait_ge(mT_ps, q + 1)
                for k in (2 * q, 2 * q + 1):
                    last = A(mT[:, k, :], bk[4 + q][:, (k % 2) * SEQ:(k % 2 + 1) * SEQ], ACT.Copy,
                             scale=gT[:, 8 + k:9 + k])
                last.then_inc(mT_ready, 1)
            act.wait_ge(proj_used, CONV_CH + 3)
            evac(CONV_CH + 3, Csv)
            act.wait_ge(proj_used, CONV_CH + 6)
            for q in range(K_CH, K_CH + 4):
                evac(q, kT[:, 2 * (q - K_CH):2 * (q - K_CH) + 2, :])
            act.wait_ge(yc_ready, 2)
            act.wait_ge(s_ready, ST_TILES)
            ch.link(A(sq_c, ycT, ACT.Square))
            for c in range(CT):
                last = A(ycT[:, c, :], ycT[:, c, :], ACT.Copy, scale=gT[:, 44 + c:45 + c])
            last.then_inc(ycg_ready, 1)
            fetch(ACT.Sigmoid)
            act.wait_ge(gelu_arg, 1)
            A(ge2, ge2, ACT.Sigmoid).then_inc(gelu_sig, 1)
            act.wait_ge(chunk_used, V_CH + 4)
            act.wait_ge(y_ps, CT)
            for t in range(TT):
                for h in range(2):
                    A(V[:, t, h * HALF:(h + 1) * HALF], bk[2 * t + h][:, :], ACT.Copy).then_inc(v_evac, 1)
            act.wait_ge(chunk_used, GLU_CH + 1)
            for i in range(2):
                A(ge[:, 2 * i:2 * i + 2, :], bk[4 + i][:, :].rearrange("p (m t) -> p m t", m=2),
                  ACT.Sigmoid).then_inc(glu_sig, 1)
            act.wait_ge(ys_ready, 1)
            ch.link(A(sq_s, ysT, ACT.Square))
            for c in range(CT):
                last = A(ysT[:, c, :], ysT[:, c, :], ACT.Copy, scale=gT[:, 48 + c:49 + c])
            last.then_inc(ysg_ready, 1)
            fetch(ACT.Sqrt)
            act.wait_ge(ss_ps, 2)
            for g in range(2):
                for t in range(TT):
                    last = A(sd_cs[:, 2 * g + t:2 * g + t + 1], bk[6][:, 8 * g + 2 * t:8 * g + 2 * t + 1], ACT.Sqrt,
                             bias=eps, scale=1.0 / D_CONV)
            last.then_inc(ss_sd, 1)
            norm_stats(x_res, xn2, ssx, sdx, x1_sd, (x1_ready, 6, 2))
            fetch(ACT.Exp)
            for h in range(HEADS):
                act.wait_ge(chunk_used, WQ_CH + h + 1)
                A(QT[:, 2 * h:2 * h + 2, :], bk[4 + h][:, :].rearrange("p (m t) -> p m t", m=2),
                  ACT.Copy).then_inc(qT_ready, 1)
            for h in range(HEADS):
                act.wait_ge(mx_ready, h + 1)
                for t in range(TT):
                    last = A(PA[:, h, t, :], bk[h][:, t * SEQ:(t + 1) * SEQ], ACT.Exp,
                             bias=nmx[:, 2 * h + t:2 * h + t + 1], scale=r16[:, t:t + 1],
                             accum_out=sm[:, 2 * h + t:2 * h + t + 1])
                last.then_inc(exp_ready, 1)
            fetch(ACT.Sqrt)
            for h in range(HEADS):
                act.wait_ge(pt_ps, h + 1)
                A(PT[:, h], bk[4 + h][:, :].rearrange("p (m t) -> p m t", m=TT), ACT.Copy).then_inc(pt_ready, 1)
            norm_stats(x_res, xn2, ssx, sdx, x2_sd, (x2_ready, 2, 2))
            fetch(ACT.Exp)
            for s in range(3):
                for t in range(TT):
                    act.wait_ge(part_sub[t], s + 1)
                    i = A(xr3[:, t, s, :], xn2[:, t, :], ACT.Copy)
                    i.then_inc(part_hi[t] if s < 2 else xr3_ready, 1)
            act.wait_ge(lmax_ready, 1)
            for t in range(TT):
                last = A(gexp[:, t, :], lg[:, t, :], ACT.Exp, bias=ngm[:, t:t + 1])
            last.then_inc(gexp_ready, 1)
            fetch(ACT.Sigmoid)

            def job(t):
                act.wait_ge(glu_min, t + 1)
                A(sg, g7, ACT.Sigmoid, scale=ALPHA).then_inc(sig_ready, 1)
                act.wait_ge(chunk_used, t * SLOTS + (N_PRE + SLOTS))
                A(ye, pg_t[:, :], ACT.Copy).then_inc(y_ready, 1)

            job(0)
            job(1)
            with act.Fori(2, E) as t:
                job(t)
            act.wait_ge(jobs_ready, 1)
            n_jobs = act.value_load(n_jobs_i[0:1, :], min_val=E, max_val=E + MAX_EXTRA)
            with act.If(n_jobs > E):
                with act.Fori(E, n_jobs) as t:
                    job(t)
            fetch(ACT.Sqrt)
            norm_stats(x_res, junk_n, ssx, sdx, fin_sd, (fin_x, 1, 1))

        @block.vector
        def _(dve):
            v = nc.vector
            TTo, TS, STT, TC = v.tensor_tensor, v.tensor_scalar, v.scalar_tensor_tensor, v.tensor_copy
            ch = Chain(dve, dvec)
            v.memset(eps, EPS)
            v.memset(ones2, 1.0)
            v.memset(BDn, 0.0)
            v.memset(vp[:, :], 0.0).then_inc(dve_consts, 1)

            def normalise(src, dst, sd, rs, sd_done, done):
                for t in range(TT):
                    dve.wait_ge(sd_done, t + 1)
                    ch.link(v.reciprocal(rs[:, t:t + 1], sd[:, t:t + 1]))
                    TS(dst[:, t, :], src[:, t, :], rs[:, t:t + 1], None, ALU.mult).then_inc(done, 1)

            def gained(dst, banks, g0, ps, ready):
                for q, b in enumerate(banks):
                    dve.wait_ge(ps, q + 1)
                    TTo(dst[:, 2 * q:2 * q + 2, :], bk[b][:, :].rearrange("p (k t) -> p k t", k=2),
                        bc_last(gT[:, g0 + 2 * q:g0 + 2 * q + 2], [P, 2, SEQ]), ALU.mult).then_inc(ready, 1)

            dve.wait_ge(dve_consts, 1)
            normalise(x_res, xn, sdx, rsx, x_sd, xn_ready)
            dve.wait_ge(rows_t, 1)
            TC(gT[:, :], bk[6][:, 0:56]).then_inc(gT_ready, 1)
            dve.wait_ge(gT_ready, 1)
            gained(hT, (0, 1, 2, 3), 0, xT_ps, xT_ready)

            dve.wait_ge(dt_ready, 1)
            dtb = bc_last(par(3)[:, 0:2], [16, 2, NST])

            def wn(ap):
                return ap.rearrange("p (w n) -> p w n", w=2)
            TTo(wn(par(4)), wn(par(0)), dtb, ALU.mult)
            ch.link(TTo(wn(par(5)), wn(par(1)), dtb, ALU.mult))
            MAGIC = 1.5 * 2.0 ** 23
            HI = 6.28125
            LO = 2 * math.pi - HI
            PI_DOWN = 3.1415925
            ch.link(TS(par(7), par(5), 1.0 / (2 * math.pi), MAGIC, ALU.mult, ALU.add))
            ch.link(TS(par(7), par(7), MAGIC, None, ALU.subtract))
            ch.link(STT(par(5), par(7), -HI, par(5), ALU.mult, ALU.add))
            ch.link(STT(par(5), par(7), -LO, par(5), ALU.mult, ALU.add))
            ch.link(TS(par(6), par(5), math.pi / 2, None, ALU.add))
            ch.link(TS(par(7), par(6), math.pi, -2 * math.pi, ALU.is_gt, ALU.mult))
            ch.link(TTo(par(6), par(6), par(7), ALU.add))
            TS(par(6), par(6), PI_DOWN, -PI_DOWN, ALU.min, ALU.max)
            TS(par(5), par(5), PI_DOWN, -PI_DOWN, ALU.min, ALU.max).then_inc(arg_ready, 1)
            TTo(par(13), par(0), par(0), ALU.mult)
            ch.link(TTo(par(14), par(1), par(1), ALU.mult))
            ch.link(TTo(par(13), par(13), par(14), ALU.add))
            dve.wait_ge(trig_ready, 3)
            TTo(par(4), par(8), par(9), ALU.mult)
            ch.link(TTo(par(7), par(8), par(10), ALU.mult))
            ch.link(TS(par(4), par(4), 1.0, None, ALU.subtract))
            TTo(par(11), par(4), par(0), ALU.mult)
            TTo(par(12), par(7), par(0), ALU.mult)
            TTo(par(5), par(7), par(1), ALU.mult)
            TTo(par(6), par(4), par(1), ALU.mult)
            ch.link(v.reciprocal(par(13), par(13)))
            TTo(par(11), par(11), par(5), ALU.add)
            ch.link(TTo(par(12), par(12), par(6), ALU.subtract))
            TTo(par(11), par(11), par(13), ALU.mult)
            TTo(par(12), par(12), par(13), ALU.mult).then_inc(par_math, 1)

            normalise(mem_n, mem_n, sdm, rsm, m_sd, mn_ready)
            dve.wait_ge(consts, 4)
            dve.wait_ge(bc_ld, 64)
            for r in range(2):
                for w in range(2):
                    last = TS(CNn[:, r, :, w, :], c_nat[:, r], sel_mask[:, 2 * r + w:2 * r + w + 1], None, ALU.mult)
            last.then_inc(cn_ready, 1)
            dve.wait_ge(par_ps, 1)
            ch.link(TC(pT, bk[6][:, 64:144].rearrange("p (q i) -> p q i", q=5)))
            mag, cos1, sin1, q_re, q_im = (pT[:, i, :] for i in range(5))
            shp = [P, ST_TILES, GCH]
            TTo(b_bar[:, 0], b_nat[:, 0], bc_last(q_re, shp), ALU.mult)
            TTo(b_tmp[:, 0], b_nat[:, 1], bc_last(q_im, shp), ALU.mult)
            TTo(b_bar[:, 1], b_nat[:, 1], bc_last(q_re, shp), ALU.mult)
            ch.link(TTo(b_tmp[:, 1], b_nat[:, 0], bc_last(q_im, shp), ALU.mult))
            for w in range(2):
                ps_ = slice(NST * w, NST * (w + 1))
                TTo(BDn[ps_, 0, :, w, :], b_bar[ps_, 0], b_tmp[ps_, 0], ALU.subtract)
                last = TTo(BDn[ps_, 1, :, w, :], b_bar[ps_, 1], b_tmp[ps_, 1], ALU.add)
            last.then_inc(bd_ready, 1)
            v.memset(sinT[:, :, 0:1], 0.0)
            ch.link(TC(sinT[:, :, 1:2], bc_last(sin1, [P, ST_TILES, 1])))
            v.memset(cosT[:, :, 0:1], 1.0)
            TC(cosT[:, :, 1:2], bc_last(cos1, [P, ST_TILES, 1])).then_inc(pT_ready, 1)
            L, lv = 1, 0
            dve.wait_ge(pT_ready, 1)
            while L < SEQ:
                if lv:
                    dve.wait_ge(tab_pool, lv)
                n = min(L, SEQ - 1 - L)
                def level(dst, x0, y0, x1, y1, op, i0, i1):
                    s3 = [P, i1 - i0, n]
                    tv = tmp_dve[:, 0:(i1 - i0) * n].rearrange("p (i t) -> p i t", t=n)
                    to = dst[:, i0:i1, L + 1:L + 1 + n]
                    TTo(to, x0[:, i0:i1, 1:1 + n], y0[:, i0:i1, L:L + 1].to_broadcast(s3), ALU.mult)
                    ch.link(TTo(tv, x1[:, i0:i1, 1:1 + n], y1[:, i0:i1, L:L + 1].to_broadcast(s3), ALU.mult))
                    ch.link(TTo(to, to, tv, op))
                for i0, i1 in (((0, 16),) if n * ST_TILES <= 1024 else ((0, 8), (8, 16))):
                    level(sinT, sinT, cosT, cosT, sinT, ALU.add, i0, i1)
                if shared(L):
                    level(cosT, cosT, cosT, sinT, sinT, ALU.subtract, 0, COS_DVE)
                dve.sem_inc(tab_dve, 1)
                L, lv = 2 * L, lv + 1
            dve.wait_ge(tab_pool, lv)

            def rotate_in(i):
                b = i % 2
                dve.wait_ge(bu_ps, i + 1)
                if i >= 2:
                    dve.wait_ge(zin_ready, i - 1)
                src = bk[4 + b][:, :].rearrange("p (r t) -> p r t", r=2)
                TTo(sA[:, b], src, cosT[:, i:i + 1, :].to_broadcast([P, 2, SEQ]), ALU.mult)
                TTo(sB[:, b], src, sinT[:, i:i + 1, :].to_broadcast([P, 2, SEQ]), ALU.mult).then_inc(ab_ready, 1)

            def scan(i):
                b = i % 2
                dve.wait_ge(zin_ready, i + 1)
                if i >= 2:
                    dve.wait_ge(s_ready, i - 1)
                for r in range(2):
                    last = v.tensor_tensor_scan(zz[:, b, r, :], mag[:, i:i + 1].to_broadcast([P, SEQ]),
                                                zin[:, b, r, :], 0.0, ALU.mult, ALU.add)
                last.then_inc(z_ready, 1)
                dve.wait_ge(z_ready, i + 1)
                TTo(Qb[:, b], zz[:, b], sinT[:, i:i + 1, :].to_broadcast([P, 2, SEQ]), ALU.mult).then_inc(q_ready, 1)

            Csv = Cs[:, :].rearrange("p (m t) -> p m t", m=2)
            vpv = vp[:, :].rearrange("p (m t) -> p m t", m=2)

            def conv_x(i):
                q = CONV_CH + 3 * i + 1
                dve.wait_ge(chunk_used, q + 1)
                dve.wait_ge(proj_used, q)
                ch.link(TTo(vpv[:, :, 2:SEQ + 2], bk[q % 4][:, :].rearrange("p (m t) -> p m t", m=2), Csv,
                            ALU.mult))
                dve.sem_inc(proj_used, 1)

            def conv_b(i):
                q = CONV_CH + 3 * i + 2
                dve.wait_ge(chunk_used, q + 1)
                for m in range(2):
                    c = 2 * i + m
                    ch.link(TS(cv[:, :], vpv[:, m, 2:SEQ + 2], gT[:, 40 + c:41 + c], None, ALU.mult))
                    ch.link(STT(cv[:, :], vpv[:, m, 1:SEQ + 1], gT[:, 36 + c:37 + c], cv[:, :], ALU.mult, ALU.add))
                    ch.link(STT(cv[:, :], vpv[:, m, 0:SEQ], gT[:, 32 + c:33 + c], cv[:, :], ALU.mult, ALU.add))
                    ch.link(TTo(ycT[:, c, :], bk[q % 4][:, m * SEQ:(m + 1) * SEQ], cv[:, :], ALU.mult))
                dve.sem_inc(proj_used, 1)
                dve.sem_inc(yc_ready, 1)

            def y_add(m):
                dve.wait_ge(y_ps, m + 1)
                STT(ysT[:, m, :], uT[:, m, :], gT[:, 52 + m:53 + m], bk[6 + m % 2][:, 0:SEQ], ALU.mult,
                    ALU.add).then_inc(yv_ready, 1)

            for i in range(ST_TILES):
                rotate_in(i)
                if i >= 1:
                    scan(i - 1)
                if i in (1, 5):
                    conv_x((i - 1) // 4)
                if i in (2, 7):
                    conv_b((i - 2) // 4)
                if i in (7, 11, 15):
                    y_add((i - 7) // 4)
            scan(ST_TILES - 1)
            y_add(3)
            dve.wait_ge(yv_ready, 4)
            dve.wait_ge(s_ready, ST_TILES)
            ch.link(TTo(ge, ysT, ysT, ALU.mult))
            ch.link(TS(ge, ge, 0.044715, 1.0, ALU.mult, ALU.add))
            GC = 2.0 * math.sqrt(2.0 / math.pi)
            STT(ge2, ge, GC, ysT, ALU.mult, ALU.mult).then_inc(gelu_arg, 1)
            dve.wait_ge(gelu_sig, 1)
            TTo(yg, ysT, ge2, ALU.mult).then_inc(yg_ready, 1)
            dve.wait_ge(yg_ready, 1)
            for i in range(2):
                dve.wait_ge(glu_sig, i + 1)
                last = TTo(ysT[:, 2 * i:2 * i + 2, :], yg[:, 2 * i:2 * i + 2, :], ge[:, 2 * i:2 * i + 2, :], ALU.mult)
            last.then_inc(ys_ready, 1)
            dve.wait_ge(ss_sd, 1)
            v.reciprocal(r_conv, sd_cs[:, 0:2])
            ch.link(v.reciprocal(r_ssm, sd_cs[:, 2:4]))
            dve.sem_inc(r_ready, 1)
            dve.wait_ge(x2_ld, 16)
            for g, r in ((0, r_conv), (1, r_ssm)):
                for t in range(TT):
                    for h in range(2):
                        b = 2 * t + h
                        dve.wait_ge(*((mix_ps, 3 * g + b + 1) if b < 3 else (chunk_used, WO_CH + 2 * (g + 1))))
                        xs = x_res[:, t, h * HALF:(h + 1) * HALF]
                        if g:
                            dve.wait_ge(x1_ready, 2 * t + h + 1)
                        STT(xs, bk[4 * g + 2 * t + h][:, :], r[:, t:t + 1], xs, ALU.mult, ALU.add).then_inc(x1_ready, 1)

            gained(hT, (0, 1, 2, 3), 16, x1T_ps, x1T_ready)
            dve.wait_ge(x1_sd, 2)
            ch.link(v.reciprocal(rsx, sdx))
            ch.link(TS(r16, rsx, HD ** -0.5, None, ALU.mult))

            def row_max(h):
                dve.wait_ge(sc_ps, h + 1)
                ch.link(v.tensor_reduce(mx[:, 2 * h:2 * h + 2], bk[h][:, :].rearrange("p (t m) -> p t m", t=TT),
                                        AX.X, ALU.max))
                STT(nmx[:, 2 * h:2 * h + 2], mx[:, 2 * h:2 * h + 2], -1.0, r16, ALU.mult, ALU.mult).then_inc(mx_ready, 1)

            def probabilities(h):
                dve.wait_ge(exp_ready, h + 1)
                ch.link(v.reciprocal(rsum[:, 2 * h:2 * h + 2], sm[:, 2 * h:2 * h + 2]))
                for t in range(TT):
                    last = TS(PA[:, h, t, :], PA[:, h, t, :], rsum[:, 2 * h + t:2 * h + t + 1], None, ALU.mult)
                last.then_inc(p_ready, 1)

            for h in range(HEADS):
                row_max(h)
                if h >= 1:
                    probabilities(h - 1)
            probabilities(HEADS - 1)
            for h in range(HEADS):
                dve.wait_ge(o_ps, h + 1)
                TC(OT[:, 2 * h:2 * h + 2, :], bk[h][:, :].rearrange("p (d t) -> p d t", d=2)).then_inc(o_ready, 1)
            for t in range(TT):
                for h in range(2):
                    b = 2 * t + h
                    dve.wait_ge(*((xo_ps, b + 1) if b < 3 else (chunk_used, XO_CH + 4)))
                    xs = x_res[:, t, h * HALF:(h + 1) * HALF]
                    TTo(xs, xs, bk[4 + 2 * t + h][:, :], ALU.add).then_inc(x2_ready, 1)
            gained(hT, (0, 1, 2, 3), 24, x2T_ps, x2T_ready)
            dve.wait_ge(x2_sd, 2)
            ch.link(v.reciprocal(rsx, sdx))
            for t in range(TT):
                TS(xn2[:, t, :], x_res[:, t, :], rsx[:, t:t + 1], None, ALU.mult).then_inc(part_sub[t], 1)
            for s in range(2):
                dve.wait_ge(part_hi[0], s + 1)
                TTo(xn2[:, 0, :], xn2[:, 0, :], xr3[:, 0, s, :], ALU.subtract).then_inc(part_sub[0], 1)

            dve.wait_ge(consts, 5)
            v.memset(gates, 0.0)
            v.memset(rankm, 0.0)
            v.memset(STz, 0.0)
            dve.wait_ge(wr_ld, 32)
            dve.wait_ge(lg_ps, 1)
            for t in range(TT):
                last = STT(lg[:, t, :], bk[4][:, E * t:E * (t + 1)], rsx[:, t:t + 1], br, ALU.mult, ALU.add)
            ch.link(last)
            for t in range(TT):
                last = v.max(top8[:, t, :], lg[:, t, :])
            ch.link(last)
            TS(ngm, top8[:, :, 0:1].rearrange("p t o -> p (t o)"), -1.0, None, ALU.mult).then_inc(lmax_ready, 1)
            fourth = top8[:, :, TOPK - 1:TOPK].to_broadcast([P, TT, E])
            TTo(gt, lg, fourth, ALU.is_gt)
            ch.link(TTo(eq, lg, fourth, ALU.is_equal))
            for t in range(TT):
                v.tensor_tensor_scan(cum[:, t, :], ones96[:, 0:E], eq[:, t, :], 0.0, ALU.mult, ALU.add)
            ch.link(v.tensor_reduce(need, gt, AX.X, ALU.add))
            ch.link(TS(need, need, -1.0, float(TOPK), ALU.mult, ALU.add))
            for t in range(TT):
                last = STT(cum[:, t, :], cum[:, t, :], need[:, t:t + 1], eq[:, t, :], ALU.is_le, ALU.mult)
            ch.link(last)
            ch.link(TTo(maskf, gt, cum, ALU.add))
            TC(mask16, maskf).then_inc(mask_ready, 1)
            dve.wait_ge(gexp_ready, 1)
            ch.link(TTo(gexp, gexp, maskf, ALU.mult))
            ch.link(v.tensor_reduce(gsum, gexp, AX.X, ALU.add))
            ch.link(v.reciprocal(grec, gsum))
            for t in range(TT):
                last = TS(gates[:, t, 0:E], gexp[:, t, :], grec[:, t:t + 1], None, ALU.mult)
            last.then_inc(gates_ready, 1)
            dve.wait_ge(rank_ps, 1)
            ch.link(STT(rankm[:, :, 0:E], bk[5][:, 0:2 * E].rearrange("p (t e) -> p t e", t=TT), 1.0, maskf,
                        ALU.add, ALU.mult))
            def select(t, e):
                for tt in range(TT):
                    last = TS(sel[:, tt, :], iota_c, job_b[:, bass.ds(t, 1)], rankm[:, tt, bass.ds(e, 1)],
                              ALU.add, ALU.is_equal)
                return last

            def select_gated(e):
                for tt in range(TT):
                    last = TS(selG[:, tt], sel[:, tt:tt + 1, :].to_broadcast([P, 2, C]), gates[:, tt, bass.ds(e, 1)],
                              None, ALU.mult)
                return last

            def gathered(t):
                dve.wait_ge(g_ps, t + 1)
                TTo(hTe, pg_g[:, :].rearrange("p (k c) -> p k c", k=KT), bc_last(gT[:, 24:32], [P, KT, C]),
                    ALU.mult).then_inc(hTe_ready, 1)

            def back(t):
                dve.wait_ge(st_ps, t + 1)
                for w in range(2):
                    last = TC(STz[C * w:C * (w + 1), w, :], pg_g[C * w:C * (w + 1), 0:SEQ])
                last.then_inc(st_ready, 1)

            TC(oh_cur, onehot[:, 0:1].to_broadcast([96, C])).then_inc(oh_ready, 1)
            select(0, 0).then_inc(sel_ready, 1)
            dve.wait_ge(sel_ready, 1)
            ch.link(select_gated(0))
            dve.wait_ge(gT_ps, 1)
            TC(gatesT, bk[6][0:E, 0:SEQ]).then_inc(gatesT_ready, 1)
            ch.link(TC(cnt, bk[5][:, 2 * E:3 * E]))
            gathered(0)
            back(0)
            ch.link(TC(job_ei[:, 0:E], job_e[:, 0:E]))
            for c in range(PASSES):
                last = TS(flag[:, c * E:(c + 1) * E], cnt, float(C * (c + 1)), None, ALU.is_gt)
            ch.link(last)
            ch.link(v.tensor_tensor_scan(incl, ones96, flag, 0.0, ALU.mult, ALU.add))
            ch.link(TTo(pos, incl, flag, ALU.subtract))
            jf = [P, 8, 96]
            for j in (0, 8):
                ch.link(TTo(eqj, pos.unsqueeze(1).to_broadcast(jf), bc_last(iota_j[:, j:j + 8], jf), ALU.is_equal))
                ch.link(TTo(eqj, eqj, flag.unsqueeze(1).to_broadcast(jf), ALU.mult))
                ch.link(TTo(eqi, eqj, id_b.unsqueeze(1).to_broadcast(jf), ALU.mult))
                ch.link(v.tensor_reduce(job_b[:, E + j:E + j + 8], eqi, AX.X, ALU.add))
                ch.link(TTo(eqi, eqj, id_e.unsqueeze(1).to_broadcast(jf), ALU.mult))
                ch.link(v.tensor_reduce(job_e[:, E + j:E + j + 8], eqi, AX.X, ALU.add))
            TS(n_jobs_i, incl[:, 95:96], float(E), None, ALU.add)
            ch.link(TS(job_ei[:, E:E + 16], job_e[:, E:E + 16], float(E), None, ALU.add))
            dve.sem_inc(jobs_ready, 1)
            dve.wait_ge(jobs_ready, 1)

            lp = Chain(dve, dvel)

            def job(t):
                lp.count = t * DVE_LOOP_LINKS
                e = dve.value_load(job_ei[0:1, bass.ds(t + 1, 1)], min_val=0, max_val=E)
                dve.wait_ge(st_ps, t + 1)
                select(t + 1, e).then_inc(sel_ready, 1)
                dve.wait_ge(sel_ready, t + 2)
                lp.link(select_gated(e))
                dve.wait_ge(chunk_used, t * SLOTS + (N_PRE + KT))
                TS(g7, pg_glu[:, :], LIMIT, None, ALU.min).then_inc(glu_min, 1)
                lp.link(TS(l7, pg_lin[:, :], LIMIT, -LIMIT, ALU.min, ALU.max))
                dve.wait_ge(glu_min, t + 1)
                lp.link(STT(l7, l7, 1.0, g7, ALU.add, ALU.mult))
                dve.wait_ge(sig_ready, t + 1)
                TTo(aa, l7, sg, ALU.mult).then_inc(act_ready, 1)
                TC(oh_cur, onehot[:, bass.ds(e, 1)].to_broadcast([96, C])).then_inc(oh_ready, 1)
                dve.wait_ge(actT_ps, t + 1)
                TC(actT.rearrange("p (w c) s -> p c w s", w=2),
                   pg_t[:, :].rearrange("p (c w s) -> p c w s", c=4, w=2)).then_inc(actT_ready, 1)
                gathered(t + 1)
                dve.wait_ge(scattered[TT - 1], t + 1)
                back(t + 1)
                return lp.count

            job(0)
            job(1)
            with dve.Fori(2, E) as t:
                job(t)
            n_jobs = dve.value_load(n_jobs_i[0:1, :], min_val=E, max_val=E + MAX_EXTRA)
            with dve.If(n_jobs > E):
                with dve.Fori(E, n_jobs) as t:
                    job(t)
            for t in range(TT):
                dve.wait_ge(scattered[t], n_jobs)
                for h in range(2):
                    xs = x_res[:, t, h * HALF:(h + 1) * HALF]
                    last = TTo(xs, xs, acc[t][h][:, :], ALU.add)
                last.then_inc(fin_x, 1)
            dve.wait_ge(gf_ld, 16)
            for t in range(TT):
                dve.wait_ge(fin_sd, t + 1)
                ch.link(v.reciprocal(rsx[:, t:t + 1], sdx[:, t:t + 1]))
                STT(out_n[:, t, :], x_res[:, t, :], rsx[:, t:t + 1], gfin, ALU.mult, ALU.mult).then_inc(fin_ready, 1)

        @block.gpsimd
        def _(pool):
            g = nc.gpsimd
            ch = Chain(pool, poolc)
            ch.link(g.memset(ident[:, :], 0.0))
            pool.sem_inc(consts, 1)
            g.affine_select(out=ident[:, :], in_=ident[:, :], compare_op=ALU.not_equal, fill=1.0, base=0,
                            pattern=[[-1, P]], channel_multiplier=1).then_inc(consts, 1)
            pool.wait_ge(x_ld[1], 16)
            for r, src in ((0, ssm_b_re), (1, ssm_b_im)):
                pool.dma_start(b_nat[:, r], src[0].rearrange("(i w) n c -> (w n) i c", w=2)).then_inc(bc_ld, 16)
            for r, src in ((0, ssm_c_re), (1, ssm_c_im)):
                pool.dma_start(c_nat[:, r], src[0].rearrange("(m g) c n -> (g c) m n", m=CT)).then_inc(bc_ld, 16)
            g.memset(BT, 0.0).then_inc(consts, 1)
            mrow = tmp_pool[:, 0:32].rearrange("p (a b) -> p a b", a=4)
            ch.link(g.memset(tmp_pool[:, 0:64], 0.0))
            for w in range(2):
                for a in range(4):
                    lo = 32 * a + 16 * w
                    col = tmp_pool[:, 8 * w + a:8 * w + a + 1]
                    ch.link(g.affine_select(out=col, in_=tmp_pool[:, 32:33], compare_op=ALU.is_gt, fill=1.0,
                                            base=lo, pattern=[[0, 1]], channel_multiplier=-1))
                    ch.link(g.affine_select(out=col, in_=col, compare_op=ALU.is_gt, fill=0.0,
                                            base=lo + 16, pattern=[[0, 1]], channel_multiplier=-1))
            for w in range(2):
                for a in range(4):
                    col = tmp_pool[:, 8 * w + a:8 * w + a + 1]
                    if a == 0:
                        ch.link(g.tensor_copy(sel_mask[:, w:w + 1], col))
                    else:
                        ch.link(g.tensor_tensor(sel_mask[:, w:w + 1], sel_mask[:, w:w + 1], col, ALU.add))
            ch.link(g.tensor_scalar(sel_mask[:, 2:4], sel_mask[:, 0:2], -1.0, None, ALU.mult))
            pool.sem_inc(consts, 1)
            L, lv = 1, 0
            pool.wait_ge(pT_ready, 1)
            while L < SEQ:
                if lv:
                    pool.wait_ge(tab_dve, lv)
                n = min(L, SEQ - 1 - L)
                first = COS_DVE if shared(L) else 0
                for i0, i1 in (((first, 16),) if n * ST_TILES <= 1024 else ((first, 10), (10, 16))):
                    s3 = [P, i1 - i0, n]
                    tv = tmp_pool[:, 0:(i1 - i0) * n].rearrange("p (i t) -> p i t", t=n)
                    dst = cosT[:, i0:i1, L + 1:L + 1 + n]
                    g.tensor_tensor(dst, cosT[:, i0:i1, 1:1 + n], cosT[:, i0:i1, L:L + 1].to_broadcast(s3), ALU.mult)
                    ch.link(g.tensor_tensor(tv, sinT[:, i0:i1, 1:1 + n], sinT[:, i0:i1, L:L + 1].to_broadcast(s3),
                                            ALU.mult))
                    ch.link(g.tensor_tensor(dst, dst, tv, ALU.subtract))
                pool.sem_inc(tab_pool, 1)
                L, lv = 2 * L, lv + 1
            pool.wait_ge(tab_dve, lv)

            def rotate_sum(i):
                b = i % 2
                pool.wait_ge(ab_ready, i + 1)
                if i >= 2:
                    pool.wait_ge(z_ready, i - 1)
                g.tensor_tensor(zin[:, b, 0, :], sA[:, b, 0, :], sB[:, b, 1, :], ALU.add)
                g.tensor_tensor(zin[:, b, 1, :], sA[:, b, 1, :], sB[:, b, 0, :], ALU.subtract).then_inc(zin_ready, 1)

            def states(i):
                b = i % 2
                pool.wait_ge(z_ready, i + 1)
                ch.link(g.tensor_tensor(Pb, zz[:, b], cosT[:, i:i + 1, :].to_broadcast([P, 2, SEQ]), ALU.mult))
                pool.wait_ge(q_ready, i + 1)
                m = i // 4
                if m >= 2:
                    pool.wait_ge(y_ps, m - 1)
                elif m == 1:
                    pool.wait_ge(mT_ps, 4)
                else:
                    pool.wait_ge(xn_ready, 2)
                g.tensor_tensor(s4[m % 2][:, i % 4, 0, :], Pb[:, 0, :], Qb[:, b, 1, :], ALU.subtract)
                g.tensor_tensor(s4[m % 2][:, i % 4, 1, :], Pb[:, 1, :], Qb[:, b, 0, :], ALU.add).then_inc(s_ready, 1)
                pool.wait_ge(s_ready, i + 1)

            for i in range(ST_TILES):
                rotate_sum(i)
                if i >= 1:
                    states(i - 1)
            states(ST_TILES - 1)
            pool.wait_ge(y_ps, 4)
            pool.dma_start(x_res, x[0].rearrange("(t p) n -> p t n", p=P)).then_inc(x2_ld, 16)
            pool.wait_ge(bu_ps, ST_TILES)
            for s in range(3):
                pool.dma_start(bg_raw[E * s:E * (s + 1), :], b_gu[0]).then_inc(bg_ld, 16)
            pool.wait_ge(chunk_used, V_CH + 4)
            pool.dma_start(bdown, b_down[0]).then_inc(bd_ld, 16)
            pool.wait_ge(bg_ld, 48)
            ch.link(g.tensor_copy(bias3, bg_raw))
            for s in (1, 2):
                for q in range(s, 3):
                    rows_q = slice(E * q, E * (q + 1))
                    ch.link(g.tensor_tensor(bg_raw[rows_q, :], bg_raw[rows_q, :], bias3[rows_q, :], ALU.subtract))
                    ch.link(g.tensor_copy(bias3[rows_q, :], bg_raw[rows_q, :]))
            pool.sem_inc(bias_ready, 1)
            pool.wait_ge(yc_ready, 2)
            pool.dma_start(wr, w_router[0].rearrange("(k p) e -> p k e", p=P)).then_inc(wr_ld, 16)
            pool.dma_start(br, b_router[0].partition_broadcast(P)).then_inc(wr_ld, 16)
            pool.dma_start(gfin, norm_final.partition_broadcast(P)).then_inc(gf_ld, 16)
            pool.wait_ge(sc_ps, HEADS)
            g.memset(tri, 1.0)
            g.memset(ones_b, 1.0)
            g.memset(ones96, 1.0)
            g.memset(job_b, 0.0)
            ch.link(g.memset(onehot, 0.0))
            g.affine_select(out=tri, in_=tri, compare_op=ALU.is_gt, fill=0.0, base=0, pattern=[[1, P]],
                            channel_multiplier=-1)
            for s in range(3):
                ch.link(g.affine_select(out=onehot[:, 0:E], in_=onehot[:, 0:E], compare_op=ALU.not_equal, fill=1.0,
                                        base=-E * s, pattern=[[-1, E]], channel_multiplier=1))
            g.iota(iota_c, [[1, C]], base=1, channel_multiplier=0, allow_small_or_imprecise_dtypes=True)
            g.iota(iota_j, [[1, 16]], base=0, channel_multiplier=0, allow_small_or_imprecise_dtypes=True)
            g.iota(job_e, [[1, JT]], base=0, channel_multiplier=0, allow_small_or_imprecise_dtypes=True)
            g.iota(id_e, [[0, PASSES], [1, E]], base=-E, channel_multiplier=0, allow_small_or_imprecise_dtypes=True)
            ch.link(g.iota(id_b, [[C, PASSES], [0, E]], base=C, channel_multiplier=0,
                           allow_small_or_imprecise_dtypes=True))
            pool.sem_inc(consts, 1)
            for s in range(2):
                pool.wait_ge(part_hi[1], s + 1)
                g.tensor_tensor(xn2[:, 1, :], xn2[:, 1, :], xr3[:, 1, s, :], ALU.subtract).then_inc(part_sub[1], 1)


_INS = ["x", "mem", "norm_mix", "w_in", "conv_w", "ssm_a_re", "ssm_a_im", "ssm_log_dt", "ssm_b_re", "ssm_b_im",
        "ssm_c_re", "ssm_c_im", "ssm_d", "w_glu", "norm_conv_out", "norm_ssm_out", "w_out", "norm_xattn", "norm_mem",
        "w_q", "w_kv", "w_o", "norm_moe", "w_router", "b_router", "w_gu", "b_gu", "w_down", "b_down", "norm_final"]


def kernel(**inputs):
    import numpy as _np
    import concourse.bacc as _bacc
    from concourse import mybir as _mybir
    from concourse.bass_utils import run_bass_kernel_spmd as _run

    nc = _bacc.Bacc("TRN2", target_bir_lowering=False, num_devices=1)
    arrays, args = {}, []
    for name in _INS:
        a = _np.ascontiguousarray(inputs[name])
        arrays[f"in_{name}"] = a
        args.append(nc.dram_tensor(f"in_{name}", a.shape, _mybir.dt.from_np(a.dtype), kind="ExternalInput").ap())
    out = nc.dram_tensor("out_0", (1, SEQ, D), F32, kind="ExternalOutput").ap()
    hybrid_layer(nc, *args, out)
    r = _run(nc, [arrays], core_ids=[0])
    return r.results[0]["out_0"]
```

```python
import math
from contextlib import ExitStack

import concourse.bass as bass
from concourse import mybir

F32 = mybir.dt.float32
BF16 = mybir.dt.bfloat16
I32 = mybir.dt.int32
ALU = mybir.AluOpType
ACT = mybir.ActivationFunctionType
AX = mybir.AxisListType

P = 128
D = 1024
SEQ = 256
TT = SEQ // P
KT = D // P
HALF = 512
D_CONV = 512
CT = D_CONV // P
GROUPS, GCH, NST = 32, 16, 64
ST_TILES = GROUPS * NST // P
HEADS, HD = 4, 256
E = 32
C = 64
TOPK = 4
LIMIT, ALPHA = 7.0, 1.702
EPS = 1e-5
MAX_EXTRA = SEQ * TOPK // (C + 1)
PASSES = SEQ // C - 1
JT = E + MAX_EXTRA + 1

PRE_SLOTS = 9
SLOTS = 12
CONV_CH, K_CH, V_CH, GLU_CH, WO_CH, WQ_CH, XO_CH = 2, 8, 12, 16, 17, 21, 25
N_PRE = 29
FIFO_JOBS = 5
TILE_JOB = 5
DVE_LOOP_LINKS = 5
DOWN_ORDER = (0, 2, 1, 3)


class Chain:

    def __init__(self, engine, sem):
        self.engine, self.sem, self.count = engine, sem, 0

    def link(self, instruction):
        instruction.then_inc(self.sem, 1)
        self.count = self.count + 1
        self.engine.wait_ge(self.sem, self.count)


def hybrid_layer(nc, x, mem, norm_mix, w_in, conv_w, ssm_a_re, ssm_a_im, ssm_log_dt, ssm_b_re, ssm_b_im,
                 ssm_c_re, ssm_c_im, ssm_d, w_glu, norm_conv_out, norm_ssm_out, w_out, norm_xattn, norm_mem,
                 w_q, w_kv, w_o, norm_moe, w_router, b_router, w_gu, b_gu, w_down, b_down, norm_final, out):
    ctx = ExitStack()
    with ctx:
        def sb(name, cols, dt=F32, parts=P):
            return ctx.enter_context(nc.sbuf_tensor(name, [parts, cols], dt))

        def sem(name):
            return ctx.enter_context(nc.semaphore(name))

        W = ctx.enter_context(nc.sbuf_tensor("W", [P, SLOTS, 2 * D], F32))
        R1 = sb("R1", 12288)
        XR = sb("XR", TT * D)
        HT = sb("HT", KT * SEQ)
        MT = sb("MT", KT * SEQ)
        KR = sb("KR", KT * SEQ)
        VR = sb("VR", KT * SEQ)
        R3 = sb("R3", 3 * CT * SEQ)
        CTm = sb("CTm", 2 * CT * P)
        ident = sb("ident", P)
        small = sb("small", 256)
        gT = sb("gT", 56)
        Cs = sb("Cs", 2 * SEQ)
        vp = sb("vp", 2 * (SEQ + 2))
        cv = sb("cv", SEQ)
        SCR = W[:, PRE_SLOTS:SLOTS, :].rearrange("p s n -> p (s n)")

        x_res = XR[:, :].rearrange("p (t n) -> p t n", t=TT)
        hT = HT[:, :].rearrange("p (k t) -> p k t", k=KT)
        mT = MT[:, :].rearrange("p (k t) -> p k t", k=KT)
        xn = KR[:, :].rearrange("p (t n) -> p t n", t=TT)
        mem_n = VR[:, :].rearrange("p (t n) -> p t n", t=TT)
        kT = KR[:, :].rearrange("p (k t) -> p k t", k=KT)
        V = VR[:, :].rearrange("p (t n) -> p t n", t=TT)
        uT = R3[:, 0:1024].rearrange("p (c t) -> p c t", c=CT)
        ycT = R3[:, 1024:2048].rearrange("p (c t) -> p c t", c=CT)
        ysT = R3[:, 2048:3072].rearrange("p (c t) -> p c t", c=CT)
        tmp_dve = R3[:, 1024:2048]
        tmp_pool = R3[:, 2048:3072]
        cosT = R1[:, 0:4096].rearrange("p (i t) -> p i t", i=ST_TILES)
        sinT = R1[:, 4096:8192].rearrange("p (i t) -> p i t", i=ST_TILES)
        BT = R1[:, 8192:12288].rearrange("p (m j r s) -> p m j r s", m=CT, j=4, r=2)
        CTv = CTm[:, :].rearrange("p (r m c) -> p r m c", r=2, m=CT)

        ssx, sdx, rsx = small[:, 0:2], small[:, 2:4], small[:, 4:6]
        ssm, sdm, rsm = small[:, 6:8], small[:, 8:10], small[:, 10:12]
        eps = small[:, 12:13]
        spare = small[:, 13:14]
        r16 = small[:, 28:30]
        ones2 = small[:, 14:16]
        sel_mask = small[:, 16:20]
        r_conv, r_ssm, sd_cs = small[:, 20:22], small[:, 22:24], small[:, 24:28]
        mx, nmx, sm, rsum = small[:, 32:40], small[:, 40:48], small[:, 48:56], small[:, 56:64]
        pT = small[:, 64:144].rearrange("p (q i) -> p q i", q=5)

        BDn = SCR[:, 0:1024].rearrange("p (r i w c) -> p r i w c", r=2, i=ST_TILES, w=2)
        CNn = SCR[:, 1024:2048].rearrange("p (r m w n) -> p r m w n", r=2, m=CT, w=2)
        b_nat = SCR[:, 2048:2560].rearrange("p (r i c) -> p r i c", r=2, i=ST_TILES)
        b_bar = SCR[:, 2560:3072].rearrange("p (r i c) -> p r i c", r=2, i=ST_TILES)
        b_tmp = SCR[:, 3072:3584].rearrange("p (r i c) -> p r i c", r=2, i=ST_TILES)
        c_nat = SCR[:, 3584:4096].rearrange("p (r m n) -> p r m n", r=2, m=CT)
        rows = SCR[0:56, 4096:4224]
        PR = SCR[0:16, 4224:6144]

        def par(i):
            return PR[:, P * i:P * (i + 1)]

        sA = SCR[:, 0:1024].rearrange("p (b r t) -> p b r t", b=2, r=2)
        sB = SCR[:, 1024:2048].rearrange("p (b r t) -> p b r t", b=2, r=2)
        zin = SCR[:, 2048:3072].rearrange("p (b r t) -> p b r t", b=2, r=2)
        zz = SCR[:, 3072:4096].rearrange("p (b r t) -> p b r t", b=2, r=2)
        Qb = SCR[:, 4096:5120].rearrange("p (b r t) -> p b r t", b=2, r=2)
        Pb = SCR[:, 5120:5632].rearrange("p (r t) -> p r t", r=2)
        s4 = [R[:, :].rearrange("p (j r t) -> p j r t", j=4, r=2) for R in (XR, VR)]
        ge = SCR[:, 0:1024].rearrange("p (c t) -> p c t", c=CT)
        ge2 = SCR[:, 1024:2048].rearrange("p (c t) -> p c t", c=CT)
        yg = SCR[:, 2048:3072].rearrange("p (c t) -> p c t", c=CT)
        sq_s = SCR[:, 3072:4096].rearrange("p (c t) -> p c t", c=CT)
        sq_c = SCR[:, 4096:5120].rearrange("p (c t) -> p c t", c=CT)

        QT = R1[:, 0:2048].rearrange("p (k t) -> p k t", k=KT)
        PA = R1[:, 2048:4096].rearrange("p (h t m) -> p h t m", h=HEADS, t=TT)
        PT = R1[:, 4096:6144].rearrange("p (h m t) -> p h m t", h=HEADS, m=TT)
        OT = R1[:, 6144:8192].rearrange("p (k t) -> p k t", k=KT)
        xn2 = R1[:, 8192:10240].rearrange("p (t n) -> p t n", t=TT)

        bg_raw = R1[0:96, 10240:12288]
        bias3 = MT[0:96, 0:1024].bitcast(BF16)
        bdown = MT[0:E, 1024:2048]

        xr3 = R3[:, :].bitcast(BF16).rearrange("p (t s n) -> p t s n", t=TT, s=3)
        wr = Cs[:, 0:256].rearrange("p (k e) -> p k e", k=KT)
        br = Cs[:, 256:288]
        gfin = CTm[:, :]
        out_n = W[:, 4:4 + TT, 0:D]
        junk_n = W[:, 0:TT, 0:D]
        place_of = [W[:, s, :] for s in range(SLOTS)]
        place_of += [R1[:, c:c + 2 * D] for c in (10240, 2048, 4096, 6144)]
        place_of += [HT[:, :], R1[:, 8192:10240]]
        place_of += [XR[:, :], KR[:, :], VR[:, :]]
        IN_BIAS, IN_P, IN_PT, IN_OT, IN_HT, IN_XN, IN_RES, IN_K, IN_V = range(SLOTS, SLOTS + 9)
        EB = R1[:, 0:2048]
        lg = EB[:, 0:64].rearrange("p (t e) -> p t e", t=TT)
        top8 = EB[:, 64:80].rearrange("p (t e) -> p t e", t=TT)
        gt = EB[:, 80:144].rearrange("p (t e) -> p t e", t=TT)
        eq = EB[:, 144:208].rearrange("p (t e) -> p t e", t=TT)
        cum = EB[:, 208:272].rearrange("p (t e) -> p t e", t=TT)
        need = EB[:, 272:274]
        maskf = EB[:, 288:352].rearrange("p (t e) -> p t e", t=TT)
        mask16 = EB[:, 352:384].bitcast(BF16).rearrange("p (t e) -> p t e", t=TT)
        gates = EB[:, 384:450].rearrange("p (t e) -> p t e", t=TT)
        rankm = EB[:, 450:516].rearrange("p (t e) -> p t e", t=TT)
        gexp = EB[:, 516:580].rearrange("p (t e) -> p t e", t=TT)
        gsum, grec, ngm = EB[:, 580:582], EB[:, 582:584], EB[:, 584:586]
        cnt = EB[:, 586:618]
        flag = EB[:, 618:714]
        incl = EB[:, 714:810]
        pos = EB[:, 810:906]
        id_e = EB[:, 906:1002]
        id_b = EB[:, 1002:1098]
        iota_j = EB[:, 1098:1114]
        iota_c = EB[:, 1114:1178]
        job_e = EB[:, 1178:1178 + JT]
        job_b = EB[:, 1242:1242 + JT]
        job_ei = EB[:, 1306:1306 + JT].bitcast(I32)
        n_jobs_i = EB[:, 1370:1371].bitcast(I32)
        ones96 = EB[:, 1376:1472]
        tri = EB[:, 1472:1536].bitcast(BF16)
        ones_b = EB[:, 1536:1600].bitcast(BF16)
        onehot = EB[0:96, 1600:1664].bitcast(BF16)[:, 0:E + 1]
        oh_cur = EB[0:96, 1664:1696].bitcast(BF16)
        sel = EB[:, 1696:1760].bitcast(BF16).rearrange("p (t c) -> p t c", t=TT)
        selG = EB[:, 1760:2016].rearrange("p (t w c) -> p t w c", t=TT, w=2)
        eqj = KR[:, 0:768].rearrange("p (j f) -> p j f", j=8)
        eqi = KR[:, 768:1536].rearrange("p (j f) -> p j f", j=8)
        gatesT = cv[0:E, :]

        g7 = KR[:, 0:512]
        sg = KR[:, 512:1024]
        l7 = KR[:, 1024:1536]
        aa = KR[:, 1536:2048]
        actT = VR[:, 0:512].rearrange("p (k c) -> p k c", k=KT)
        ye = VR[:, 512:1024]
        hTe = Cs[:, :].rearrange("p (k c) -> p k c", k=KT)
        STz = vp[:, 0:2 * SEQ].rearrange("p (w t) -> p w t", w=2)

        bk = [ctx.enter_context(nc.psum_tensor(f"bank{i}", [P, HALF], F32)) for i in range(8)]
        acc = [[bk[2 * t + h] for h in range(2)] for t in range(TT)]
        pg_glu, pg_lin, pg_t, pg_g = bk[4], bk[5], bk[6], bk[7]
        pg_tr = (pg_glu, pg_lin)

        full = [sem(f"slot{i}_full") for i in range(SLOTS)]
        full += [sem(f"further_place{i}_full") for i in range(9)]
        chunk_used = sem("chunk_used")
        x_ld = [sem(f"x_tile{t}_ld") for t in range(TT)]
        mem_ld, rows_ld, par_ld, bc_ld = sem("mem_ld"), sem("rows_ld"), sem("par_ld"), sem("bc_ld")
        x2_ld, bg_ld, bd_ld, wr_ld, gf_ld = sem("x2_ld"), sem("bg_ld"), sem("bd_ld"), sem("wr_ld"), sem("gf_ld")
        consts, dve_consts, dvec = sem("consts"), sem("dve_consts"), sem("dve_step")
        actc, poolc = sem("act_step"), sem("pool_step")
        dvel = sem("dve_loop_step")
        x_sd, m_sd, xn_ready, mn_ready = sem("x_sd"), sem("m_sd"), sem("xn_ready"), sem("mn_ready")
        rows_t, gT_ready, xT_ps = sem("rows_t"), sem("gT_ready"), sem("xT_ps")
        xT_ready, mT_ps, mT_ready = sem("xT_ready"), sem("mT_ps"), sem("mT_ready")
        dt_ready, arg_ready, trig_ready = sem("dt_ready"), sem("arg_ready"), sem("trig_ready")
        par_math, par_ps, pT_ready = sem("par_math"), sem("par_ps"), sem("pT_ready")
        bd_ready, cn_ready, bct_ps, bct_ready = sem("bd_ready"), sem("cn_ready"), sem("bct_ps"), sem("bct_ready")
        tab_dve, tab_pool = sem("tab_dve"), sem("tab_pool")
        proj_used = sem("proj_used")
        bu_ps, ab_ready, zin_ready = sem("bu_ps"), sem("ab_ready"), sem("zin_ready")
        z_ready, q_ready, s_ready = sem("z_ready"), sem("q_ready"), sem("s_ready")
        y_ps, yv_ready, gelu_arg = sem("y_ps"), sem("yv_ready"), sem("gelu_arg")
        gelu_sig, yg_ready = sem("gelu_sig"), sem("yg_ready")
        yc_ready, ycg_ready = sem("yc_ready"), sem("ycg_ready")
        v_evac = sem("v_evac")
        glu_sig, ys_ready, ysg_ready = sem("glu_sig"), sem("ys_ready"), sem("ysg_ready")
        ss_ps, ss_sd, r_ready = sem("ss_ps"), sem("ss_sd"), sem("r_ready")
        mix_ps, x1_ready = sem("mix_ps"), sem("x1_ready")
        x1_sd, x1T_ps, x1T_ready = sem("x1_sd"), sem("x1T_ps"), sem("x1T_ready")
        qT_ready, sc_ps, mx_ready = sem("qT_ready"), sem("sc_ps"), sem("mx_ready")
        exp_ready, p_ready = sem("exp_ready"), sem("p_ready")
        pt_ps, pt_ready, o_ps = sem("pt_ps"), sem("pt_ready"), sem("o_ps")
        o_ready, xo_ps, x2_ready = sem("o_ready"), sem("xo_ps"), sem("x2_ready")
        x2_sd, x2T_ps, x2T_ready = sem("x2_sd"), sem("x2T_ps"), sem("x2T_ready")
        rx_ready, xn2_ready = sem("x2_factor_ready"), sem("xn2_ready")
        part_hi = [sem(f"part_copied_tile{t}") for t in range(TT)]
        part_sub = [sem(f"part_subtracted_tile{t}") for t in range(TT)]
        lg_ps, lmax_ready, gexp_ready = sem("lg_ps"), sem("lmax_ready"), sem("gexp_ready")
        mask_ready, rank_ps, xr3_ready = sem("mask_ready"), sem("rank_ps"), sem("xr3_ready")
        gates_ready, gT_ps, gatesT_ready = sem("gates_ready"), sem("gatesT_ps"), sem("gatesT_ready")
        bias_ready, jobs_ready = sem("bias_ready"), sem("jobs_ready")
        sel_ready, oh_ready, g_ps = sem("sel_ready"), sem("onehot_ready"), sem("gather_ps")
        hTe_ready, st_ps, st_ready = sem("hTe_ready"), sem("st_ps"), sem("st_ready")
        glu_min, sig_ready, act_ready = sem("glu_min"), sem("sig_ready"), sem("act_ready")
        actT_ps, actT_ready = sem("actT_ps"), sem("actT_ready")
        y_ready = sem("y_ready")
        scattered = [sem(f"scattered_to_bank{b}") for b in range(2 * TT)]
        x_seeded = sem("residual_seeded")
        fin_sq = sem("fin_sq")
        fin_ss, fin_sd, fin_ready, out_done = sem("fin_ss"), sem("fin_sd"), sem("fin_ready"), sem("out_done")

        block = ctx.enter_context(nc.Block())

        COS_DVE = 4

        def shared(step):
            return step >= 32

        def bc_last(ap, shape):
            return ap.unsqueeze(len(ap.shape)).to_broadcast(shape)

        def last_chunk(s):
            return max(n for n in range(N_PRE) if n % PRE_SLOTS == s)

        by_use = sorted(range(PRE_SLOTS), key=last_chunk)
        before_wo = [s for s in by_use if last_chunk(s) < XO_CH]
        after_wo = [s for s in by_use if last_chunk(s) >= XO_CH]
        scratch_slots = list(range(PRE_SLOTS, SLOTS))
        at = ([IN_K, IN_V] + scratch_slots + before_wo + [IN_BIAS, IN_P, IN_PT] + after_wo
              + [IN_OT, IN_HT, IN_XN, IN_RES])
        FIRST = len(at)
        while len(at) < FIFO_JOBS * SLOTS:
            at.append(at[len(at) - (FIRST - 2)])
        at += sorted(range(SLOTS), key=lambda s: max(n for n in range(len(at)) if at[n] == s))

        def holder_before(n):
            return max(m for m in range(n) if at[m] == at[n])

        def filling(n):
            pre = sum(1 for m in range(N_PRE) if m % PRE_SLOTS == at[n]) if at[n] < PRE_SLOTS else 0
            return pre + sum(1 for m in range(n + 1) if at[m] == at[n])

        @block.sync
        def _(sp):
            sp.dma_start(par(0), ssm_a_re[0].rearrange("(i w) n -> i (w n)", w=2)).then_inc(par_ld, 16)
            sp.dma_start(par(1), ssm_a_im[0].rearrange("(i w) n -> i (w n)", w=2)).then_inc(par_ld, 16)
            sp.dma_start(par(2)[:, 0:2], ssm_log_dt[0].rearrange("(i w) -> i w", w=2)).then_inc(par_ld, 16)
            for r0, src in ((0, norm_mix[0]), (8, norm_mem[0]), (16, norm_xattn[0]), (24, norm_moe[0]),
                            (44, norm_conv_out[0]), (48, norm_ssm_out[0]), (52, ssm_d[0])):
                n = src.shape[0] // P
                sp.dma_start(rows[r0:r0 + n, :], src.rearrange("(r c) -> r c", c=P)).then_inc(rows_ld, 16)
            sp.dma_start(rows[32:44, :], conv_w[0].rearrange("w (r c) -> (w r) c", c=P)).then_inc(rows_ld, 16)
            def slot(n):
                return W[:, n % PRE_SLOTS, :]

            def cols(w, c0):
                return w.rearrange("(k p) n -> p k n", p=P)[:, :, c0:c0 + 256], KT

            def two_rows(w, k0, c0):
                return w.rearrange("(k p) n -> p k n", p=P)[:, k0:k0 + 2, c0:c0 + D], 2

            chunks = [cols(w_in[0], 3 * D_CONV + 256 * i) for i in range(2)]
            chunks += [cols(w_in[0], base + 256 * i) for i in range(2) for base in (D_CONV, 2 * D_CONV, 0)]
            chunks += [cols(w_kv[0], 256 * i) for i in range(4)]
            chunks += [two_rows(w_kv[0], 2 * i, D) for i in range(4)]
            chunks += [(w_glu[0].rearrange("(k p) n -> p k n", p=P), CT)]
            chunks += [two_rows(w_out[0], 2 * i, 0) for i in range(4)]
            chunks += [cols(w_q[0], 256 * i) for i in range(4)]
            chunks += [two_rows(w_o[0], 2 * i, 0) for i in range(4)]
            assert len(chunks) == N_PRE
            for n, (src, k) in enumerate(chunks):
                if n == 1:
                    sp.dma_start(mem_n, mem[0].rearrange("(t p) n -> p t n", p=P)).then_inc(mem_ld, 16)
                if n == 2:
                    sp.wait_ge(bc_ld, 16 * 4)
                if n >= PRE_SLOTS:
                    sp.wait_ge(chunk_used, n - PRE_SLOTS + 1)
                sp.dma_start(slot(n).rearrange("p (k n) -> p k n", k=k), src).then_inc(full[n % PRE_SLOTS], 16)

            def expert_chunk(e, c, dst, done):
                if c < KT:
                    src = w_gu[0][bass.ds(e, 1), P * c:P * (c + 1), :].rearrange("o p n -> p (o n)")
                    sp.dma_start(dst, src).then_inc(done, 16)
                else:
                    k0 = 2 * DOWN_ORDER[c - KT]
                    src = w_down[0][bass.ds(e, 1), P * k0:P * (k0 + 2), :].rearrange("o (k p) n -> p (o k) n", p=P)
                    sp.dma_start(dst.rearrange("p (k n) -> p k n", k=2), src).then_inc(done, 16)

            def load(n):
                expert_chunk(n // SLOTS, n % SLOTS, place_of[at[n]], full[at[n]])

            free = {IN_BIAS: ((bias_ready, 1),), IN_K: ((sc_ps, HEADS),), IN_P: ((pt_ps, HEADS),),
                    IN_PT: ((o_ps, HEADS),), IN_V: ((o_ps, HEADS),), IN_OT: ((chunk_used, N_PRE),),
                    IN_HT: ((lg_ps, 1),), IN_RES: ((x_seeded, TT), (xn2_ready, 2), (part_hi[0], 1), (part_hi[1], 1)),
                    IN_XN: ((xr3_ready, 2),)}
            for s in scratch_slots:
                free[s] = ((ss_ps, 2),)
            for s in range(PRE_SLOTS):
                free[s] = ((chunk_used, last_chunk(s) + 1),)
            for s in (scratch_slots + before_wo + [IN_BIAS, IN_K, IN_P, IN_PT, IN_V] + after_wo
                      + [IN_OT, IN_HT, IN_RES, IN_XN]):
                for signal, value in free[s]:
                    sp.wait_ge(signal, value)
                load(at.index(s))
            for n in range(FIRST, len(at)):
                sp.wait_ge(chunk_used, N_PRE + holder_before(n) + 1)
                load(n)

            def later_job(t, e):
                for c in range(SLOTS):
                    sp.wait_ge(chunk_used, t * SLOTS + (N_PRE - SLOTS + c + 1))
                    s = at[FIFO_JOBS * SLOTS + c]
                    expert_chunk(e, c, place_of[s], full[s])

            with sp.Fori(FIFO_JOBS + 1, E) as t:
                later_job(t, t)
            sp.wait_ge(jobs_ready, 1)
            n_jobs = sp.value_load(n_jobs_i[0:1, :], min_val=E, max_val=E + MAX_EXTRA)
            with sp.If(n_jobs > E):
                with sp.Fori(E, n_jobs) as t:
                    later_job(t, sp.value_load(job_ei[0:1, bass.ds(t, 1)], min_val=0, max_val=E - 1))
            for t in range(TT):
                for h in range(2):
                    sp.wait_ge(fin_ready, 2 * t + h + 1)
                    sp.dma_start(out[0, t * P:(t + 1) * P, h * HALF:(h + 1) * HALF],
                                 out_n[:, t, h * HALF:(h + 1) * HALF]).then_inc(out_done, 16)
            sp.wait_ge(out_done, 16 * TT * 2)

        @block.tensor
        def _(pe):
            mm, tr = nc.tensor.matmul, nc.tensor.transpose

            def chunk(n):
                pe.wait_ge(full[n % PRE_SLOTS], 16 * (n // PRE_SLOTS + 1))
                return W[:, n % PRE_SLOTS, :]

            pe.wait_ge(consts, 2)

            def small_rows():
                pe.wait_ge(rows_ld, 16 * 8)
                tr(bk[6][:, 0:56], rows, ident[0:56, 0:56]).then_inc(rows_t, 1)

            def transpose_tokens(src, banks, done, ready, base, halves, between=None):
                for t in range(TT):
                    if t == 1 and between is not None:
                        between()
                    for q, b in enumerate(banks):
                        if halves and q % 2 == 0:
                            pe.wait_ge(ready, base + 2 * t + q // 2 + 1)
                        elif not halves and q == 0:
                            pe.wait_ge(ready, base + t + 1)
                        for k in range(2):
                            last = tr(bk[b][:, k * SEQ + t * P:k * SEQ + (t + 1) * P],
                                      src[:, t, (2 * q + k) * P:(2 * q + k + 1) * P], ident[:, :])
                        if t == TT - 1:
                            last.then_inc(done, 1)

            transpose_tokens(xn, (0, 1, 2, 3), xT_ps, xn_ready, 0, False, between=small_rows)

            def proj(q, n, act):
                w = chunk(n).rearrange("p (k n) -> p k n", k=KT)
                if q >= 4:
                    pe.wait_ge(proj_used, q - 3)
                for m in range(2):
                    for k in range(KT):
                        if q in (0, K_CH) and m == 0 and k % 2 == 0:
                            pe.wait_ge(xT_ready if q == 0 else mT_ready, k // 2 + 1)
                        last = mm(bk[q % 4][:, m * SEQ:(m + 1) * SEQ], w[:, k, m * P:(m + 1) * P],
                                  act[:, k, :], start=(k == 0), stop=(k == KT - 1))
                last.then_inc(chunk_used, 1)

            proj(0, 0, hT)
            proj(1, 1, hT)
            pe.wait_ge(par_math, 1)
            for i in range(5):
                last = tr(bk[6][:, 64 + 16 * i:80 + 16 * i], par(8 + i), ident[0:16, 0:16])
            last.then_inc(par_ps, 1)
            proj(2, 2, hT)
            pe.wait_ge(cn_ready, 1)
            for r, b in ((0, 7), (1, 6)):
                if r == 1:
                    pe.wait_ge(pT_ready, 1)
                for m in range(CT):
                    last = tr(bk[b][:, m * P:(m + 1) * P], CNn[:, r, m].rearrange("p w n -> p (w n)"), ident[:, :])
                last.then_inc(bct_ps, 1)
            pe.wait_ge(bd_ready, 1)
            for r, b in ((0, 4), (1, 5)):
                for m in range(CT):
                    last = tr(bk[b][:, m * P:(m + 1) * P],
                              BDn[:, r, 4 * m:4 * m + 4].rearrange("p i w c -> p (i w c)"), ident[:, :])
                last.then_inc(bct_ps, 1)
            proj(3, 3, hT)
            proj(4, 4, hT)
            pe.wait_ge(bct_ready, 4)
            transpose_tokens(mem_n, (4, 5, 6, 7), mT_ps, mn_ready, 0, False)

            def b_u(i):
                if i >= 2:
                    pe.wait_ge(ab_ready, i - 1)
                else:
                    pe.wait_ge(mT_ready, i + 1)
                for r in range(2):
                    last = mm(bk[4 + i % 2][:, r * SEQ:(r + 1) * SEQ], BT[:, i // 4, i % 4, r, :], uT[:, i // 4, :],
                              start=True, stop=True)
                last.then_inc(bu_ps, 1)

            def y_out(m):
                pe.wait_ge(s_ready, 4 * (m + 1))
                if m >= 2:
                    pe.wait_ge(yv_ready, m - 1)
                else:
                    pe.wait_ge(mT_ready, 4)
                for r in range(2):
                    for j in range(4):
                        last = mm(bk[6 + m % 2][32 * j:32 * j + 32, 0:SEQ], CTv[:, r, m, 32 * j:32 * j + 32],
                                  s4[m % 2][:, j, r, :], start=(r == 0), stop=(r == 1))
                last.then_inc(y_ps, 1)

            def v_rows(i):
                w = chunk(V_CH + i).rearrange("p (k n) -> p k n", k=2)
                if i == 0:
                    pe.wait_ge(proj_used, V_CH)
                for k in range(2):
                    for t in range(TT):
                        for h in range(2):
                            last = mm(bk[2 * t + h][:, :], mT[:, 2 * i + k, t * P:(t + 1) * P],
                                      w[:, k, h * HALF:(h + 1) * HALF], start=(i + k == 0), stop=(i == 3 and k == 1))
                last.then_inc(chunk_used, 1)

            pe.wait_ge(proj_used, 2)
            for q in range(TILE_JOB, V_CH + 4):
                i = 2 * (q - TILE_JOB)
                if i < ST_TILES:
                    b_u(i)
                    b_u(i + 1)
                if q < V_CH:
                    proj(q, q, hT if q < K_CH else mT)
                else:
                    v_rows(q - V_CH)
                if q in (7, 9, 11, 13):
                    y_out((q - 7) // 2)

            w = chunk(GLU_CH).rearrange("p (k n) -> p k n", k=CT)
            pe.wait_ge(yg_ready, 1)
            for m in range(CT):
                for k in range(CT):
                    last = mm(bk[4 + m // 2][:, (m % 2) * SEQ:(m % 2 + 1) * SEQ], w[:, k, m * P:(m + 1) * P],
                              yg[:, k, :], start=(k == 0), stop=(k == CT - 1))
            last.then_inc(chunk_used, 1)
            pe.wait_ge(ycg_ready, 1)
            pe.wait_ge(yv_ready, 4)
            for t in range(TT):
                for k in range(CT):
                    last = mm(bk[6][:, 2 * t:2 * t + 2], sq_c[:, k, t * P:(t + 1) * P], ones2,
                              start=(k == 0), stop=(k == CT - 1))
            last.then_inc(ss_ps, 1)

            def out_proj(first_chunk, n_chunks, act, banks, bank_done, act_ready=None, bank_free=None):
                for i in range(n_chunks):
                    w = chunk(first_chunk + i).rearrange("p (k n) -> p k n", k=2)
                    if act_ready is not None:
                        pe.wait_ge(act_ready, i + 1)
                    for t in range(TT):
                        if bank_free is not None and i == 0 and t == 1:
                            pe.wait_ge(*bank_free)
                        for k in range(2):
                            for h in range(2):
                                last = mm(bk[banks[2 * t + h]][:, :], act[:, 2 * i + k, t * P:(t + 1) * P],
                                          w[:, k, h * HALF:(h + 1) * HALF], start=(i + k == 0),
                                          stop=(i == n_chunks - 1 and k == 1))
                                if i == n_chunks - 1 and k == 1 and 2 * t + h < 3:
                                    last.then_inc(bank_done, 1)
                    last.then_inc(chunk_used, 1)

            pe.wait_ge(v_evac, 4)
            out_proj(WO_CH, 2, ycT, (0, 1, 2, 3), mix_ps)
            pe.wait_ge(ysg_ready, 1)
            for t in range(TT):
                for k in range(CT):
                    last = mm(bk[6][:, 8 + 2 * t:10 + 2 * t], sq_s[:, k, t * P:(t + 1) * P], ones2,
                              start=(k == 0), stop=(k == CT - 1))
            last.then_inc(ss_ps, 1)
            out_proj(WO_CH + 2, 2, ysT, (4, 5, 6, 7), mix_ps, bank_free=(ss_sd, 1))

            transpose_tokens(x_res, (0, 1, 2, 3), x1T_ps, x1_ready, 2 * TT, True)

            def queries(i):
                w = chunk(WQ_CH + i).rearrange("p (k n) -> p k n", k=KT)
                for m in range(2):
                    for k in range(KT):
                        if i == m == 0 and k % 2 == 0:
                            pe.wait_ge(x1T_ready, k // 2 + 1)
                        last = mm(bk[4 + i][:, m * SEQ:(m + 1) * SEQ], w[:, k, m * P:(m + 1) * P], hT[:, k, :],
                                  start=(k == 0), stop=(k == KT - 1))
                last.then_inc(chunk_used, 1)

            def scores(h):
                pe.wait_ge(qT_ready, h + 1)
                for t in range(TT):
                    for k in range(2):
                        last = mm(bk[h][:, t * SEQ:(t + 1) * SEQ], QT[:, 2 * h + k, t * P:(t + 1) * P],
                                  kT[:, 2 * h + k, :], start=(k == 0), stop=(k == 1))
                last.then_inc(sc_ps, 1)

            def probs_t(h):
                pe.wait_ge(p_ready, h + 1)
                for m in range(TT):
                    for t in range(TT):
                        last = tr(bk[4 + h][:, m * SEQ + t * P:m * SEQ + (t + 1) * P],
                                  PA[:, h, t, m * P:(m + 1) * P], ident[:, :])
                last.then_inc(pt_ps, 1)

            def attend(h):
                pe.wait_ge(pt_ready, h + 1)
                for d in range(2):
                    for m in range(TT):
                        last = mm(bk[h][:, d * SEQ:(d + 1) * SEQ], V[:, m, h * HD + d * P:h * HD + (d + 1) * P],
                                  PT[:, h, m, :], start=(m == 0), stop=(m == TT - 1))
                last.then_inc(o_ps, 1)

            queries(0)
            for h in range(1, HEADS):
                queries(h)
                scores(h - 1)
            probs_t(0)
            scores(HEADS - 1)
            for h in range(1, HEADS):
                probs_t(h)
                attend(h - 1)
            attend(HEADS - 1)
            out_proj(XO_CH, 4, OT, (4, 5, 6, 7), xo_ps, act_ready=o_ready)

            transpose_tokens(x_res, (0, 1, 2, 3), x2T_ps, x2_ready, 0, True)
            pe.wait_ge(wr_ld, 32)
            for t in range(TT):
                for k in range(KT):
                    if t == 0 and k % 2 == 0:
                        pe.wait_ge(x2T_ready, k // 2 + 1)
                    last = mm(bk[4][:, E * t:E * (t + 1)], hT[:, k, t * P:(t + 1) * P], wr[:, k, :],
                              start=(k == 0), stop=(k == KT - 1))
            last.then_inc(lg_ps, 1)

            def seed(t):
                for h in range(2):
                    last = mm(acc[t][h][:, :], ident[:, :], x_res[:, t, h * HALF:(h + 1) * HALF], start=True,
                              stop=True)
                last.then_inc(x_seeded, 1)

            seed(0)
            seed(1)
            pe.wait_ge(mask_ready, 1)
            mm(bk[5][:, 0:E], tri, mask16[:, 0, :], start=True, stop=True)
            mm(bk[5][:, E:2 * E], ones_b, mask16[:, 0, :], start=True, stop=False)
            mm(bk[5][:, E:2 * E], tri, mask16[:, 1, :], start=False, stop=True)
            mm(bk[5][:, 2 * E:3 * E], ones_b, mask16[:, 0, :], start=True, stop=False)
            mm(bk[5][:, 2 * E:3 * E], ones_b, mask16[:, 1, :], start=False, stop=True).then_inc(rank_ps, 1)
            pe.wait_ge(xr3_ready, 2)

            def gather(t):
                pe.wait_ge(sel_ready, t + 1)
                for k in range(KT):
                    for tt in range(TT):
                        for s in range(3):
                            last = mm(pg_g[:, k * C:(k + 1) * C], xr3[:, tt, s, k * P:(k + 1) * P], sel[:, tt, :],
                                      start=(tt + s == 0), stop=(tt == TT - 1 and s == 2))
                last.then_inc(g_ps, 1)

            def selection_t(t):
                pe.wait_ge(hTe_ready, t + 1)
                for tt in range(TT):
                    last = tr(pg_g[:, tt * P:(tt + 1) * P], selG[:, tt].rearrange("p w c -> p (w c)"), ident[:, :])
                last.then_inc(st_ps, 1)

            def biases(t):
                pe.wait_ge(oh_ready, t + 1)
                for h in range(2):
                    for w, b in ((0, pg_glu), (1, pg_lin)):
                        mm(b[C * h:C * (h + 1), :], oh_cur, bias3[:, w * D + h * HALF:w * D + (h + 1) * HALF],
                           start=True, stop=False)

            gather(0)
            pe.wait_ge(gates_ready, 1)
            for t in range(TT):
                last = tr(bk[6][0:E, t * P:(t + 1) * P], gates[:, t, 0:E], ident[:, :])
            last.then_inc(gT_ps, 1)
            pe.wait_ge(bias_ready, 1)
            biases(0)
            selection_t(0)

            def place(t, c):
                if isinstance(t, int):
                    n = t * SLOTS + c
                    pe.wait_ge(full[at[n]], 16 * filling(n))
                else:
                    n = FIFO_JOBS * SLOTS + c
                    pe.wait_ge(full[at[n]], t * 16 + 16 * (filling(n) - FIFO_JOBS))
                return place_of[at[n]]

            def job(t):
                for k in range(KT):
                    wk = place(t, k)
                    for w, b in ((0, pg_glu), (1, pg_lin)):
                        for h in range(2):
                            last = mm(b[C * h:C * (h + 1), :], hTe[:, k, :],
                                      wk[:, w * D + h * HALF:w * D + (h + 1) * HALF],
                                      start=False, stop=(k == KT - 1))
                    last.then_inc(chunk_used, 1)
                if isinstance(t, int) and t == 0:
                    pe.wait_ge(gatesT_ready, 1)
                    pe.wait_ge(bd_ld, 16)
                    for tt in range(TT):
                        for h in range(2):
                            last = mm(acc[tt][h][:, :], gatesT[:, tt * P:(tt + 1) * P],
                                      bdown[:, h * HALF:(h + 1) * HALF], start=False, stop=True,
                                      skip_group_check=True)
                pe.wait_ge(st_ready, t + 1)
                gather(t + 1)
                for c in range(4):
                    if c < 2:
                        pe.wait_ge(act_ready, 2 * t + (c + 1))
                        for b in range(2):
                            last = tr(pg_tr[c][:, b * P:(b + 1) * P], aa[:, (2 * c + b) * P:(2 * c + b + 1) * P],
                                      ident[:, :])
                        last.then_inc(actT_ps, 1)
                    if c % 2 == 0:
                        pe.wait_ge(actT_ready, 2 * t + (c // 2 + 1))
                    wk = place(t, KT + c)
                    for k in range(2):
                        for h in range(2):
                            last = mm(pg_t[C * h:C * (h + 1), :], actT[:, 2 * DOWN_ORDER[c] + k, :],
                                      wk[:, k * D + h * HALF:k * D + (h + 1) * HALF],
                                      start=(c + k == 0), stop=(c == 3 and k == 1))
                    last.then_inc(chunk_used, 1)
                selection_t(t + 1)
                biases(t + 1)
                pe.wait_ge(y_ready, t + 1)
                for tt in range(TT):
                    for h in range(2):
                        last = mm(acc[tt][h][:, :], STz[:, h, tt * P:(tt + 1) * P], ye, start=False, stop=True,
                                  skip_group_check=True)
                        last.then_inc(scattered[2 * tt + h], 1)

            for t in range(FIFO_JOBS):
                job(t)
            with pe.Fori(FIFO_JOBS, E) as t:
                job(t)
            pe.wait_ge(jobs_ready, 1)
            n_jobs = pe.value_load(n_jobs_i[0:1, :], min_val=E, max_val=E + MAX_EXTRA)
            with pe.If(n_jobs > E):
                with pe.Fori(E, n_jobs) as t:
                    job(t)

        @block.scalar
        def _(act):
            A = nc.scalar.activation
            ch = Chain(act, actc)
            for t in range(TT):
                act.dma_start(x_res[:, t, :], x[0, t * P:(t + 1) * P, :]).then_inc(x_ld[t], 16)

            def norm_stats(src, junk, ss, sd, done, ready=None):
                for t in range(TT):
                    if isinstance(ready, list):
                        act.wait_ge(ready[t], 16)
                    elif ready is not None:
                        act.wait_ge(ready[0], ready[1] + ready[2] * t)
                    ch.link(A(junk[:, t, :], src[:, t, :], ACT.Square, accum_out=ss[:, t:t + 1]))
                    A(sd[:, t:t + 1], ss[:, t:t + 1], ACT.Sqrt, bias=eps, scale=1.0 / D).then_inc(done, 1)

            def fetch(func):
                ch.link(A(spare, eps, func))

            act.wait_ge(dve_consts, 1)
            fetch(ACT.Sqrt)
            norm_stats(x_res, xn, ssx, sdx, x_sd, x_ld)
            act.wait_ge(par_ld, 48)
            A(par(3)[:, 0:2], par(2)[:, 0:2], ACT.Exp).then_inc(dt_ready, 1)
            fetch(ACT.Sqrt)
            act.wait_ge(mem_ld, 16)
            norm_stats(mem_n, mT[:, :, :].rearrange("p k t -> p (k t)").rearrange("p (t n) -> p t n", t=TT), ssm, sdm, m_sd)
            act.wait_ge(arg_ready, 1)
            A(par(8), par(4), ACT.Exp).then_inc(trig_ready, 1)
            A(par(9), par(6), ACT.Sin).then_inc(trig_ready, 1)
            A(par(10), par(5), ACT.Sin).then_inc(trig_ready, 1)

            def evac(q, dst):
                act.wait_ge(chunk_used, q + 1)
                A(dst, bk[q % 4][:, :].rearrange("p (m t) -> p m t", m=2), ACT.Copy).then_inc(proj_used, 1)

            evac(0, uT[:, 0:2, :])
            evac(1, uT[:, 2:4, :])
            Csv = Cs[:, :].rearrange("p (m t) -> p m t", m=2)
            evac(CONV_CH, Csv)
            for r, b in ((0, 7), (1, 6)):
                act.wait_ge(bct_ps, r + 1)
                A(CTv[:, r], bk[b][:, :].rearrange("p (m c) -> p m c", m=CT), ACT.Copy).then_inc(bct_ready, 1)
            act.wait_ge(consts, 3)
            for r, b in ((0, 4), (1, 5)):
                act.wait_ge(bct_ps, 3 + r)
                for j in range(4):
                    last = A(BT[32 * j:32 * j + 32, :, j, r, :],
                             bk[b][32 * j:32 * j + 32, :].rearrange("p (m s) -> p m s", m=CT), ACT.Copy)
                last.then_inc(bct_ready, 1)
            act.wait_ge(gT_ready, 1)
            for q in range(4):
                act.wait_ge(mT_ps, q + 1)
                for k in (2 * q, 2 * q + 1):
                    last = A(mT[:, k, :], bk[4 + q][:, (k % 2) * SEQ:(k % 2 + 1) * SEQ], ACT.Copy,
                             scale=gT[:, 8 + k:9 + k])
                last.then_inc(mT_ready, 1)
            act.wait_ge(proj_used, CONV_CH + 3)
            evac(CONV_CH + 3, Csv)
            act.wait_ge(proj_used, CONV_CH + 6)
            for q in range(K_CH, K_CH + 4):
                evac(q, kT[:, 2 * (q - K_CH):2 * (q - K_CH) + 2, :])
            act.wait_ge(yc_ready, 2)
            act.wait_ge(s_ready, ST_TILES)
            ch.link(A(sq_c, ycT, ACT.Square))
            for c in range(CT):
                last = A(ycT[:, c, :], ycT[:, c, :], ACT.Copy, scale=gT[:, 44 + c:45 + c])
            last.then_inc(ycg_ready, 1)
            fetch(ACT.Sigmoid)
            act.wait_ge(gelu_arg, 1)
            A(ge2, ge2, ACT.Sigmoid).then_inc(gelu_sig, 1)
            act.wait_ge(chunk_used, V_CH + 4)
            act.wait_ge(y_ps, CT)
            for t in range(TT):
                for h in range(2):
                    A(V[:, t, h * HALF:(h + 1) * HALF], bk[2 * t + h][:, :], ACT.Copy).then_inc(v_evac, 1)
            act.wait_ge(chunk_used, GLU_CH + 1)
            for i in range(2):
                A(ge[:, 2 * i:2 * i + 2, :], bk[4 + i][:, :].rearrange("p (m t) -> p m t", m=2),
                  ACT.Sigmoid).then_inc(glu_sig, 1)
            act.wait_ge(ys_ready, 1)
            ch.link(A(sq_s, ysT, ACT.Square))
            for c in range(CT):
                last = A(ysT[:, c, :], ysT[:, c, :], ACT.Copy, scale=gT[:, 48 + c:49 + c])
            last.then_inc(ysg_ready, 1)
            fetch(ACT.Sqrt)
            act.wait_ge(ss_ps, 2)
            for g in range(2):
                for t in range(TT):
                    last = A(sd_cs[:, 2 * g + t:2 * g + t + 1], bk[6][:, 8 * g + 2 * t:8 * g + 2 * t + 1], ACT.Sqrt,
                             bias=eps, scale=1.0 / D_CONV)
            last.then_inc(ss_sd, 1)
            norm_stats(x_res, xn2, ssx, sdx, x1_sd, (x1_ready, 6, 2))
            fetch(ACT.Exp)

            def q_out(h):
                act.wait_ge(chunk_used, WQ_CH + h + 1)
                A(QT[:, 2 * h:2 * h + 2, :], bk[4 + h][:, :].rearrange("p (m t) -> p m t", m=2),
                  ACT.Copy).then_inc(qT_ready, 1)

            def exponentials(h):
                act.wait_ge(mx_ready, h + 1)
                for t in range(TT):
                    last = A(PA[:, h, t, :], bk[h][:, t * SEQ:(t + 1) * SEQ], ACT.Exp,
                             bias=nmx[:, 2 * h + t:2 * h + t + 1], scale=r16[:, t:t + 1],
                             accum_out=sm[:, 2 * h + t:2 * h + t + 1])
                last.then_inc(exp_ready, 1)

            def probs_t_out(h):
                act.wait_ge(pt_ps, h + 1)
                A(PT[:, h], bk[4 + h][:, :].rearrange("p (m t) -> p m t", m=TT), ACT.Copy).then_inc(pt_ready, 1)

            q_out(0)
            for h in range(1, HEADS):
                q_out(h)
                exponentials(h - 1)
            probs_t_out(0)
            exponentials(HEADS - 1)
            for h in range(1, HEADS):
                probs_t_out(h)
            fetch(ACT.Sqrt)
            for t in range(TT):
                act.wait_ge(x2_ready, 2 + 2 * t)
                ch.link(A(xr3[:, t, 0, :], x_res[:, t, :], ACT.Square, accum_out=ssx[:, t:t + 1]))
                A(sdx[:, t:t + 1], ssx[:, t:t + 1], ACT.Sqrt, bias=eps, scale=1.0 / D).then_inc(x2_sd, 1)
                act.wait_ge(rx_ready, t + 1)
                A(xr3[:, t, 0, :], x_res[:, t, :], ACT.Copy, scale=rsx[:, t:t + 1]).then_inc(part_hi[t], 1)
            fetch(ACT.Exp)
            for s in (1, 2):
                if s == 2:
                    act.wait_ge(lmax_ready, 1)
                    for t in range(TT):
                        last = A(gexp[:, t, :], lg[:, t, :], ACT.Exp, bias=ngm[:, t:t + 1])
                    last.then_inc(gexp_ready, 1)
                for t in range(TT):
                    act.wait_ge(part_sub[t], s)
                    i = A(xr3[:, t, s, :], xn2[:, t, :], ACT.Copy)
                    i.then_inc(part_hi[t] if s < 2 else xr3_ready, 1)
            fetch(ACT.Sigmoid)

            def job(t):
                for j in range(2):
                    act.wait_ge(glu_min, 2 * t + (j + 1))
                    cols = slice(j * SEQ, (j + 1) * SEQ)
                    A(sg[:, cols], g7[:, cols], ACT.Sigmoid, scale=ALPHA).then_inc(sig_ready, 1)
                for j in range(2):
                    act.wait_ge(actT_ps, 2 * t + (j + 1))
                    A(actT.rearrange("p (w c) s -> p c w s", w=2)[:, 2 * j:2 * j + 2],
                      pg_tr[j][:, 0:2 * P].rearrange("p (c w s) -> p c w s", c=2, w=2), ACT.Copy).then_inc(actT_ready, 1)
                act.wait_ge(chunk_used, t * SLOTS + (N_PRE + SLOTS))
                A(ye, pg_t[:, :], ACT.Copy).then_inc(y_ready, 1)

            job(0)
            job(1)
            with act.Fori(2, E) as t:
                job(t)
            act.wait_ge(jobs_ready, 1)
            n_jobs = act.value_load(n_jobs_i[0:1, :], min_val=E, max_val=E + MAX_EXTRA)
            with act.If(n_jobs > E):
                with act.Fori(E, n_jobs) as t:
                    job(t)
            fetch(ACT.Sqrt)
            for t in range(TT):
                for h, ss in ((0, ssx), (1, ssm)):
                    act.wait_ge(scattered[2 * t + h], n_jobs)
                    A(junk_n[:, t, h * HALF:(h + 1) * HALF], acc[t][h][:, :], ACT.Square,
                      accum_out=ss[:, t:t + 1]).then_inc(fin_sq, 1)
            act.wait_ge(fin_ss, 1)
            A(sdx, rsm, ACT.Sqrt, bias=eps, scale=1.0 / D).then_inc(fin_sd, 1)

        @block.vector
        def _(dve):
            v = nc.vector
            TTo, TS, STT, TC = v.tensor_tensor, v.tensor_scalar, v.scalar_tensor_tensor, v.tensor_copy
            ch = Chain(dve, dvec)
            v.memset(eps, EPS)
            v.memset(ones2, 1.0)
            v.memset(BDn, 0.0)
            v.memset(vp[:, :], 0.0).then_inc(dve_consts, 1)

            def normalise(src, dst, sd, rs, sd_done, done):
                for t in range(TT):
                    dve.wait_ge(sd_done, t + 1)
                    ch.link(v.reciprocal(rs[:, t:t + 1], sd[:, t:t + 1]))
                    TS(dst[:, t, :], src[:, t, :], rs[:, t:t + 1], None, ALU.mult).then_inc(done, 1)

            def gained(dst, banks, g0, ps, ready):
                for q in banks:
                    dve.wait_ge(ps, q + 1)
                    TTo(dst[:, 2 * q:2 * q + 2, :], bk[q][:, :].rearrange("p (k t) -> p k t", k=2),
                        bc_last(gT[:, g0 + 2 * q:g0 + 2 * q + 2], [P, 2, SEQ]), ALU.mult).then_inc(ready, 1)

            dve.wait_ge(dve_consts, 1)
            normalise(x_res, xn, sdx, rsx, x_sd, xn_ready)
            dve.wait_ge(rows_t, 1)
            TC(gT[:, :], bk[6][:, 0:56]).then_inc(gT_ready, 1)
            dve.wait_ge(gT_ready, 1)
            gained(hT, (0, 1, 2, 3), 0, xT_ps, xT_ready)

            dve.wait_ge(dt_ready, 1)
            dtb = bc_last(par(3)[:, 0:2], [16, 2, NST])

            def wn(ap):
                return ap.rearrange("p (w n) -> p w n", w=2)
            TTo(wn(par(4)), wn(par(0)), dtb, ALU.mult)
            ch.link(TTo(wn(par(5)), wn(par(1)), dtb, ALU.mult))
            MAGIC = 1.5 * 2.0 ** 23
            HI = 6.28125
            LO = 2 * math.pi - HI
            PI_DOWN = 3.1415925
            ch.link(TS(par(7), par(5), 1.0 / (2 * math.pi), MAGIC, ALU.mult, ALU.add))
            ch.link(TS(par(7), par(7), MAGIC, None, ALU.subtract))
            ch.link(STT(par(5), par(7), -HI, par(5), ALU.mult, ALU.add))
            ch.link(STT(par(5), par(7), -LO, par(5), ALU.mult, ALU.add))
            ch.link(TS(par(6), par(5), math.pi / 2, None, ALU.add))
            ch.link(TS(par(7), par(6), math.pi, -2 * math.pi, ALU.is_gt, ALU.mult))
            ch.link(TTo(par(6), par(6), par(7), ALU.add))
            TS(par(6), par(6), PI_DOWN, -PI_DOWN, ALU.min, ALU.max)
            TS(par(5), par(5), PI_DOWN, -PI_DOWN, ALU.min, ALU.max).then_inc(arg_ready, 1)
            TTo(par(13), par(0), par(0), ALU.mult)
            ch.link(TTo(par(14), par(1), par(1), ALU.mult))
            ch.link(TTo(par(13), par(13), par(14), ALU.add))
            dve.wait_ge(trig_ready, 3)
            TTo(par(4), par(8), par(9), ALU.mult)
            ch.link(TTo(par(7), par(8), par(10), ALU.mult))
            ch.link(TS(par(4), par(4), 1.0, None, ALU.subtract))
            TTo(par(11), par(4), par(0), ALU.mult)
            TTo(par(12), par(7), par(0), ALU.mult)
            TTo(par(5), par(7), par(1), ALU.mult)
            TTo(par(6), par(4), par(1), ALU.mult)
            ch.link(v.reciprocal(par(13), par(13)))
            TTo(par(11), par(11), par(5), ALU.add)
            ch.link(TTo(par(12), par(12), par(6), ALU.subtract))
            TTo(par(11), par(11), par(13), ALU.mult)
            TTo(par(12), par(12), par(13), ALU.mult).then_inc(par_math, 1)

            normalise(mem_n, mem_n, sdm, rsm, m_sd, mn_ready)
            dve.wait_ge(consts, 4)
            dve.wait_ge(bc_ld, 64)
            for r in range(2):
                for w in range(2):
                    last = TS(CNn[:, r, :, w, :], c_nat[:, r], sel_mask[:, 2 * r + w:2 * r + w + 1], None, ALU.mult)
            last.then_inc(cn_ready, 1)
            dve.wait_ge(par_ps, 1)
            ch.link(TC(pT, bk[6][:, 64:144].rearrange("p (q i) -> p q i", q=5)))
            mag, cos1, sin1, q_re, q_im = (pT[:, i, :] for i in range(5))
            shp = [P, ST_TILES, GCH]
            TTo(b_bar[:, 0], b_nat[:, 0], bc_last(q_re, shp), ALU.mult)
            TTo(b_tmp[:, 0], b_nat[:, 1], bc_last(q_im, shp), ALU.mult)
            TTo(b_bar[:, 1], b_nat[:, 1], bc_last(q_re, shp), ALU.mult)
            ch.link(TTo(b_tmp[:, 1], b_nat[:, 0], bc_last(q_im, shp), ALU.mult))
            for w in range(2):
                ps_ = slice(NST * w, NST * (w + 1))
                TTo(BDn[ps_, 0, :, w, :], b_bar[ps_, 0], b_tmp[ps_, 0], ALU.subtract)
                last = TTo(BDn[ps_, 1, :, w, :], b_bar[ps_, 1], b_tmp[ps_, 1], ALU.add)
            last.then_inc(bd_ready, 1)
            v.memset(sinT[:, :, 0:1], 0.0)
            ch.link(TC(sinT[:, :, 1:2], bc_last(sin1, [P, ST_TILES, 1])))
            v.memset(cosT[:, :, 0:1], 1.0)
            TC(cosT[:, :, 1:2], bc_last(cos1, [P, ST_TILES, 1])).then_inc(pT_ready, 1)
            L, lv = 1, 0
            dve.wait_ge(pT_ready, 1)
            while L < SEQ:
                if lv:
                    dve.wait_ge(tab_pool, lv)
                n = min(L, SEQ - 1 - L)
                def level(dst, x0, y0, x1, y1, op, i0, i1):
                    s3 = [P, i1 - i0, n]
                    tv = tmp_dve[:, 0:(i1 - i0) * n].rearrange("p (i t) -> p i t", t=n)
                    to = dst[:, i0:i1, L + 1:L + 1 + n]
                    TTo(to, x0[:, i0:i1, 1:1 + n], y0[:, i0:i1, L:L + 1].to_broadcast(s3), ALU.mult)
                    ch.link(TTo(tv, x1[:, i0:i1, 1:1 + n], y1[:, i0:i1, L:L + 1].to_broadcast(s3), ALU.mult))
                    ch.link(TTo(to, to, tv, op))
                for i0, i1 in (((0, 16),) if n * ST_TILES <= 1024 else ((0, 8), (8, 16))):
                    level(sinT, sinT, cosT, cosT, sinT, ALU.add, i0, i1)
                if shared(L):
                    level(cosT, cosT, cosT, sinT, sinT, ALU.subtract, 0, COS_DVE)
                dve.sem_inc(tab_dve, 1)
                L, lv = 2 * L, lv + 1
            dve.wait_ge(tab_pool, lv)

            def rotate_in(i):
                b = i % 2
                dve.wait_ge(bu_ps, i + 1)
                if i >= 2:
                    dve.wait_ge(zin_ready, i - 1)
                src = bk[4 + b][:, :].rearrange("p (r t) -> p r t", r=2)
                TTo(sA[:, b], src, cosT[:, i:i + 1, :].to_broadcast([P, 2, SEQ]), ALU.mult)
                TTo(sB[:, b], src, sinT[:, i:i + 1, :].to_broadcast([P, 2, SEQ]), ALU.mult).then_inc(ab_ready, 1)

            def scan(i):
                b = i % 2
                dve.wait_ge(zin_ready, i + 1)
                if i >= 2:
                    dve.wait_ge(s_ready, i - 1)
                for r in range(2):
                    last = v.tensor_tensor_scan(zz[:, b, r, :], mag[:, i:i + 1].to_broadcast([P, SEQ]),
                                                zin[:, b, r, :], 0.0, ALU.mult, ALU.add)
                last.then_inc(z_ready, 1)
                dve.wait_ge(z_ready, i + 1)
                TTo(Qb[:, b], zz[:, b], sinT[:, i:i + 1, :].to_broadcast([P, 2, SEQ]), ALU.mult).then_inc(q_ready, 1)

            Csv = Cs[:, :].rearrange("p (m t) -> p m t", m=2)
            vpv = vp[:, :].rearrange("p (m t) -> p m t", m=2)

            def conv_x(i):
                q = CONV_CH + 3 * i + 1
                dve.wait_ge(chunk_used, q + 1)
                dve.wait_ge(proj_used, q)
                ch.link(TTo(vpv[:, :, 2:SEQ + 2], bk[q % 4][:, :].rearrange("p (m t) -> p m t", m=2), Csv,
                            ALU.mult))
                dve.sem_inc(proj_used, 1)

            def conv_b(i):
                q = CONV_CH + 3 * i + 2
                dve.wait_ge(chunk_used, q + 1)
                for m in range(2):
                    c = 2 * i + m
                    ch.link(TS(cv[:, :], vpv[:, m, 2:SEQ + 2], gT[:, 40 + c:41 + c], None, ALU.mult))
                    ch.link(STT(cv[:, :], vpv[:, m, 1:SEQ + 1], gT[:, 36 + c:37 + c], cv[:, :], ALU.mult, ALU.add))
                    ch.link(STT(cv[:, :], vpv[:, m, 0:SEQ], gT[:, 32 + c:33 + c], cv[:, :], ALU.mult, ALU.add))
                    ch.link(TTo(ycT[:, c, :], bk[q % 4][:, m * SEQ:(m + 1) * SEQ], cv[:, :], ALU.mult))
                dve.sem_inc(proj_used, 1)
                dve.sem_inc(yc_ready, 1)

            def y_add(m):
                dve.wait_ge(y_ps, m + 1)
                STT(ysT[:, m, :], uT[:, m, :], gT[:, 52 + m:53 + m], bk[6 + m % 2][:, 0:SEQ], ALU.mult,
                    ALU.add).then_inc(yv_ready, 1)

            for i in range(ST_TILES):
                rotate_in(i)
                if i >= 1:
                    scan(i - 1)
                if i in (1, 5):
                    conv_x((i - 1) // 4)
                if i in (2, 7):
                    conv_b((i - 2) // 4)
                if i in (7, 11, 15):
                    y_add((i - 7) // 4)
            scan(ST_TILES - 1)
            y_add(3)
            dve.wait_ge(yv_ready, 4)
            dve.wait_ge(s_ready, ST_TILES)
            ch.link(TTo(ge, ysT, ysT, ALU.mult))
            ch.link(TS(ge, ge, 0.044715, 1.0, ALU.mult, ALU.add))
            GC = 2.0 * math.sqrt(2.0 / math.pi)
            STT(ge2, ge, GC, ysT, ALU.mult, ALU.mult).then_inc(gelu_arg, 1)
            dve.wait_ge(gelu_sig, 1)
            TTo(yg, ysT, ge2, ALU.mult).then_inc(yg_ready, 1)
            dve.wait_ge(yg_ready, 1)
            for i in range(2):
                dve.wait_ge(glu_sig, i + 1)
                last = TTo(ysT[:, 2 * i:2 * i + 2, :], yg[:, 2 * i:2 * i + 2, :], ge[:, 2 * i:2 * i + 2, :], ALU.mult)
            last.then_inc(ys_ready, 1)
            dve.wait_ge(ss_sd, 1)
            v.reciprocal(r_conv, sd_cs[:, 0:2])
            ch.link(v.reciprocal(r_ssm, sd_cs[:, 2:4]))
            dve.sem_inc(r_ready, 1)
            dve.wait_ge(x2_ld, 16)
            for g, r in ((0, r_conv), (1, r_ssm)):
                for t in range(TT):
                    for h in range(2):
                        b = 2 * t + h
                        dve.wait_ge(*((mix_ps, 3 * g + b + 1) if b < 3 else (chunk_used, WO_CH + 2 * (g + 1))))
                        xs = x_res[:, t, h * HALF:(h + 1) * HALF]
                        if g:
                            dve.wait_ge(x1_ready, 2 * t + h + 1)
                        STT(xs, bk[4 * g + 2 * t + h][:, :], r[:, t:t + 1], xs, ALU.mult, ALU.add).then_inc(x1_ready, 1)

            gained(hT, (0, 1, 2, 3), 16, x1T_ps, x1T_ready)
            dve.wait_ge(x1_sd, 2)
            ch.link(v.reciprocal(rsx, sdx))
            ch.link(TS(r16, rsx, HD ** -0.5, None, ALU.mult))

            def row_max(h):
                dve.wait_ge(sc_ps, h + 1)
                ch.link(v.tensor_reduce(mx[:, 2 * h:2 * h + 2], bk[h][:, :].rearrange("p (t m) -> p t m", t=TT),
                                        AX.X, ALU.max))
                STT(nmx[:, 2 * h:2 * h + 2], mx[:, 2 * h:2 * h + 2], -1.0, r16, ALU.mult, ALU.mult).then_inc(mx_ready, 1)

            def probabilities(h):
                dve.wait_ge(exp_ready, h + 1)
                ch.link(v.reciprocal(rsum[:, 2 * h:2 * h + 2], sm[:, 2 * h:2 * h + 2]))
                for t in range(TT):
                    last = TS(PA[:, h, t, :], PA[:, h, t, :], rsum[:, 2 * h + t:2 * h + t + 1], None, ALU.mult)
                last.then_inc(p_ready, 1)

            for h in range(HEADS):
                row_max(h)
                if h >= 1:
                    probabilities(h - 1)
            probabilities(HEADS - 1)
            for h in range(HEADS):
                dve.wait_ge(o_ps, h + 1)
                TC(OT[:, 2 * h:2 * h + 2, :], bk[h][:, :].rearrange("p (d t) -> p d t", d=2)).then_inc(o_ready, 1)
            v.memset(STz, 0.0)
            dve.wait_ge(consts, 5)
            v.memset(gates, 0.0)
            v.memset(rankm, 0.0)

            def factor(t):
                dve.wait_ge(x2_sd, t + 1)
                v.reciprocal(rsx[:, t:t + 1], sdx[:, t:t + 1]).then_inc(rx_ready, 1)

            def scaled(t):
                dve.wait_ge(rx_ready, t + 1)
                TS(xn2[:, t, :], x_res[:, t, :], rsx[:, t:t + 1], None, ALU.mult).then_inc(xn2_ready, 1)

            for t in range(TT):
                for h in range(2):
                    b = 2 * t + h
                    dve.wait_ge(*((xo_ps, b + 1) if b < 3 else (chunk_used, XO_CH + 4)))
                    xs = x_res[:, t, h * HALF:(h + 1) * HALF]
                    TTo(xs, xs, bk[4 + 2 * t + h][:, :], ALU.add).then_inc(x2_ready, 1)
                if t == 0:
                    factor(0)
                    scaled(0)
            gained(hT, (0, 1), 24, x2T_ps, x2T_ready)
            factor(1)
            gained(hT, (2, 3), 24, x2T_ps, x2T_ready)
            scaled(1)

            def rest(s):
                dve.wait_ge(part_hi[0], s + 1)
                TTo(xn2[:, 0, :], xn2[:, 0, :], xr3[:, 0, s, :], ALU.subtract).then_inc(part_sub[0], 1)

            for s in range(2):
                dve.wait_ge(xn2_ready, 1)
                rest(s)

            def select(t, e):
                for tt in range(TT):
                    last = TS(sel[:, tt, :], iota_c, job_b[:, bass.ds(t, 1)], rankm[:, tt, bass.ds(e, 1)],
                              ALU.add, ALU.is_equal)
                return last

            def select_gated(e):
                for tt in range(TT):
                    last = TS(selG[:, tt], sel[:, tt:tt + 1, :].to_broadcast([P, 2, C]), gates[:, tt, bass.ds(e, 1)],
                              None, ALU.mult)
                return last

            def gathered(t):
                dve.wait_ge(g_ps, t + 1)
                TTo(hTe, pg_g[:, :].rearrange("p (k c) -> p k c", k=KT), bc_last(gT[:, 24:32], [P, KT, C]),
                    ALU.mult).then_inc(hTe_ready, 1)

            def back(t):
                dve.wait_ge(st_ps, t + 1)
                for w in range(2):
                    last = TC(STz[C * w:C * (w + 1), w, :], pg_g[C * w:C * (w + 1), 0:SEQ])
                last.then_inc(st_ready, 1)

            dve.wait_ge(wr_ld, 32)
            dve.wait_ge(lg_ps, 1)
            for t in range(TT):
                last = STT(lg[:, t, :], bk[4][:, E * t:E * (t + 1)], rsx[:, t:t + 1], br, ALU.mult, ALU.add)
            ch.link(last)
            for t in range(TT):
                last = v.max(top8[:, t, :], lg[:, t, :])
            ch.link(last)
            TS(ngm, top8[:, :, 0:1].rearrange("p t o -> p (t o)"), -1.0, None, ALU.mult).then_inc(lmax_ready, 1)
            fourth = top8[:, :, TOPK - 1:TOPK].to_broadcast([P, TT, E])
            TTo(gt, lg, fourth, ALU.is_gt)
            ch.link(TTo(eq, lg, fourth, ALU.is_equal))
            for t in range(TT):
                v.tensor_tensor_scan(cum[:, t, :], ones96[:, 0:E], eq[:, t, :], 0.0, ALU.mult, ALU.add)
            ch.link(v.tensor_reduce(need, gt, AX.X, ALU.add))
            ch.link(TS(need, need, -1.0, float(TOPK), ALU.mult, ALU.add))
            for t in range(TT):
                last = STT(cum[:, t, :], cum[:, t, :], need[:, t:t + 1], eq[:, t, :], ALU.is_le, ALU.mult)
            ch.link(last)
            ch.link(TTo(maskf, gt, cum, ALU.add))
            TC(mask16, maskf).then_inc(mask_ready, 1)
            dve.wait_ge(rank_ps, 1)
            ch.link(STT(rankm[:, :, 0:E], bk[5][:, 0:2 * E].rearrange("p (t e) -> p t e", t=TT), 1.0, maskf,
                        ALU.add, ALU.mult))
            select(0, 0).then_inc(sel_ready, 1)
            ch.link(TC(cnt, bk[5][:, 2 * E:3 * E]))
            TC(oh_cur, onehot[:, 0:1].to_broadcast([96, C])).then_inc(oh_ready, 1)
            dve.wait_ge(gexp_ready, 1)
            ch.link(TTo(gexp, gexp, maskf, ALU.mult))
            ch.link(v.tensor_reduce(gsum, gexp, AX.X, ALU.add))
            ch.link(v.reciprocal(grec, gsum))
            for t in range(TT):
                last = TS(gates[:, t, 0:E], gexp[:, t, :], grec[:, t:t + 1], None, ALU.mult)
            last.then_inc(gates_ready, 1)
            dve.wait_ge(gates_ready, 1)
            dve.wait_ge(sel_ready, 1)
            ch.link(select_gated(0))
            gathered(0)
            dve.wait_ge(gT_ps, 1)
            TC(gatesT, bk[6][0:E, 0:SEQ]).then_inc(gatesT_ready, 1)
            back(0)
            dve.wait_ge(chunk_used, N_PRE + 1)
            ch.link(TC(job_ei[:, 0:E], job_e[:, 0:E]))
            for c in range(PASSES):
                last = TS(flag[:, c * E:(c + 1) * E], cnt, float(C * (c + 1)), None, ALU.is_gt)
            ch.link(last)
            ch.link(v.tensor_tensor_scan(incl, ones96, flag, 0.0, ALU.mult, ALU.add))
            ch.link(TTo(pos, incl, flag, ALU.subtract))
            jf = [P, 8, 96]
            for j in (0, 8):
                ch.link(TTo(eqj, pos.unsqueeze(1).to_broadcast(jf), bc_last(iota_j[:, j:j + 8], jf), ALU.is_equal))
                ch.link(TTo(eqj, eqj, flag.unsqueeze(1).to_broadcast(jf), ALU.mult))
                ch.link(TTo(eqi, eqj, id_b.unsqueeze(1).to_broadcast(jf), ALU.mult))
                ch.link(v.tensor_reduce(job_b[:, E + j:E + j + 8], eqi, AX.X, ALU.add))
                ch.link(TTo(eqi, eqj, id_e.unsqueeze(1).to_broadcast(jf), ALU.mult))
                ch.link(v.tensor_reduce(job_e[:, E + j:E + j + 8], eqi, AX.X, ALU.add))
            TS(n_jobs_i, incl[:, 95:96], float(E), None, ALU.add)
            ch.link(TS(job_ei[:, E:E + 16], job_e[:, E:E + 16], float(E), None, ALU.add))
            dve.sem_inc(jobs_ready, 1)
            dve.wait_ge(jobs_ready, 1)

            lp = Chain(dve, dvel)

            def job(t):
                lp.count = t * DVE_LOOP_LINKS
                e = dve.value_load(job_ei[0:1, bass.ds(t + 1, 1)], min_val=0, max_val=E)
                dve.wait_ge(st_ps, t + 1)
                select(t + 1, e).then_inc(sel_ready, 1)
                dve.wait_ge(sel_ready, t + 2)
                lp.link(select_gated(e))
                dve.wait_ge(chunk_used, t * SLOTS + (N_PRE + KT))
                halves = [slice(j * HALF // 2, (j + 1) * HALF // 2) for j in range(2)]
                for cols in halves:
                    TS(g7[:, cols], pg_glu[:, cols], LIMIT, None, ALU.min).then_inc(glu_min, 1)
                dve.wait_ge(glu_min, 2 * t + 2)
                for j, cols in enumerate(halves):
                    lp.link(TS(l7[:, cols], pg_lin[:, cols], LIMIT, -LIMIT, ALU.min, ALU.max))
                    lp.link(STT(l7[:, cols], l7[:, cols], 1.0, g7[:, cols], ALU.add, ALU.mult))
                    dve.wait_ge(sig_ready, 2 * t + (j + 1))
                    TTo(aa[:, cols], l7[:, cols], sg[:, cols], ALU.mult).then_inc(act_ready, 1)
                TC(oh_cur, onehot[:, bass.ds(e, 1)].to_broadcast([96, C])).then_inc(oh_ready, 1)
                gathered(t + 1)
                dve.wait_ge(scattered[2 * TT - 1], t + 1)
                back(t + 1)
                return lp.count

            job(0)
            job(1)
            with dve.Fori(2, E) as t:
                job(t)
            n_jobs = dve.value_load(n_jobs_i[0:1, :], min_val=E, max_val=E + MAX_EXTRA)
            with dve.If(n_jobs > E):
                with dve.Fori(E, n_jobs) as t:
                    job(t)
            dve.wait_ge(gf_ld, 16)
            dve.wait_ge(fin_sq, 2 * TT)
            TTo(rsm, ssx, ssm, ALU.add).then_inc(fin_ss, 1)
            dve.wait_ge(fin_sd, 1)
            ch.link(v.reciprocal(rsx, sdx))
            for t in range(TT):
                for h in range(2):
                    STT(out_n[:, t, h * HALF:(h + 1) * HALF], acc[t][h][:, :], rsx[:, t:t + 1],
                        gfin[:, h * HALF:(h + 1) * HALF], ALU.mult, ALU.mult).then_inc(fin_ready, 1)

        @block.gpsimd
        def _(pool):
            g = nc.gpsimd
            ch = Chain(pool, poolc)
            ch.link(g.memset(ident[:, :], 0.0))
            pool.sem_inc(consts, 1)
            g.affine_select(out=ident[:, :], in_=ident[:, :], compare_op=ALU.not_equal, fill=1.0, base=0,
                            pattern=[[-1, P]], channel_multiplier=1).then_inc(consts, 1)
            pool.wait_ge(x_ld[1], 16)
            for r, src in ((0, ssm_b_re), (1, ssm_b_im)):
                pool.dma_start(b_nat[:, r], src[0].rearrange("(i w) n c -> (w n) i c", w=2)).then_inc(bc_ld, 16)
            for r, src in ((0, ssm_c_re), (1, ssm_c_im)):
                pool.dma_start(c_nat[:, r], src[0].rearrange("(m g) c n -> (g c) m n", m=CT)).then_inc(bc_ld, 16)
            g.memset(BT, 0.0).then_inc(consts, 1)
            ch.link(g.memset(tmp_pool[:, 0:64], 0.0))
            for w in range(2):
                for a in range(4):
                    lo = 32 * a + 16 * w
                    col = tmp_pool[:, 8 * w + a:8 * w + a + 1]
                    ch.link(g.affine_select(out=col, in_=tmp_pool[:, 32:33], compare_op=ALU.is_gt, fill=1.0,
                                            base=lo, pattern=[[0, 1]], channel_multiplier=-1))
                    ch.link(g.affine_select(out=col, in_=col, compare_op=ALU.is_gt, fill=0.0,
                                            base=lo + 16, pattern=[[0, 1]], channel_multiplier=-1))
            for w in range(2):
                for a in range(4):
                    col = tmp_pool[:, 8 * w + a:8 * w + a + 1]
                    if a == 0:
                        ch.link(g.tensor_copy(sel_mask[:, w:w + 1], col))
                    else:
                        ch.link(g.tensor_tensor(sel_mask[:, w:w + 1], sel_mask[:, w:w + 1], col, ALU.add))
            ch.link(g.tensor_scalar(sel_mask[:, 2:4], sel_mask[:, 0:2], -1.0, None, ALU.mult))
            pool.sem_inc(consts, 1)
            L, lv = 1, 0
            pool.wait_ge(pT_ready, 1)
            while L < SEQ:
                if lv:
                    pool.wait_ge(tab_dve, lv)
                n = min(L, SEQ - 1 - L)
                first = COS_DVE if shared(L) else 0
                for i0, i1 in (((first, 16),) if n * ST_TILES <= 1024 else ((first, 10), (10, 16))):
                    s3 = [P, i1 - i0, n]
                    tv = tmp_pool[:, 0:(i1 - i0) * n].rearrange("p (i t) -> p i t", t=n)
                    dst = cosT[:, i0:i1, L + 1:L + 1 + n]
                    g.tensor_tensor(dst, cosT[:, i0:i1, 1:1 + n], cosT[:, i0:i1, L:L + 1].to_broadcast(s3), ALU.mult)
                    ch.link(g.tensor_tensor(tv, sinT[:, i0:i1, 1:1 + n], sinT[:, i0:i1, L:L + 1].to_broadcast(s3),
                                            ALU.mult))
                    ch.link(g.tensor_tensor(dst, dst, tv, ALU.subtract))
                pool.sem_inc(tab_pool, 1)
                L, lv = 2 * L, lv + 1
            pool.wait_ge(tab_dve, lv)

            def rotate_sum(i):
                b = i % 2
                pool.wait_ge(ab_ready, i + 1)
                if i >= 2:
                    pool.wait_ge(z_ready, i - 1)
                g.tensor_tensor(zin[:, b, 0, :], sA[:, b, 0, :], sB[:, b, 1, :], ALU.add)
                g.tensor_tensor(zin[:, b, 1, :], sA[:, b, 1, :], sB[:, b, 0, :], ALU.subtract).then_inc(zin_ready, 1)

            def states(i):
                b = i % 2
                pool.wait_ge(z_ready, i + 1)
                ch.link(g.tensor_tensor(Pb, zz[:, b], cosT[:, i:i + 1, :].to_broadcast([P, 2, SEQ]), ALU.mult))
                pool.wait_ge(q_ready, i + 1)
                m = i // 4
                if m >= 2:
                    pool.wait_ge(y_ps, m - 1)
                elif m == 1:
                    pool.wait_ge(mT_ps, 4)
                else:
                    pool.wait_ge(xn_ready, 2)
                g.tensor_tensor(s4[m % 2][:, i % 4, 0, :], Pb[:, 0, :], Qb[:, b, 1, :], ALU.subtract)
                g.tensor_tensor(s4[m % 2][:, i % 4, 1, :], Pb[:, 1, :], Qb[:, b, 0, :], ALU.add).then_inc(s_ready, 1)
                pool.wait_ge(s_ready, i + 1)

            for i in range(ST_TILES):
                rotate_sum(i)
                if i >= 1:
                    states(i - 1)
            states(ST_TILES - 1)
            pool.wait_ge(y_ps, 4)
            pool.dma_start(x_res, x[0].rearrange("(t p) n -> p t n", p=P)).then_inc(x2_ld, 16)
            pool.wait_ge(bu_ps, ST_TILES)
            for s in range(3):
                pool.dma_start(bg_raw[E * s:E * (s + 1), :], b_gu[0]).then_inc(bg_ld, 16)
            pool.wait_ge(chunk_used, V_CH + 4)
            pool.dma_start(bdown, b_down[0]).then_inc(bd_ld, 16)
            pool.wait_ge(bg_ld, 48)
            ch.link(g.tensor_copy(bias3, bg_raw))
            for s in (1, 2):
                for q in range(s, 3):
                    rows_q = slice(E * q, E * (q + 1))
                    ch.link(g.tensor_tensor(bg_raw[rows_q, :], bg_raw[rows_q, :], bias3[rows_q, :], ALU.subtract))
                    ch.link(g.tensor_copy(bias3[rows_q, :], bg_raw[rows_q, :]))
            pool.sem_inc(bias_ready, 1)
            pool.wait_ge(yc_ready, 2)
            pool.dma_start(wr, w_router[0].rearrange("(k p) e -> p k e", p=P)).then_inc(wr_ld, 16)
            pool.dma_start(br, b_router[0].partition_broadcast(P)).then_inc(wr_ld, 16)
            pool.dma_start(gfin, norm_final.partition_broadcast(P)).then_inc(gf_ld, 16)
            pool.wait_ge(sc_ps, HEADS)
            g.memset(tri, 1.0)
            g.memset(ones_b, 1.0)
            g.memset(ones96, 1.0)
            g.memset(job_b, 0.0)
            ch.link(g.memset(onehot, 0.0))
            g.affine_select(out=tri, in_=tri, compare_op=ALU.is_gt, fill=0.0, base=0, pattern=[[1, P]],
                            channel_multiplier=-1)
            for s in range(3):
                ch.link(g.affine_select(out=onehot[:, 0:E], in_=onehot[:, 0:E], compare_op=ALU.not_equal, fill=1.0,
                                        base=-E * s, pattern=[[-1, E]], channel_multiplier=1))
            g.iota(iota_c, [[1, C]], base=1, channel_multiplier=0, allow_small_or_imprecise_dtypes=True)
            g.iota(iota_j, [[1, 16]], base=0, channel_multiplier=0, allow_small_or_imprecise_dtypes=True)
            g.iota(job_e, [[1, JT]], base=0, channel_multiplier=0, allow_small_or_imprecise_dtypes=True)
            g.iota(id_e, [[0, PASSES], [1, E]], base=-E, channel_multiplier=0, allow_small_or_imprecise_dtypes=True)
            ch.link(g.iota(id_b, [[C, PASSES], [0, E]], base=C, channel_multiplier=0,
                           allow_small_or_imprecise_dtypes=True))
            pool.sem_inc(consts, 1)
            for s in range(2):
                if s == 0:
                    pool.wait_ge(xn2_ready, 2)
                pool.wait_ge(part_hi[1], s + 1)
                g.tensor_tensor(xn2[:, 1, :], xn2[:, 1, :], xr3[:, 1, s, :], ALU.subtract).then_inc(part_sub[1], 1)


_INS = ["x", "mem", "norm_mix", "w_in", "conv_w", "ssm_a_re", "ssm_a_im", "ssm_log_dt", "ssm_b_re", "ssm_b_im",
        "ssm_c_re", "ssm_c_im", "ssm_d", "w_glu", "norm_conv_out", "norm_ssm_out", "w_out", "norm_xattn", "norm_mem",
        "w_q", "w_kv", "w_o", "norm_moe", "w_router", "b_router", "w_gu", "b_gu", "w_down", "b_down", "norm_final"]


def kernel(**inputs):
    import numpy as _np
    import concourse.bacc as _bacc
    from concourse import mybir as _mybir
    from concourse.bass_utils import run_bass_kernel_spmd as _run

    nc = _bacc.Bacc("TRN2", target_bir_lowering=False, num_devices=1)
    arrays, args = {}, []
    for name in _INS:
        a = _np.ascontiguousarray(inputs[name])
        arrays[f"in_{name}"] = a
        args.append(nc.dram_tensor(f"in_{name}", a.shape, _mybir.dt.from_np(a.dtype), kind="ExternalInput").ap())
    out = nc.dram_tensor("out_0", (1, SEQ, D), F32, kind="ExternalOutput").ap()
    hybrid_layer(nc, *args, out)
    r = _run(nc, [arrays], core_ids=[0])
    return r.results[0]["out_0"]
```
